# Optimizing a Trainium2 kernel written in Bass

```python
import math
import jax, jax.numpy as jnp
from jax import lax
import numpy as np

D_MODEL = 1024
BATCH = 1
SEQ = 256
DEPTH = 2

GRID_W = 64
CTX_LEN = 256
N_MOD = 6
EPS = 1e-6

N_POOL_GROUPS = 4
POOL_GROUP_DIM = D_MODEL // 16
POOL_WIDTH = N_POOL_GROUPS * POOL_GROUP_DIM
POOL_WINDOWS = (2, 4, 8, 16)
N_FNO_GROUPS = 4
FNO_GROUP_DIM = D_MODEL // 16
FNO_WIDTH = N_FNO_GROUPS * FNO_GROUP_DIM
N_HEADS = 8
QK_NOPE = 64
QK_ROPE = 32
V_DIM = 64
Q_LORA = 384
KV_LORA = 256
ATTN_WIDTH = N_HEADS * V_DIM
MIX_WIDTH = POOL_WIDTH + FNO_WIDTH + ATTN_WIDTH
COL_FNO = POOL_WIDTH
COL_Q = COL_FNO + FNO_WIDTH
COL_KV = COL_Q + Q_LORA
COL_KR = COL_KV + KV_LORA
IN_WIDTH = COL_KR + QK_ROPE
ROPE_AXIS_DIM = QK_ROPE // 2
ROPE_FREQS = ROPE_AXIS_DIM // 2
ROPE_THETA = 10000.0
SOFTMAX_SCALE = (QK_NOPE + QK_ROPE) ** -0.5
Q_BLOCK = 128
N_EXPERTS = 64
TOP_K = 8
N_EXPERT_GROUPS = 8
TOPK_GROUPS = 4
EXPERTS_PER_GROUP = N_EXPERTS // N_EXPERT_GROUPS
D_EXPERT = 256
D_SHARED = 256
ROUTED_SCALE = 2.5
EXPERT_BLOCK = 128
BLOCKS_PER_STEP = 8

kernel_name = "hybrid_pool_fourier_mla_moe_dit"

def rmsnorm(x, g):
    xf = x.astype(jnp.float32)
    y = xf * lax.rsqrt(jnp.mean(xf * xf, axis=-1, keepdims=True) + EPS)
    return y.astype(x.dtype) * g

def modulate(h, shift, scale):
    return h * (1.0 + scale) + shift

def axial_rope_tables(n_tokens):
    rows = n_tokens // GRID_W
    row = jnp.repeat(jnp.arange(rows, dtype=jnp.float32), GRID_W)
    col = jnp.tile(jnp.arange(GRID_W, dtype=jnp.float32), rows)
    inv_freq = ROPE_THETA ** (-jnp.arange(ROPE_FREQS, dtype=jnp.float32) * 2.0 / ROPE_AXIS_DIM)
    ang = jnp.stack([row[:, None] * inv_freq, col[:, None] * inv_freq], axis=1)
    return jnp.cos(ang), jnp.sin(ang)

def rope2d(x, cos, sin):
    xr = x.reshape(x.shape[:-1] + (2, 2, ROPE_FREQS))
    x1, x2 = xr[..., 0, :], xr[..., 1, :]
    cos, sin = cos.astype(x.dtype), sin.astype(x.dtype)
    out = jnp.stack([x1 * cos - x2 * sin, x2 * cos + x1 * sin], axis=-2)
    return out.reshape(x.shape)

def pool_mixer(u, w_pool, pool_scale):
    B, L, _ = u.shape
    ug = u.astype(jnp.float32).reshape(B, L, N_POOL_GROUPS, POOL_GROUP_DIM)
    cs = jnp.concatenate([jnp.zeros((B, 1, N_POOL_GROUPS, POOL_GROUP_DIM), jnp.float32),
                          jnp.cumsum(ug, axis=1)], axis=1)
    half = jnp.array(POOL_WINDOWS, jnp.int32) // 2
    t = jnp.arange(L, dtype=jnp.int32)[:, None]
    lo = jnp.clip(t - half, 0, L)
    hi = jnp.clip(t + half, 0, L)
    grp = jnp.arange(N_POOL_GROUPS)[None, :]
    win_sum = cs[:, hi, grp] - cs[:, lo, grp]
    count = (hi - lo).astype(jnp.float32)[None, :, :, None]
    d = (win_sum / count - ug).astype(u.dtype)
    y = jnp.einsum('blgc,gcd->blgd', d, w_pool).reshape(B, L, POOL_WIDTH)
    return y * pool_scale

def fourier_mixer(u, w_fno):
    B, L, _ = u.shape
    ug = u.astype(jnp.float32).reshape(B, L, N_FNO_GROUPS, FNO_GROUP_DIM)
    f = jnp.fft.fft2(ug, axes=(1, 3), norm='ortho').real.astype(u.dtype)
    return jnp.einsum('blgc,gcd->blgd', f, w_fno).reshape(B, L, FNO_WIDTH)

def mla_queries(u, g_q, w_uq):
    B, L, _ = u.shape
    cq = rmsnorm(u[..., COL_Q:COL_KV], g_q)
    return (cq @ w_uq).reshape(B, L, N_HEADS, QK_NOPE + QK_ROPE)

def mla_keys_values(u_kvr, g_kv, w_ukv, rope=None):
    B, L, _ = u_kvr.shape
    ckv = rmsnorm(u_kvr[..., :KV_LORA], g_kv)
    kv = (ckv @ w_ukv).reshape(B, L, N_HEADS, QK_NOPE + V_DIM)
    k_rope = u_kvr[..., KV_LORA:]
    if rope is not None:
        k_rope = rope2d(k_rope, rope[0], rope[1])
    k = jnp.concatenate([kv[..., :QK_NOPE],
                         jnp.broadcast_to(k_rope[:, :, None, :], (B, L, N_HEADS, QK_ROPE))], axis=-1)
    return k, kv[..., QK_NOPE:]

def attend(q, k, v):
    s = jnp.einsum('bqhd,bkhd->bhqk', q, k).astype(jnp.float32) * SOFTMAX_SCALE
    p = jax.nn.softmax(s, axis=-1).astype(v.dtype)
    return jnp.einsum('bhqk,bkhd->bqhd', p, v)

def latent_attention(q, k, v, k_ctx, v_ctx):
    B, L, H, Dqk = q.shape
    keys = jnp.concatenate([k_ctx, k], axis=1)
    vals = jnp.concatenate([v_ctx, v], axis=1)
    nb = L // Q_BLOCK
    qb = q.reshape(B, nb, Q_BLOCK, H, Dqk).transpose(1, 0, 2, 3, 4)
    o = lax.map(lambda qblk: attend(qblk, keys, vals), qb)
    return o.transpose(1, 0, 2, 3, 4).reshape(B, L, H * V_DIM)

def head_groups_output(u, attn_out, w_pool, pool_scale, w_fno, w_out):
    y = jnp.concatenate([pool_mixer(u[..., :COL_FNO], w_pool, pool_scale),
                         fourier_mixer(u[..., COL_FNO:COL_Q], w_fno),
                         attn_out], axis=-1)
    return y @ w_out

def route(h, w_router, router_bias):
    T = h.shape[0]
    s = jax.nn.sigmoid((h @ w_router).astype(jnp.float32))
    sel = s + router_bias.astype(jnp.float32)
    grp_score = lax.top_k(sel.reshape(T, N_EXPERT_GROUPS, EXPERTS_PER_GROUP), 2)[0].sum(-1)
    _, top_g = lax.top_k(grp_score, TOPK_GROUPS)
    gmask = jax.nn.one_hot(top_g, N_EXPERT_GROUPS, dtype=jnp.float32).sum(1) > 0
    emask = jnp.repeat(gmask, EXPERTS_PER_GROUP, axis=1)
    _, idx = lax.top_k(jnp.where(emask, sel, -jnp.inf), TOP_K)
    w = jnp.take_along_axis(s, idx, axis=1)
    w = w / jnp.sum(w, axis=-1, keepdims=True) * ROUTED_SCALE
    return idx, w

def moe_ffn(h, w_router, router_bias, w_gate, w_up, w_down, w_sh_gate, w_sh_up, w_sh_down):
    T = h.shape[0]
    idx, wts = route(h, w_router, router_bias)
    n_assign = T * TOP_K
    e_flat = idx.reshape(-1)
    tok_flat = jnp.arange(n_assign, dtype=jnp.int32) // TOP_K
    order = jnp.argsort(e_flat)
    e_sorted = e_flat[order]
    tok_sorted = tok_flat[order]
    w_sorted = wts.reshape(-1)[order]
    counts = jnp.zeros((N_EXPERTS,), jnp.int32).at[e_flat].add(1)
    padded = (counts + EXPERT_BLOCK - 1) // EXPERT_BLOCK * EXPERT_BLOCK
    pad_end = jnp.cumsum(padded)
    pad_start = pad_end - padded
    start = jnp.cumsum(counts) - counts
    dest = pad_start[e_sorted] + jnp.arange(n_assign, dtype=jnp.int32) - start[e_sorted]
    step_rows = EXPERT_BLOCK * BLOCKS_PER_STEP
    n_steps = -(-(n_assign + N_EXPERTS * (EXPERT_BLOCK - 1)) // step_rows)
    n_rows = n_steps * step_rows
    src = jnp.zeros((n_rows,), jnp.int32).at[dest].set(tok_sorted)
    row_w = jnp.zeros((n_rows,), h.dtype).at[dest].set(w_sorted.astype(h.dtype))
    block_start = jnp.arange(n_rows // EXPERT_BLOCK, dtype=jnp.int32) * EXPERT_BLOCK
    block_expert = jnp.minimum(jnp.searchsorted(pad_end, block_start, side='right'), N_EXPERTS - 1)

    def run_step(args):
        src_s, exp_s, w_s = args
        xb = h[src_s]
        a = jnp.einsum('nmd,ndf->nmf', xb, w_gate[exp_s])
        b = jnp.einsum('nmd,ndf->nmf', xb, w_up[exp_s])
        y = jnp.einsum('nmf,nfd->nmd', jax.nn.silu(a) * b, w_down[exp_s])
        return y * w_s[..., None]

    y = lax.map(run_step, (src.reshape(n_steps, BLOCKS_PER_STEP, EXPERT_BLOCK),
                           block_expert.reshape(n_steps, BLOCKS_PER_STEP),
                           row_w.reshape(n_steps, BLOCKS_PER_STEP, EXPERT_BLOCK)))
    routed = jax.ops.segment_sum(y.reshape(n_rows, -1), src, num_segments=T)
    shared = (jax.nn.silu(h @ w_sh_gate) * (h @ w_sh_up)) @ w_sh_down
    return routed + shared

def setup_inputs(seed: int = 0) -> dict:
    key = jax.random.key(seed)
    ks = jax.random.split(key, 26)

    def nrm(k, shape, scale):
        return scale * jax.random.normal(k, shape, jnp.float32)

    def gain(k, shape):
        return 1.0 + 0.1 * jax.random.normal(k, shape, jnp.float32)

    return {
        "x": nrm(ks[0], (BATCH, SEQ, D_MODEL), 1.0),
        "c": nrm(ks[1], (BATCH, D_MODEL), 1.0),
        "ctx": nrm(ks[2], (BATCH, CTX_LEN, D_MODEL), 1.0),
        "c_ctx": nrm(ks[3], (D_MODEL,), 1.0),
        "w_mod": nrm(ks[4], (DEPTH, D_MODEL, N_MOD * D_MODEL), 0.5 * D_MODEL ** -0.5),
        "b_mod": nrm(ks[5], (DEPTH, N_MOD * D_MODEL), 0.02),
        "g_mix": gain(ks[6], (DEPTH, D_MODEL)),
        "g_ffn": gain(ks[7], (DEPTH, D_MODEL)),
        "w_in": nrm(ks[8], (DEPTH, D_MODEL, IN_WIDTH), D_MODEL ** -0.5),
        "w_pool": nrm(ks[9], (DEPTH, N_POOL_GROUPS, POOL_GROUP_DIM, POOL_GROUP_DIM), POOL_GROUP_DIM ** -0.5),
        "pool_scale": gain(ks[10], (DEPTH, POOL_WIDTH)),
        "w_fno": nrm(ks[11], (DEPTH, N_FNO_GROUPS, FNO_GROUP_DIM, FNO_GROUP_DIM), FNO_GROUP_DIM ** -0.5),
        "g_q": gain(ks[12], (DEPTH, Q_LORA)),
        "w_uq": nrm(ks[13], (DEPTH, Q_LORA, N_HEADS * (QK_NOPE + QK_ROPE)), Q_LORA ** -0.5),
        "g_kv": gain(ks[14], (DEPTH, KV_LORA)),
        "w_ukv": nrm(ks[15], (DEPTH, KV_LORA, N_HEADS * (QK_NOPE + V_DIM)), KV_LORA ** -0.5),
        "w_out": nrm(ks[16], (DEPTH, MIX_WIDTH, D_MODEL), MIX_WIDTH ** -0.5),
        "w_router": nrm(ks[17], (DEPTH, D_MODEL, N_EXPERTS), D_MODEL ** -0.5),
        "router_bias": nrm(ks[18], (DEPTH, N_EXPERTS), 0.01),
        "w_gate": nrm(ks[19], (DEPTH, N_EXPERTS, D_MODEL, D_EXPERT), D_MODEL ** -0.5),
        "w_up": nrm(ks[20], (DEPTH, N_EXPERTS, D_MODEL, D_EXPERT), D_MODEL ** -0.5),
        "w_down": nrm(ks[21], (DEPTH, N_EXPERTS, D_EXPERT, D_MODEL), D_EXPERT ** -0.5),
        "w_sh_gate": nrm(ks[22], (DEPTH, D_MODEL, D_SHARED), D_MODEL ** -0.5),
        "w_sh_up": nrm(ks[23], (DEPTH, D_MODEL, D_SHARED), D_MODEL ** -0.5),
        "w_sh_down": nrm(ks[24], (DEPTH, D_SHARED, D_MODEL), D_SHARED ** -0.5),
        "g_final": gain(ks[25], (D_MODEL,)),
    }

def reference(x, c, ctx, c_ctx, w_mod, b_mod, g_mix, g_ffn, w_in, w_pool, pool_scale, w_fno,
              g_q, w_uq, g_kv, w_ukv, w_out, w_router, router_bias, w_gate, w_up, w_down,
              w_sh_gate, w_sh_up, w_sh_down, g_final):
    B, L, D = x.shape
    Lc = ctx.shape[1]
    cos, sin = axial_rope_tables(L)
    silu_c = jax.nn.silu(c)
    silu_cc = jax.nn.silu(c_ctx)
    xc = ctx
    for l in range(DEPTH):
        last = l == DEPTH - 1
        mod = silu_c @ w_mod[l] + b_mod[l]
        modc = silu_cc @ w_mod[l] + b_mod[l]
        sh1, sc1, gt1, sh2, sc2, gt2 = [m[:, None, :] for m in jnp.split(mod, N_MOD, axis=-1)]
        shc1, scc1, gtc1, shc2, scc2, gtc2 = jnp.split(modc, N_MOD, axis=-1)
        w_in_l = w_in[l]

        h = modulate(rmsnorm(x, g_mix[l]), sh1, sc1)
        hc = modulate(rmsnorm(xc, g_mix[l]), shc1, scc1)
        u = h @ w_in_l
        if last:
            uc_kvr = hc @ w_in_l[:, COL_KV:]
        else:
            uc = hc @ w_in_l
            uc_kvr = uc[..., COL_KV:]
        k_ctx, v_ctx = mla_keys_values(uc_kvr, g_kv[l], w_ukv[l])
        q = mla_queries(u, g_q[l], w_uq[l])
        q = jnp.concatenate([q[..., :QK_NOPE], rope2d(q[..., QK_NOPE:], cos[:, None], sin[:, None])], axis=-1)
        k, v = mla_keys_values(u[..., COL_KV:], g_kv[l], w_ukv[l], rope=(cos, sin))
        attn = latent_attention(q, k, v, k_ctx, v_ctx)
        y = head_groups_output(u, attn, w_pool[l], pool_scale[l], w_fno[l], w_out[l])
        x = x + gt1 * y
        if not last:
            qc = mla_queries(uc, g_q[l], w_uq[l])
            attn_c = attend(qc, k_ctx, v_ctx).reshape(B, Lc, ATTN_WIDTH)
            yc = head_groups_output(uc, attn_c, w_pool[l], pool_scale[l], w_fno[l], w_out[l])
            xc = xc + gtc1 * yc

        h2 = modulate(rmsnorm(x, g_ffn[l]), sh2, sc2)
        if last:
            out = moe_ffn(h2.reshape(B * L, D), w_router[l], router_bias[l], w_gate[l], w_up[l],
                          w_down[l], w_sh_gate[l], w_sh_up[l], w_sh_down[l])
            x = x + gt2 * out.reshape(B, L, D)
        else:
            hc2 = modulate(rmsnorm(xc, g_ffn[l]), shc2, scc2)
            tokens = jnp.concatenate([h2.reshape(B * L, D), hc2.reshape(B * Lc, D)], axis=0)
            out = moe_ffn(tokens, w_router[l], router_bias[l], w_gate[l], w_up[l],
                          w_down[l], w_sh_gate[l], w_sh_up[l], w_sh_down[l])
            x = x + gt2 * out[:B * L].reshape(B, L, D)
            xc = xc + gtc2 * out[B * L:].reshape(B, Lc, D)
    return rmsnorm(x, g_final)


_drawn_inputs = setup_inputs


def setup_inputs(seed=0):
    import zlib

    import numpy as np

    out = dict(_drawn_inputs(seed))
    spreads = {}
    factors = {'g_q': 3.735}
    for name, (base, spread) in spreads.items():
        noise = np.random.default_rng([zlib.crc32(name.encode()), seed]).standard_normal(out[name].shape)
        drawn = base * np.exp(spread * noise) if base else spread * noise
        out[name] = __import__('jax').numpy.asarray(drawn.astype(out[name].dtype))
    for name, factor in factors.items():
        out[name] = (out[name] * factor).astype(out[name].dtype)
    return out
```

```python
from contextlib import ExitStack

import numpy as np

import concourse.bass as bass
from concourse import mybir

F32 = mybir.dt.float32
I32 = mybir.dt.int32
U32 = mybir.dt.uint32
ALU = mybir.AluOpType
ACT = mybir.ActivationFunctionType
AX = mybir.AxisListType

P = 128
BANKS = 8
BANK = 512

D = 1024
DK = D // P
SEQ = 256
CTX = 256
DEPTH = 2
EPS = 1e-6
TILES = (SEQ + CTX) // P
LATENT_TILES = SEQ // P
STREAM_TILES = 2
TOKENS = TILES * P

GROUP = 64
POOL_WINDOWS = (2, 4, 8, 16)
COL_FNO = 256
COL_Q = 512
Q_LORA = 384
KV_LORA = 256
COL_KV = COL_Q + Q_LORA
COL_KR = COL_KV + KV_LORA
IN_WIDTH = COL_KR + 32
HEADS = 8
NOPE = 64
ROPE = 32
QK = NOPE + ROPE
V_DIM = 64
SCALE = QK ** -0.5
GRID_W = 64
ROPE_FREQS = 8
ROPE_THETA = 10000.0

EXPERTS = 64
TOP_K = 8
EGROUPS = 8
TOP_GROUPS = 4
FE = 256
ROUTED_SCALE = 2.5
AHEAD = 4
LISTED = EXPERTS + AHEAD
UNROLL = 8
SKIP = 65536
MAX_EXTRA = 64

MOD_N = 512
MOD_CHUNKS = 6 * D // MOD_N
MOD_SLOTS = 6

SLOT = 6144
GU_W = 2 * DK * FE
QTR = 8192


def active_tiles(layer):
    return TILES if layer < DEPTH - 1 else LATENT_TILES


def u_chunks(layer, t):
    if t < active_tiles(layer):
        return [(0, 512), (512, 1024), (1024, IN_WIDTH)]
    return [(COL_KV, IN_WIDTH)]


def units(layer):
    return [(qt, h) for qt in range(active_tiles(layer)) for h in range(HEADS)]


def keys_of(qt):
    return (0, TOKENS) if qt < LATENT_TILES else (SEQ, TOKENS)


def plan_jobs():
    jobs = []

    def add(eng, *key):
        jobs.append((key, eng))

    for l in range(DEPTH):
        nt = active_tiles(l)
        for t in range(TILES):
            add("act", l, "T1", t, 0)
            add("dve", l, "T1", t, 1)
        n = 0
        for t in range(TILES):
            for c in range(len(u_chunks(l, t))):
                add(("act", "dve")[n % 2], l, "U", t, c)
                n += 1
        for s in range(nt // STREAM_TILES):
            for c in range(2):
                add("act", l, "POOLED", s, c)
            for c in range(2):
                add("dve", l, "DFT_POS", s, c)
            for c in range(2):
                add("dve", l, "POOL_OUT", s, c)
            for c in range(2):
                add("act", l, "DFT_CH", s, c)
            for c in range(2):
                add("act", l, "FNO_OUT", s, c)
        for t in range(TILES):
            if t < nt:
                add("act", l, "CQ", t)
            add("dve", l, "CKV", t)
        for t in range(TILES + 1):
            if t < TILES:
                if t < nt:
                    add("act", l, "Q", t, 0)
                    add("dve", l, "Q", t, 1)
                add("act", l, "KV", t, 0)
                add("dve", l, "KV", t, 1)
            if t >= 1:
                for g in range(2):
                    if t - 1 < nt:
                        add("act", l, "QT", t - 1, g)
                    add("dve", l, "KT", t - 1, g)
        m = len(units(l))
        for i in range(m + 3):
            if i < m:
                add("act", l, "S", i)
            if 2 <= i < m + 2:
                add("act", l, "PT", i - 2)
            if 3 <= i:
                add("dve", l, "O", i - 3)
        for t in range(nt):
            for c in range(2):
                add("dve", l, "OUT", t, c)
        for t in range(nt):
            add("act", l, "T2", t, 0)
            add("dve", l, "T2", t, 1)
        for t in range(nt):
            add("act", l, "R", t)
        for t in range(nt + 1):
            if t < nt:
                add("dve", l, "SG", t)
            if t >= 1:
                add("act", l, "SH", t - 1)
                add("dve", l, "SD", t - 1, 0)
                add("dve", l, "SD", t - 1, 1)
        add("dve", l, "MT")
        add("dve", l, "RANK")
        add("dve", l, "POS")
        add("dve", l, "ENDS")
        add("dve", l, "EXTRA")
    return jobs


class Jobs:

    def __init__(self):
        self.number, self.by, self.nth = {}, {}, {}
        count = {"act": 0, "dve": 0}
        self.order = plan_jobs()
        for n, (key, eng) in enumerate(self.order):
            count[eng] += 1
            self.number[key], self.by[key], self.nth[key] = n, eng, count[eng]
        self.total = count

    def bank(self, *key):
        return self.number[key] % BANKS

    def filled(self, *key):
        return self.number[key] + 1

    def before(self, *key):
        n = self.number[key] - BANKS
        return self.order[n][0] if n >= 0 else None


def build(nc, a, out):
    jobs = Jobs()
    with ExitStack() as ctx:
        def sb(name, shape, dt=F32):
            return ctx.enter_context(nc.sbuf_tensor(name, shape, dt))

        def sem(name):
            return ctx.enter_context(nc.semaphore(name))

        banks = [ctx.enter_context(nc.psum_tensor(f"bank{i}", [P, BANK], F32)) for i in range(BANKS)]

        mod_rows_d = nc.dram_tensor("mod_rows_d", [DEPTH, 2, 6 * D], F32, kind="Internal").ap()
        h2_d = [nc.dram_tensor(f"h2_d{l}", [active_tiles(l) * P, D], F32, kind="Internal").ap() for l in range(DEPTH)]
        expert_rows = [nc.dram_tensor(f"expert_rows{l}", [active_tiles(l) * P * TOP_K, D], F32, kind="Internal").ap() for l in range(DEPTH)]

        x_rows = sb("x_rows", [P, TILES, D])
        mods = sb("mods", [P, 2, 3, D])
        ident = sb("ident", [P, P])
        strict = sb("strict", [P, P])
        ones = sb("ones", [P, P])
        slots_iota = sb("slots_iota", [P, TOKENS])
        ends_rhs = sb("ends_rhs", [64, 128])
        token_cols = sb("token_cols", [P, 8])
        lane = sb("lane", [P, 1])
        tie = sb("tie", [P, 64])
        rope_tab = sb("rope_tab", [P, 2, 2, 16])
        g_lora = sb("g_lora", [P, Q_LORA + KV_LORA])
        w_router = sb("w_router", [P, DK, EXPERTS])
        r_bias = sb("r_bias", [P, EXPERTS])
        pool_scale = sb("pool_scale", [P, 2])
        cond = sb("cond", [P, 2, DK])
        cond_silu = sb("cond_silu", [P, DK, 2])
        stats = sb("stats", [P, 4, 8])
        newton = sb("newton", [P, 8])
        soft = sb("soft", [P, 3, 32])
        row_idx = sb("row_idx", [P, UNROLL, 2], U32)
        row_w = sb("row_w", [P, UNROLL])
        extra_row = sb("extra_row", [1, 3 * MAX_EXTRA], I32)

        ring = sb("ring", [P, 4 * SLOT])
        arena = sb("arena", [P, 15488])

        def view(lo, n, *shape):
            v = arena[:, lo:lo + n]
            return split(v, shape)

        def split(v, shape):
            if len(shape) == 1:
                return v
            if len(shape) == 2:
                return v.rearrange("p (a b) -> p a b", b=shape[1])
            return v.rearrange("p (a b c) -> p a b c", b=shape[1], c=shape[2])

        A, B, U, C = 0, 4096, 8192, 12928
        bias_rows = arena[0:2, 0:6 * D]
        mod_rows = arena[0:2, 6144:6144 + 6 * D]
        gain_rows = arena[0:2, 12288:12288 + 2 * D]
        mod_w = ring[:, :].rearrange("p (s k n) -> p s k n", s=MOD_SLOTS, k=DK)
        h_rows = view(A, 4096, TILES, D)
        mixed = view(A, 4096, DK, TOKENS)
        pooled = view(A + 2048, 512, 2, SEQ)
        dft_pos = view(A + 2560, 1024, 2, 2 * SEQ)
        dft_ch = view(A + 3584, 512, 2, SEQ)
        h_T = view(B, 4096, DK, TOKENS)
        q_rows = view(B, 1536, 2, HEADS * QK)
        k_rows = view(B + 1536, 1536, 2, HEADS * QK)
        square_out = view(B + 3072, 512, 512)
        rope_tmp = view(B + 3584, 512, 4, 128)
        u_rows = view(U, TILES * IN_WIDTH, TILES, IN_WIDTH)
        p_rows = view(U, 1024, 2, 512)
        p_T = view(U + 1024, 1024, 2, 512)
        res_tmp = view(U + 2048, 1024, 2, 512)
        c_T = view(C, 2560, 5, TOKENS)
        x_g = view(A, 4096, 4, D)
        x_gT = view(B, 2048, 2, DK, P)
        y_g = view(B + 2048, 2048, 2, D)
        one_hot = view(U, 1024, 2, TILES, P)
        vals = view(U + 1024, TILES * LISTED * 3, TILES, LISTED, 3)
        posm = view(U + 1840, TILES * LISTED, TILES, LISTED)
        hid = view(U + 2112, 512, 2, FE)
        sig = view(U + 2624, 512, 2, FE)
        hid_T = view(U + 3136, 512, 2, 2, P)
        moe_tmp = view(U + 3648, 1024, 2, 512)
        prob = view(C, 256, TILES, EXPERTS)
        sel = view(C + 256, 256, TILES, EXPERTS)
        top2 = view(C + 512, 256, TILES, EGROUPS, 8)
        cmp_a = view(C + 768, 256, TILES, EGROUPS, 8)
        cmp_b = view(C + 1024, 256, TILES, EGROUPS, 8)
        chosen = view(C + 1280, 256, TILES, EXPERTS)
        small = view(C + 1536, 256, 256)
        ranks_T = view(C + 1792, 512, TILES, P)
        gscore = split(small[:, 0:32], (TILES, 8))
        gmask = split(small[:, 32:64], (TILES, 8))
        gneg = split(small[:, 64:96], (TILES, 8))
        top8 = split(small[:, 96:128], (TILES, 8))
        wsum = small[:, 128:132]
        winv = small[:, 132:136]
        ext = small[:, 136:138]
        ext_b = top2.rearrange("p a b c -> p (a b c)")[0:64, 0:128]
        ends = cmp_a.rearrange("p a b c -> p (a b c)")
        table = small[:, 138:141]

        w_in = ring[:, 0:DK * IN_WIDTH].rearrange("p (k n) -> p k n", k=DK)
        w_out = ring[:, 0:8192].rearrange("p (k n) -> p k n", k=DK)
        k_T = ring[:, 8192:12288].rearrange("p (h n) -> p h n", h=HEADS)
        pool_m = ring[:, 9728:11776].rearrange("p (t g n) -> p t g n", t=2, g=4)
        w_uq = ring[:, 12288:12288 + 2304].rearrange("p (k n) -> p k n", k=3)
        w_ukv = ring[:, 14592:14592 + 2048].rearrange("p (k n) -> p k n", k=2)
        dft_l = ring[:, 16640:16640 + 1024].rearrange("p (t n) -> p t n", t=2)
        dft_c = ring[:, 17664:17664 + 256].rearrange("p (t n) -> p t n", t=2)
        w_poolb = ring[:, 17920:18176].rearrange("p (c n) -> p c n", c=2)
        w_fnob = ring[:, 18176:18432].rearrange("p (c n) -> p c n", c=2)
        q_T = ring[:, 18432:18432 + 4096].rearrange("p (h n) -> p h n", h=HEADS)
        v_rows = ring[:, 22528:22528 + 2048].rearrange("p (t n) -> p t n", t=TILES)
        y_all = ring[:, 0:3 * QTR].rearrange("p (t n) -> p t n", t=3)

        def slot_gu(s):
            return ring[:, s * SLOT:s * SLOT + GU_W].rearrange("p (g k f) -> p g k f", g=2, k=DK)

        def slot_dn(s):
            return ring[:, s * SLOT + GU_W:(s + 1) * SLOT].rearrange("p (j n) -> p j n", j=2)

        def expert_slot(i):
            return (i + 3) % 4

        SHARED_SLOT = 2

        psum_filled = sem("psum_filled")
        drained = {"act": sem("drained_by_act"), "dve": sem("drained_by_dve")}
        dve_link = sem("dve_link")
        act_link = sem("act_link")
        const_in = sem("const_in")
        cond_in = sem("cond_in")
        cond_sig = sem("cond_sig")
        cond_ready = sem("cond_ready")
        x_in = sem("x_in")
        ones_ready = sem("ones_ready")
        mod_w_in = [sem(f"mod_w_in{s}") for s in range(MOD_SLOTS)]
        mod_bias_in = sem("mod_bias_in")
        mod_filled = sem("mod_filled")
        mod_added = sem("mod_added")
        mod_ready = sem("mod_ready")
        mod_stored = sem("mod_stored")
        out_stored = sem("out_stored")
        row_moves = sem("row_moves")

        def layer_sems(l):
            named = {name: sem(f"{name}_{l}") for name in (
                "mods_in", "w_in_in", "w_lora_in", "mixer_in", "w_out_in", "router_in", "norm_sums",
                "norm_var", "norm_root", "h_ready", "lora_sums", "lora_var", "lora_root", "lora_ready",
                "q_rotated", "k_ready", "row_max", "p_ready", "x_mixed", "norm2_sums", "norm2_var",
                "norm2_root", "h2_ready", "h2_stored", "shared_in", "shared_sig", "chosen_ready",
                "table_ready", "extra_ready", "g_ready", "list_filled", "idx_ready", "xt_filled", "xt_act",
                "xt_dve", "gu_filled", "sig_ready", "hid_part", "hid_ready", "ht_filled", "ht_drained",
                "d_filled", "y_act", "y_dve", "e_w", "e_x", "rows_back", "last_gain_in", "x_done",
            )}
            many = {name: [sem(f"{name}{s}_{l}") for s in range(n)]
                    for name, n in (("gu_in", 4), ("dn_in", 4), ("gathered", 4), ("scattered", 2), ("y_in", 3))}
            return {**named, **many}

        L = [layer_sems(l) for l in range(DEPTH)]

        def ge(eng, s, value):
            if not (isinstance(value, int) and value <= 0):
                eng.wait_ge(s, value)

        def wait_drained(eng, *key):
            eng.wait_ge(drained[jobs.by[key]], jobs.nth[key])

        def wait_filled(eng, *key):
            eng.wait_ge(psum_filled, jobs.filled(*key))

        def bank_of(*key):
            return banks[jobs.bank(*key)]

        block = ctx.enter_context(nc.Block())

        @block.sync
        def _(sp):
            sp.dma_start(cond[:, 0, :], a["c"].rearrange("a (p k) -> (a p) k", k=DK)).then_inc(cond_in, 16)
            sp.dma_start(cond[:, 1, :], a["c_ctx"].rearrange("(p k) -> p k", k=DK)).then_inc(cond_in, 16)
            for l in range(DEPTH):
                wm = a["w_mod"][l].rearrange("(p k) n -> p k n", k=DK)
                if l == 0:
                    for s in range(MOD_SLOTS):
                        sp.dma_start(mod_w[:, s], wm[:, :, s * MOD_N:(s + 1) * MOD_N]).then_inc(mod_w_in[s], 16)
                    first = 1
                else:
                    first = 0
                with sp.Fori(first, MOD_CHUNKS // MOD_SLOTS) as j:
                    for s in range(MOD_SLOTS):
                        sp.wait_ge(mod_filled, l * MOD_CHUNKS + j * MOD_SLOTS + s + 1 - MOD_SLOTS)
                        sp.dma_start(mod_w[:, s], wm[:, :, bass.ds((j * MOD_SLOTS + s) * MOD_N, MOD_N)]).then_inc(mod_w_in[s], 16)
            for dst, name in ((ident, "k_ident"), (strict, "k_strict"), (slots_iota, "k_iota"), (ends_rhs, "k_ends"),
                              (token_cols, "k_token"), (lane, "k_lane"), (tie, "k_tie")):
                sp.dma_start(dst[:, :], a[name]).then_inc(const_in, 16)
            sp.dma_start(rope_tab[:, :, :, :], a["k_rope"]).then_inc(const_in, 16)
            sp.dma_start(x_rows[:, 0:2, :], a["x"].rearrange("a (t p) n -> p (a t) n", p=P)).then_inc(x_in, 16)
            sp.dma_start(x_rows[:, 2:4, :], a["ctx"].rearrange("a (t p) n -> p (a t) n", p=P)).then_inc(x_in, 16)

            for l in range(DEPTH):
                S = L[l]
                nt = active_tiles(l)
                if l == 0:
                    sp.wait_ge(mod_filled, DEPTH * MOD_CHUNKS)
                else:
                    sp.wait_ge(L[l - 1]["x_done"], active_tiles(l - 1))
                sp.dma_start(w_in, a["w_in"][l].rearrange("(k p) n -> p k n", p=P)).then_inc(S["w_in_in"], 16)
                sp.dma_start(w_uq, a["w_uq"][l].rearrange("(k p) n -> p k n", p=P)).then_inc(S["w_lora_in"], 16)
                sp.dma_start(w_ukv, a["w_ukv"][l].rearrange("(k p) n -> p k n", p=P)).then_inc(S["w_lora_in"], 16)
                sp.dma_start(g_lora[:, 0:Q_LORA], a["g_q"][l].partition_broadcast(P)).then_inc(S["w_lora_in"], 16)
                sp.dma_start(g_lora[:, Q_LORA:], a["g_kv"][l].partition_broadcast(P)).then_inc(S["w_lora_in"], 16)
                sp.dma_start(pool_m, a["k_pool"]).then_inc(S["mixer_in"], 16)
                sp.dma_start(dft_l, a["k_dft_l"]).then_inc(S["mixer_in"], 16)
                sp.dma_start(dft_c, a["k_dft_c"]).then_inc(S["mixer_in"], 16)
                sp.dma_start(pool_scale[:, :], a["pool_scale"][l].rearrange("(c p) -> p c", p=P),
                             allow_slow_non_contiguous=True).then_inc(S["mixer_in"], 16)
                sp.dma_start(w_poolb, a["k_zero"]).then_inc(S["mixer_in"], 16)
                sp.dma_start(w_fnob, a["k_zero"]).then_inc(S["mixer_in"], 16)
                sp.wait_ge(S["mixer_in"], 6 * 16)
                for g in range(4):
                    lo = GROUP * (g % 2)
                    sp.dma_start(w_poolb[lo:lo + GROUP, g // 2, lo:lo + GROUP], a["w_pool"][l, g]).then_inc(S["mixer_in"], 16)
                    sp.dma_start(w_fnob[lo:lo + GROUP, g // 2, lo:lo + GROUP], a["w_fno"][l, g]).then_inc(S["mixer_in"], 16)
                sp.dma_start(w_router[:, :, :], a["w_router"][l].rearrange("(p k) n -> p k n", k=DK)).then_inc(S["router_in"], 16)
                sp.dma_start(r_bias[:, :], a["router_bias"][l].partition_broadcast(P)).then_inc(S["router_in"], 16)
                wait_filled(sp, l, "U", TILES - 1, len(u_chunks(l, TILES - 1)) - 1)
                sp.dma_start(w_out, a["w_out"][l].rearrange("(k p) n -> p k n", p=P)).then_inc(S["w_out_in"], 16)
                wait_filled(sp, l, "KV", TILES - 1, 1)
                gu = slot_gu(SHARED_SLOT)
                sp.dma_start(gu[:, 0], a["w_sh_gate"][l].rearrange("(p k) f -> p k f", k=DK)).then_inc(S["shared_in"], 16)
                sp.dma_start(gu[:, 1], a["w_sh_up"][l].rearrange("(p k) f -> p k f", k=DK)).then_inc(S["shared_in"], 16)
                sp.dma_start(slot_dn(SHARED_SLOT), a["w_sh_down"][l].rearrange("(p j) n -> p j n", j=2)).then_inc(S["shared_in"], 16)

                def load_expert(e, s):
                    gu = slot_gu(s)
                    for g, name in enumerate(("w_gate", "w_up")):
                        w = a[name][l].rearrange("e (p k) f -> e p k f", k=DK)
                        sp.dma_start(gu[:, g], w[bass.ds(e, 1)].rearrange("a p k f -> p (a k) f")).then_inc(S["gu_in"][s], 16)
                    w = a["w_down"][l].rearrange("e (p j) n -> e p j n", j=2)
                    sp.dma_start(slot_dn(s), w[bass.ds(e, 1)].rearrange("a p j n -> p (a j) n")).then_inc(S["dn_in"][s], 16)

                wait_filled(sp, l, "O", len(units(l)) - 1)
                load_expert(0, expert_slot(0))
                wait_filled(sp, l, "OUT", nt - 1, 1)
                load_expert(1, expert_slot(1))
                load_expert(2, expert_slot(2))
                wait_filled(sp, l, "SD", nt - 1, 1)
                load_expert(3, expert_slot(3))
                with sp.Fori(1, EXPERTS // 4) as j:
                    for s in range(4):
                        sp.wait_ge(S["d_filled"], j * 4 + s - 3)
                        load_expert(j * 4 + s, expert_slot(s))

                sp.wait_ge(S["extra_ready"], 1)
                n_extra = sp.value_load(extra_row[0:1, 0:1], min_val=0, max_val=MAX_EXTRA)
                sp.wait_ge(S["d_filled"], EXPERTS)
                with sp.If(n_extra > 0):
                    with sp.Fori(0, n_extra) as o:
                        sp.wait_ge(S["d_filled"], o + EXPERTS)
                        e = sp.value_load(extra_row[0:1, bass.ds(o + MAX_EXTRA, 1)], min_val=0, max_val=EXPERTS - 1)
                        gu = slot_gu(0)
                        for g, name in enumerate(("w_gate", "w_up")):
                            w = a[name][l].rearrange("e (p k) f -> e p k f", k=DK)
                            sp.dma_start(gu[:, g], w[bass.ds(e, 1)].rearrange("a p k f -> p (a k) f")).then_inc(S["e_w"], 16)
                        w = a["w_down"][l].rearrange("e (p j) n -> e p j n", j=2)
                        sp.dma_start(slot_dn(0), w[bass.ds(e, 1)].rearrange("a p j n -> p (a j) n")).then_inc(S["e_w"], 16)
                for s in range(2):
                    sp.wait_ge(S["scattered"][s], 16 * (EXPERTS // 2))
                sp.wait_ge(S["rows_back"], 1)
                rows = expert_rows[l].rearrange("(t p k) n -> t p (k n)", p=P, k=TOP_K)
                for t in range(nt):
                    if t >= 3:
                        sp.wait_ge(S["x_done"], t - 2)
                    sp.dma_start(y_all[:, t % 3, :], rows[t]).then_inc(S["y_in"][t % 3], 16)
            sp.wait_ge(L[DEPTH - 1]["x_done"], LATENT_TILES + LATENT_TILES)
            sp.dma_start(out.rearrange("a (t p) n -> p (a t) n", p=P), h_rows[:, 0:2, :]).then_inc(out_stored, 16)
            sp.wait_ge(out_stored, 16)

        @block.gpsimd
        def _(pool):
            for l in range(DEPTH):
                if l:
                    pool.wait_ge(mod_stored, 16 * l)
                pool.dma_start(bias_rows, a["b_mod"][l].partition_broadcast(2)).then_inc(mod_bias_in, 16)
                pool.dma_start(gain_rows[:, 0:D], a["g_mix"][l].partition_broadcast(2)).then_inc(mod_bias_in, 16)
                pool.dma_start(gain_rows[:, D:], a["g_ffn"][l].partition_broadcast(2)).then_inc(mod_bias_in, 16)
                pool.wait_ge(mod_ready, l + 1)
                pool.dma_start(mod_rows_d[l], mod_rows).then_inc(mod_stored, 16)
            pool.wait_ge(mod_stored, 16 * DEPTH)

            def load_mods(l, half, signal):
                for s in range(2):
                    pool.dma_start(mods[:, s].rearrange("p a n -> p (a n)"),
                                   mod_rows_d[l, s, half * 3 * D:(half + 1) * 3 * D].partition_broadcast(P)).then_inc(signal, 16)

            for l in range(DEPTH):
                S = L[l]
                nt = active_tiles(l)
                if l:
                    pool.wait_ge(L[l - 1]["x_done"], active_tiles(l - 1))
                load_mods(l, 0, S["mods_in"])
                pool.wait_ge(S["x_mixed"], nt)
                load_mods(l, 1, S["mods_in"])
                for t in range(nt):
                    pool.wait_ge(S["h2_ready"], t + 1)
                    pool.dma_start(h2_d[l][t * P:(t + 1) * P, :], h_rows[:, t, :]).then_inc(S["h2_stored"], 16)

                last_token = pool.to_reg(nt * P - 1)
                last_row = pool.to_reg(nt * P * TOP_K - 1)

                def gather(slot, idx):
                    pool.sem_inc(row_moves, 1)
                    return pool.indirect_dma_start(
                        out=x_g[:, slot, :], out_offset=None, in_=h2_d[l],
                        in_offset=bass.IndirectOffsetOnAxis(ap=row_idx[:, idx, 0:1], axis=0),
                        bounds_check=last_token, oob_is_err=False)

                def scatter(slot, idx):
                    pool.sem_inc(row_moves, 1)
                    return pool.indirect_dma_start(
                        out=expert_rows[l], out_offset=bass.IndirectOffsetOnAxis(ap=row_idx[:, idx, 1:2], axis=0),
                        in_=y_g[:, slot, :], in_offset=None,
                        bounds_check=last_row, oob_is_err=False)

                if l == DEPTH - 1:
                    pool.wait_ge(S["mods_in"], 64)
                    pool.dma_start(mods[:, 1, 0, :], a["g_final"].partition_broadcast(P)).then_inc(S["last_gain_in"], 16)
                pool.wait_ge(S["h2_stored"], 16 * nt)
                wait_filled(pool, l, "T2", nt - 1, 1)
                for i in range(AHEAD):
                    pool.wait_ge(S["idx_ready"], i + 1)
                    gather(i % 4, i).then_inc(S["gathered"][i % 4], 16)

                def step(i, s):
                    pool.wait_ge(S["idx_ready"], i + AHEAD + 1)
                    pool.wait_ge(S["xt_filled"], i + 1)
                    gather(s % 4, (s + AHEAD) % UNROLL).then_inc(S["gathered"][s % 4], 16)
                    if not (isinstance(i, int) and i == 0):
                        pool.wait_ge(S["y_act"], i)
                        pool.wait_ge(S["y_dve"], i)
                        scatter((s - 1) % 2, (s - 1) % UNROLL).then_inc(S["scattered"][(s - 1) % 2], 16)

                for s in range(UNROLL):
                    step(s, s)
                with pool.Fori(1, EXPERTS // UNROLL) as j:
                    for s in range(UNROLL):
                        step(j * UNROLL + s, s)
                pool.wait_ge(S["y_act"], EXPERTS)
                pool.wait_ge(S["y_dve"], EXPERTS)
                scatter(1, UNROLL - 1).then_inc(S["scattered"][1], 16)
                for s in range(4):
                    pool.wait_ge(S["gathered"][s], 16 * (LISTED // 4))
                for s in range(2):
                    pool.wait_ge(S["scattered"][s], 16 * (EXPERTS // 2))
                pool.wait_ge(S["extra_ready"], 1)
                n_extra = pool.value_load(extra_row[0:1, 0:1], min_val=0, max_val=MAX_EXTRA)
                with pool.If(n_extra > 0):
                    with pool.Fori(0, n_extra) as o:
                        pool.wait_ge(S["idx_ready"], o + 1 + LISTED)
                        gather(0, 0).then_inc(S["e_x"], 16)
                        pool.wait_ge(S["y_act"], o + 1 + EXPERTS)
                        pool.wait_ge(S["y_dve"], o + 1 + EXPERTS)
                        scatter(0, 0).then_inc(S["e_x"], 16)

        @block.scalar
        def _(act):
            link = [0]

            def linked(ins):
                link[0] += 1
                ins.then_inc(act_link, 1)
                act.wait_ge(act_link, link[0])

            act.wait_ge(cond_in, 32)
            act.activation(cond_silu[:, :, :], cond[:, :, :].rearrange("p s k -> p k s"), ACT.Sigmoid).then_inc(cond_sig, 1)

            def drain(key, out, func=ACT.Copy, **kw):
                wait_filled(act, *key)
                act.activation(out, kw.pop("in_"), func, **kw).then_inc(drained["act"], 1)

            for l in range(DEPTH):
                S = L[l]
                nt = active_tiles(l)
                if l == 0:
                    act.wait_ge(x_in, 32)
                    act.wait_ge(mod_stored, 16 * DEPTH)
                else:
                    act.wait_ge(L[l - 1]["x_done"], active_tiles(l - 1))
                for t in range(TILES):
                    act.activation(h_rows[:, t, :], x_rows[:, t, :], ACT.Square, accum_out=stats[:, 0, t:t + 1]).then_inc(S["norm_sums"], 1)
                act.wait_ge(S["norm_var"], 1)
                act.activation(stats[:, 2, 0:TILES], stats[:, 1, 0:TILES], ACT.Sqrt).then_inc(S["norm_root"], 1)
                for t in range(TILES):
                    drain((l, "T1", t, 0), h_T[:, 0:4, t * P:(t + 1) * P], in_=split(bank_of(l, "T1", t, 0)[:, :], (4, P)))
                for t in range(TILES):
                    for c, (lo, hi) in enumerate(u_chunks(l, t)):
                        key = (l, "U", t, c)
                        if jobs.by[key] == "act":
                            drain(key, u_rows[:, t, lo:hi], in_=bank_of(*key)[:, 0:hi - lo])
                wait_drained(act, l, "U", TILES - 1, 0)
                wait_drained(act, l, "U", TILES - 1, len(u_chunks(l, TILES - 1)) - 1)
                wait_drained(act, l, "U", TILES - 2, len(u_chunks(l, TILES - 2)) - 1)
                wait_filled(act, l, "U", TILES - 1, len(u_chunks(l, TILES - 1)) - 1)
                for t in range(TILES):
                    if t < nt:
                        act.activation(square_out[:, 0:Q_LORA], u_rows[:, t, COL_Q:COL_KV], ACT.Square,
                                       accum_out=stats[:, 0, t:t + 1]).then_inc(act_link, 1)
                        link[0] += 1
                        act.wait_ge(act_link, link[0])
                    act.activation(square_out[:, 0:KV_LORA], u_rows[:, t, COL_KV:COL_KR], ACT.Square,
                                   accum_out=stats[:, 0, 4 + t:5 + t]).then_inc(act_link, 1)
                    link[0] += 1
                    act.wait_ge(act_link, link[0])
                act.activation(square_out[:, 0:1], stats[:, 0, 4:5], ACT.Copy).then_inc(S["lora_sums"], 1)
                act.wait_ge(S["lora_var"], 2 if nt else 1)
                act.activation(stats[:, 2, 4:8], stats[:, 1, 4:8], ACT.Sqrt).then_inc(S["lora_root"], 1)
                act.activation(stats[:, 2, 0:nt], stats[:, 1, 0:nt], ACT.Sqrt).then_inc(S["lora_root"], 1)
                for s in range(nt // 2):
                    for c in range(2):
                        key = (l, "POOLED", s, c)
                        if s:
                            wait_filled(act, l, "POOL_OUT", s - 1, c)
                        drain(key, pooled[:, c, :], in_=bank_of(*key)[:, 0:SEQ])
                    for c in range(2):
                        key = (l, "DFT_CH", s, c)
                        if s:
                            wait_filled(act, l, "FNO_OUT", s - 1, c)
                        drain(key, dft_ch[:, c, :], in_=bank_of(*key)[:, 0:SEQ])
                    for c in range(2):
                        key = (l, "FNO_OUT", s, c)
                        drain(key, mixed[:, 2 + c, s * SEQ:(s + 1) * SEQ], in_=bank_of(*key)[:, 0:SEQ])
                for t in range(nt):
                    drain((l, "CQ", t), c_T[:, 0:3, t * P:(t + 1) * P], in_=split(bank_of(l, "CQ", t)[:, 0:3 * P], (3, P)))
                for t in range(TILES + 1):
                    if t < TILES:
                        if t < nt:
                            drain((l, "Q", t, 0), q_rows[:, t % 2, 0:512], in_=bank_of(l, "Q", t, 0)[:, :], scale=SCALE)
                        key = (l, "KV", t, 0)
                        b = split(bank_of(*key)[:, :], (4, P))
                        wait_filled(act, *key)
                        act.activation(split(k_rows[:, t % 2, 0:4 * QK], (4, QK))[:, :, 0:NOPE], b[:, :, 0:NOPE], ACT.Copy)
                        act.activation(split(v_rows[:, t, 0:256], (4, V_DIM)), b[:, :, NOPE:], ACT.Copy).then_inc(drained["act"], 1)
                    if 1 <= t <= nt:
                        for g in range(2):
                            drain((l, "QT", t - 1, g), q_T[0:QK, 4 * g:4 * g + 4, (t - 1) * P:t * P],
                                  in_=split(bank_of(l, "QT", t - 1, g)[0:QK, :], (4, P)))
                m = len(units(l))
                for i in range(m + 2):
                    if i < m:
                        lo, hi = keys_of(units(l)[i][0])
                        n = hi - lo
                        wait_filled(act, l, "S", i)
                        act.wait_ge(S["row_max"], i + 1)
                        if i >= 2:
                            wait_filled(act, l, "PT", i - 2)
                        act.activation(p_rows[:, i % 2, 0:n], bank_of(l, "S", i)[:, 0:n], ACT.Exp, bias=soft[:, 0, i:i + 1],
                                       accum_out=soft[:, 1, i:i + 1]).then_inc(drained["act"], 1)
                    if i >= 2:
                        lo, hi = keys_of(units(l)[i - 2][0])
                        n = hi - lo
                        if i >= 4:
                            wait_filled(act, l, "O", i - 4)
                        drain((l, "PT", i - 2), p_T[:, i % 2, 0:n], in_=bank_of(l, "PT", i - 2)[:, 0:n])
                act.wait_ge(S["x_mixed"], nt)
                for t in range(nt):
                    act.activation(h_rows[:, t, :], x_rows[:, t, :], ACT.Square, accum_out=stats[:, 0, t:t + 1]).then_inc(S["norm2_sums"], 1)
                act.wait_ge(S["norm2_var"], 1)
                act.activation(stats[:, 2, 0:nt], stats[:, 1, 0:nt], ACT.Sqrt).then_inc(S["norm2_root"], 1)
                for t in range(nt):
                    drain((l, "T2", t, 0), h_T[:, 0:4, t * P:(t + 1) * P], in_=split(bank_of(l, "T2", t, 0)[:, :], (4, P)))
                for t in range(nt):
                    drain((l, "R", t), prob[:, t, :], ACT.Sigmoid, in_=bank_of(l, "R", t)[:, 0:EXPERTS])
                for t in range(nt + 1):
                    if t < nt:
                        wait_filled(act, l, "SG", t)
                        if t >= 2:
                            wait_drained(act, l, "SG", t - 2)
                        act.activation(sig[:, t % 2, :], bank_of(l, "SG", t)[:, 0:FE], ACT.Sigmoid).then_inc(S["shared_sig"], 1)
                    if t >= 1:
                        if t >= 3:
                            wait_filled(act, l, "SD", t - 3, 1)
                        drain((l, "SH", t - 1), hid_T[:, (t - 1) % 2], in_=split(bank_of(l, "SH", t - 1)[:, 0:2 * P], (2, P)))

                def x_drain(i, s):
                    act.wait_ge(S["xt_filled"], i + 1)
                    ge(act, S["gu_filled"], i - 1)
                    act.activation(x_gT[:, s % 2, 0:4, :], split(banks[0][:, :], (4, P)), ACT.Copy).then_inc(S["xt_act"], 1)

                x_drain(0, 0)

                def step(j, s):
                    i = j * UNROLL + s
                    x_drain(i + 1, s + 1)
                    act.wait_ge(S["gu_filled"], i + 1)
                    ge(act, S["hid_ready"], i - 1)
                    act.activation(sig[:, s % 2, :], banks[2 + s % 2][:, 0:FE], ACT.Sigmoid).then_inc(S["sig_ready"], 1)
                    if not (isinstance(i, int) and i == 0):
                        y_drain(i - 1, j, s - 1)

                def y_drain(i, j, s):
                    act.wait_ge(S["d_filled"], i + 1)
                    act.wait_ge(S["idx_ready"], i + 1)
                    ge(act, S["scattered"][s % 2], (j * (UNROLL // 2) + s // 2) * 16)
                    c = s % UNROLL
                    act.activation(y_g[:, s % 2, 0:512], banks[6][:, :], ACT.Copy, scale=row_w[:, c:c + 1]).then_inc(S["y_act"], 1)

                for s in range(UNROLL):
                    step(0, s)
                with act.Fori(1, EXPERTS // UNROLL) as j:
                    for s in range(UNROLL):
                        step(j, s)
                y_drain(EXPERTS - 1, EXPERTS // UNROLL - 1, UNROLL - 1)
                act.wait_ge(S["extra_ready"], 1)
                n_extra = act.value_load(extra_row[0:1, 0:1], min_val=0, max_val=MAX_EXTRA)
                with act.If(n_extra > 0):
                    with act.Fori(0, n_extra) as o:
                        act.wait_ge(S["xt_filled"], o + 1 + EXPERTS + 1)
                        act.activation(x_gT[:, 0, 0:4, :], split(banks[0][:, :], (4, P)), ACT.Copy).then_inc(S["xt_act"], 1)
                        act.wait_ge(S["gu_filled"], o + 1 + EXPERTS)
                        act.activation(sig[:, 0, :], banks[2][:, 0:FE], ACT.Sigmoid).then_inc(S["sig_ready"], 1)
                        act.wait_ge(S["d_filled"], o + 1 + EXPERTS)
                        act.activation(y_g[:, 0, 0:512], banks[6][:, :], ACT.Copy, scale=row_w[:, 0:1]).then_inc(S["y_act"], 1)
            act.wait_ge(L[DEPTH - 1]["x_done"], LATENT_TILES)
            fin = L[DEPTH - 1]
            for t in range(LATENT_TILES):
                act.activation(h_rows[:, t, :], x_rows[:, t, :], ACT.Square, accum_out=stats[:, 0, t:t + 1]).then_inc(fin["norm_sums"], 1)
            act.wait_ge(fin["norm_var"], 2)
            act.activation(stats[:, 2, 0:LATENT_TILES], stats[:, 1, 0:LATENT_TILES], ACT.Sqrt).then_inc(fin["norm_root"], 1)

        @block.vector
        def _(dve):
            link = [0]

            def linked(ins):
                link[0] += 1
                ins.then_inc(dve_link, 1)
                dve.wait_ge(dve_link, link[0])

            dve.memset(ones[:, :], 1.0).then_inc(ones_ready, 1)
            dve.wait_ge(cond_sig, 1)
            dve.tensor_tensor(cond_silu[:, :, :], cond_silu[:, :, :], cond[:, :, :].rearrange("p s k -> p k s"),
                              ALU.mult).then_inc(cond_ready, 1)
            for l in range(DEPTH):
                dve.wait_ge(mod_bias_in, 48 * (l + 1))
                with dve.Fori(0, MOD_CHUNKS // MOD_SLOTS) as j:
                    for s in range(MOD_SLOTS):
                        c = j * MOD_SLOTS + s
                        dve.wait_ge(mod_filled, l * MOD_CHUNKS + c + 1)
                        dve.tensor_tensor(mod_rows[:, bass.ds(c * MOD_N, MOD_N)], banks[s][0:2, :], bias_rows[:, bass.ds(c * MOD_N, MOD_N)],
                                          ALU.add).then_inc(mod_added, 1)
                dve.wait_ge(mod_added, (l + 1) * MOD_CHUNKS)
                linked(dve.scalar_tensor_tensor(out=mod_rows[:, D:2 * D], in0=mod_rows[:, D:2 * D], scalar=1.0,
                                                in1=gain_rows[:, 0:D], op0=ALU.add, op1=ALU.mult))
                dve.scalar_tensor_tensor(out=mod_rows[:, 4 * D:5 * D], in0=mod_rows[:, 4 * D:5 * D], scalar=1.0,
                                         in1=gain_rows[:, D:], op0=ALU.add, op1=ALU.mult).then_inc(mod_ready, 1)
                if l + 1 < DEPTH:
                    dve.wait_ge(mod_stored, 16 * (l + 1))

            def rstd(lo, hi, roots, value):
                v, root, r, tmp = stats[:, 1, lo:hi], stats[:, 2, lo:hi], stats[:, 3, lo:hi], newton[:, lo:hi]
                dve.wait_ge(roots, value)
                linked(dve.reciprocal(r, root))
                linked(dve.tensor_tensor(tmp, r, r, ALU.mult))
                linked(dve.tensor_tensor(tmp, tmp, v, ALU.mult))
                linked(dve.tensor_scalar(tmp, tmp, -0.5, 1.5, ALU.mult, ALU.add))
                linked(dve.tensor_tensor(r, r, tmp, ALU.mult))

            def normed(t, tiles, ready):
                s = t // STREAM_TILES
                linked(dve.scalar_tensor_tensor(out=h_rows[:, t, :], in0=x_rows[:, t, :], scalar=stats[:, 3, t:t + 1],
                                                in1=mods[:, s, 1, :], op0=ALU.mult, op1=ALU.mult))
                dve.tensor_tensor(h_rows[:, t, :], h_rows[:, t, :], mods[:, s, 0, :], ALU.add).then_inc(ready, 1)

            def drain(key, out, in_):
                wait_filled(dve, *key)
                dve.tensor_copy(out, in_).then_inc(drained["dve"], 1)

            def gated(key, t, c, tmp, last):
                s = t // STREAM_TILES
                wait_filled(dve, *key)
                dve.tensor_tensor(tmp, bank_of(*key)[:, :], mods[:, s, 2, c * 512:(c + 1) * 512], ALU.mult).then_inc(drained["dve"], 1)
                wait_drained(dve, *key)
                ins = dve.tensor_tensor(x_rows[:, t, c * 512:(c + 1) * 512], x_rows[:, t, c * 512:(c + 1) * 512], tmp, ALU.add)
                if last is not None:
                    ins.then_inc(last, 1)
                else:
                    linked(ins)

            dve.wait_ge(const_in, 8 * 16)
            for l in range(DEPTH):
                S = L[l]
                nt = active_tiles(l)
                dve.wait_ge(S["norm_sums"], TILES)
                dve.tensor_scalar(stats[:, 1, 0:TILES], stats[:, 0, 0:TILES], 1.0 / D, EPS, ALU.mult, ALU.add).then_inc(S["norm_var"], 1)
                rstd(0, TILES, S["norm_root"], 1)
                dve.wait_ge(S["mods_in"], 32)
                for t in range(TILES):
                    normed(t, TILES, S["h_ready"])
                for t in range(TILES):
                    drain((l, "T1", t, 1), h_T[:, 4:8, t * P:(t + 1) * P], split(bank_of(l, "T1", t, 1)[:, :], (4, P)))
                for t in range(TILES):
                    for c, (lo, hi) in enumerate(u_chunks(l, t)):
                        key = (l, "U", t, c)
                        if jobs.by[key] == "dve":
                            drain(key, u_rows[:, t, lo:hi], bank_of(*key)[:, 0:hi - lo])
                dve.wait_ge(S["lora_sums"], 1)
                dve.tensor_scalar(stats[:, 1, 0:nt], stats[:, 0, 0:nt], 1.0 / Q_LORA, EPS, ALU.mult, ALU.add).then_inc(S["lora_var"], 1)
                dve.tensor_scalar(stats[:, 1, 4:8], stats[:, 0, 4:8], 1.0 / KV_LORA, EPS, ALU.mult, ALU.add).then_inc(S["lora_var"], 1)
                rstd(0, nt, S["lora_root"], 2)
                rstd(4, 8, S["lora_root"], 2)
                dve.wait_ge(S["w_lora_in"], 64)
                for t in range(TILES):
                    if t < nt:
                        dve.scalar_tensor_tensor(out=u_rows[:, t, COL_Q:COL_KV], in0=u_rows[:, t, COL_Q:COL_KV], scalar=stats[:, 3, t:t + 1],
                                                 in1=g_lora[:, 0:Q_LORA], op0=ALU.mult, op1=ALU.mult)
                    dve.scalar_tensor_tensor(out=u_rows[:, t, COL_KV:COL_KR], in0=u_rows[:, t, COL_KV:COL_KR], scalar=stats[:, 3, 4 + t:5 + t],
                                             in1=g_lora[:, Q_LORA:], op0=ALU.mult, op1=ALU.mult).then_inc(S["lora_ready"], 1)
                dve.wait_ge(S["mixer_in"], 14 * 16)
                for s in range(nt // 2):
                    for c in range(2):
                        key = (l, "DFT_POS", s, c)
                        if s:
                            wait_filled(dve, l, "DFT_CH", s - 1, c)
                        drain(key, dft_pos[:, c, :], bank_of(*key)[:, :])
                    for c in range(2):
                        key = (l, "POOL_OUT", s, c)
                        wait_filled(dve, *key)
                        dve.tensor_scalar(mixed[:, c, s * SEQ:(s + 1) * SEQ], bank_of(*key)[:, 0:SEQ], pool_scale[:, c:c + 1], None,
                                          ALU.mult).then_inc(drained["dve"], 1)
                for t in range(TILES):
                    drain((l, "CKV", t), c_T[:, 3:5, t * P:(t + 1) * P], split(bank_of(l, "CKV", t)[:, 0:2 * P], (2, P)))

                def rotate(x1, x2, cos, sin, shape, last):
                    n = shape[0] * shape[1] * shape[2]
                    tmp = [split(rope_tmp[:, i, 0:n], shape) for i in range(4)]
                    for o, x, y in ((tmp[0], x1, cos), (tmp[1], x2, sin), (tmp[2], x2, cos)):
                        dve.tensor_tensor(o, x, y, ALU.mult)
                    linked(dve.tensor_tensor(tmp[3], x1, sin, ALU.mult))
                    dve.tensor_tensor(x1, tmp[0], tmp[1], ALU.subtract)
                    ins = dve.tensor_tensor(x2, tmp[2], tmp[3], ALU.add)
                    if last is None:
                        linked(ins)
                    else:
                        ins.then_inc(last, 1)
                        dve.wait_ge(last, rotations[0])

                rotations = [0]
                for t in range(TILES + 1):
                    if t < TILES:
                        if t < nt:
                            key = (l, "Q", t, 1)
                            wait_filled(dve, *key)
                            dve.tensor_scalar(q_rows[:, t % 2, 512:768], bank_of(*key)[:, 0:256], SCALE, None, ALU.mult).then_inc(drained["dve"], 1)
                            if t < LATENT_TILES:
                                wait_drained(dve, l, "Q", t, 0)
                                wait_drained(dve, l, "Q", t, 1)
                                q4 = q_rows[:, t % 2, :].rearrange("p (h q) -> p h q", h=HEADS)[:, :, NOPE:]
                                q4 = q4.rearrange("p h (x f) -> p h x f", x=4)
                                cos, sin = (split(rope_tab[:, t, i, :], (2, 8)).unsqueeze(1).broadcast_to([P, HEADS, 2, 8]) for i in range(2))
                                rotations[0] += 1
                                rotate(q4[:, :, 0::2, :], q4[:, :, 1::2, :], cos, sin, (HEADS, 2, 8), S["q_rotated"])
                        kr = u_rows[:, t, COL_KR:]
                        if t < LATENT_TILES:
                            k4 = kr.rearrange("p (a x f) -> p a x f", a=1, x=4)
                            cos, sin = (split(rope_tab[:, t, i, :], (1, 2, 8)) for i in range(2))
                            rotate(k4[:, :, 0::2, :], k4[:, :, 1::2, :], cos, sin, (1, 2, 8), None)
                        key = (l, "KV", t, 1)
                        b = split(bank_of(*key)[:, :], (4, P))
                        wait_filled(dve, *key)
                        dve.tensor_copy(split(k_rows[:, t % 2, 4 * QK:], (4, QK))[:, :, 0:NOPE], b[:, :, 0:NOPE])
                        dve.tensor_copy(split(v_rows[:, t, 256:], (4, V_DIM)), b[:, :, NOPE:]).then_inc(drained["dve"], 1)
                        dve.tensor_copy(split(k_rows[:, t % 2, :], (HEADS, QK))[:, :, NOPE:],
                                        kr.unsqueeze(1).broadcast_to([P, HEADS, ROPE])).then_inc(S["k_ready"], 1)
                    if t >= 1:
                        for g in range(2):
                            drain((l, "KT", t - 1, g), k_T[0:QK, 4 * g:4 * g + 4, (t - 1) * P:t * P],
                                  split(bank_of(l, "KT", t - 1, g)[0:QK, :], (4, P)))
                m = len(units(l))
                for i in range(m + 3):
                    if i < m:
                        lo, hi = keys_of(units(l)[i][0])
                        wait_filled(dve, l, "S", i)
                        dve.tensor_reduce(soft[:, 0, i:i + 1], bank_of(l, "S", i)[:, 0:hi - lo], AX.X, ALU.max, negate=True).then_inc(S["row_max"], 1)
                    if 1 <= i < m + 1:
                        lo, hi = keys_of(units(l)[i - 1][0])
                        wait_drained(dve, l, "S", i - 1)
                        linked(dve.reciprocal(soft[:, 2, i - 1:i], soft[:, 1, i - 1:i]))
                        pr = p_rows[:, (i - 1) % 2, 0:hi - lo]
                        dve.tensor_scalar(pr, pr, soft[:, 2, i - 1:i], None, ALU.mult).then_inc(S["p_ready"], 1)
                    if i >= 3:
                        qt, h = units(l)[i - 3]
                        rows = slice(64 * (h % 2), 64 * (h % 2) + 64)
                        drain((l, "O", i - 3), mixed[rows, 4 + h // 2, qt * P:(qt + 1) * P], bank_of(l, "O", i - 3)[rows, 0:P])
                for t in range(nt):
                    for c in range(2):
                        gated((l, "OUT", t, c), t, c, res_tmp[:, c, :], S["x_mixed"] if c else None)
                dve.wait_ge(S["norm2_sums"], nt)
                dve.tensor_scalar(stats[:, 1, 0:nt], stats[:, 0, 0:nt], 1.0 / D, EPS, ALU.mult, ALU.add).then_inc(S["norm2_var"], 1)
                rstd(0, nt, S["norm2_root"], 1)
                dve.wait_ge(S["mods_in"], 64)
                for t in range(nt):
                    normed(t, nt, S["h2_ready"])
                for t in range(nt):
                    drain((l, "T2", t, 1), h_T[:, 4:8, t * P:(t + 1) * P], split(bank_of(l, "T2", t, 1)[:, :], (4, P)))

                N = nt
                dve.wait_ge(S["router_in"], 32)
                for t in range(N):
                    wait_drained(dve, l, "R", t)
                    ins = dve.tensor_tensor(sel[:, t, :], prob[:, t, :], r_bias[:, :], ALU.add)
                linked(ins)
                for t in range(N):
                    for g in range(EGROUPS):
                        ins = dve.max(out=top2[:, t, g, :], in_=sel[:, t, 8 * g:8 * g + 8])
                linked(ins)
                linked(dve.tensor_tensor(gscore[:, 0:N, :], top2[:, 0:N, :, 0], top2[:, 0:N, :, 1], ALU.add))
                other = gscore[:, 0:N, :].unsqueeze(2).broadcast_to([P, N, 8, 8])
                own = gscore[:, 0:N, :].unsqueeze(3).broadcast_to([P, N, 8, 8])
                tie_b = split(tie[:, :], (8, 8)).unsqueeze(1).broadcast_to([P, N, 8, 8])
                dve.tensor_tensor(cmp_a[:, 0:N], other, own, ALU.is_gt)
                linked(dve.tensor_tensor(cmp_b[:, 0:N], other, own, ALU.is_equal))
                linked(dve.tensor_tensor(cmp_b[:, 0:N], cmp_b[:, 0:N], tie_b, ALU.mult))
                linked(dve.tensor_tensor(cmp_a[:, 0:N], cmp_a[:, 0:N], cmp_b[:, 0:N], ALU.add))
                linked(dve.tensor_reduce(gmask[:, 0:N, :], cmp_a[:, 0:N], AX.X, ALU.add))
                linked(dve.tensor_scalar(gmask[:, 0:N, :], gmask[:, 0:N, :], TOP_GROUPS - 0.5, None, ALU.is_lt))
                linked(dve.tensor_scalar(gneg[:, 0:N, :], gmask[:, 0:N, :], 1.0, 1e30, ALU.subtract, ALU.mult))
                sel4 = sel[:, 0:N, :].rearrange("p t (g e) -> p t g e", g=8)
                linked(dve.tensor_tensor(sel4, sel4, gmask[:, 0:N, :].unsqueeze(3).broadcast_to([P, N, 8, 8]), ALU.mult))
                linked(dve.tensor_tensor(sel4, sel4, gneg[:, 0:N, :].unsqueeze(3).broadcast_to([P, N, 8, 8]), ALU.add))
                for t in range(N):
                    ins = dve.max(out=top8[:, t, :], in_=sel[:, t, :])
                linked(ins)
                for t in range(N):
                    ins = dve.match_replace(out=chosen[:, t, :], in_to_replace=top8[:, t, :], in_values=sel[:, t, :], imm_value=-2e30)
                linked(ins)
                dve.tensor_scalar(chosen[:, 0:N, :], chosen[:, 0:N, :], -1.5e30, None, ALU.is_lt).then_inc(S["chosen_ready"], 1)
                dve.wait_ge(S["chosen_ready"], 1)
                linked(dve.tensor_tensor(prob[:, 0:N, :], prob[:, 0:N, :], chosen[:, 0:N, :], ALU.mult))
                linked(dve.tensor_reduce(wsum[:, 0:N], prob[:, 0:N, :], AX.X, ALU.add))
                linked(dve.reciprocal(winv[:, 0:N], wsum[:, 0:N]))
                dve.memset(vals[:, 0:N, :, :], 0.0)
                linked(dve.memset(posm[:, 0:N, :], -1.0))
                for t in range(N):
                    dve.tensor_scalar(vals[:, t, 0:EXPERTS, 2], prob[:, t, :], winv[:, t:t + 1], ROUTED_SCALE, ALU.mult, ALU.mult)
                    dve.tensor_scalar(vals[:, t, 0:EXPERTS, 0], slots_iota[:, 0:EXPERTS], 0.0, token_cols[:, t:t + 1], ALU.mult, ALU.add)

                for t in range(nt + 1):
                    if t < nt:
                        key = (l, "SG", t)
                        b = bank_of(*key)
                        wait_filled(dve, *key)
                        dve.wait_ge(S["shared_sig"], t + 1)
                        if t >= 2:
                            wait_filled(dve, l, "SH", t - 2)
                        linked(dve.tensor_tensor(hid[:, t % 2, :], sig[:, t % 2, :], b[:, 0:FE], ALU.mult))
                        dve.tensor_tensor(hid[:, t % 2, :], hid[:, t % 2, :], b[:, FE:], ALU.mult).then_inc(drained["dve"], 1)
                    if t >= 1:
                        for c in range(2):
                            gated((l, "SD", t - 1, c), t - 1, c, moe_tmp[:, c, :], None)
                drain((l, "MT"), ranks_T[0:64, 0:N, :], split(bank_of(l, "MT")[0:64, 0:N * P], (N, P)))
                key = (l, "RANK")
                wait_filled(dve, *key)
                b = split(bank_of(*key)[:, 0:N * EXPERTS], (N, EXPERTS))
                for t in range(N):
                    ins = dve.tensor_scalar(vals[:, t, 0:EXPERTS, 1], b[:, t, :], token_cols[:, 4 + t:5 + t], None, ALU.add)
                ins.then_inc(drained["dve"], 1)
                key = (l, "POS")
                wait_filled(dve, *key)
                b = split(bank_of(*key)[:, 0:(TILES + 1) * EXPERTS], (TILES + 1, EXPERTS))
                linked(dve.scalar_tensor_tensor(out=posm[:, 0:N, 0:EXPERTS], in0=b[:, 0:N, :], scalar=1.0, in1=chosen[:, 0:N, :],
                                                op0=ALU.add, op1=ALU.mult))
                linked(dve.tensor_scalar(posm[:, 0:N, 0:EXPERTS], posm[:, 0:N, 0:EXPERTS], -1.0, None, ALU.add))
                cnt = bank_of(*key)[0:64, TILES * EXPERTS:TILES * EXPERTS + 1]
                linked(dve.tensor_scalar(ext[0:64, 0:1], cnt, float(P) + 0.5, None, ALU.is_gt))
                for b_ in range(2, N):
                    linked(dve.tensor_scalar(ext[0:64, 1:2], cnt, float(P * b_) + 0.5, None, ALU.is_gt))
                    linked(dve.tensor_tensor(ext[0:64, 0:1], ext[0:64, 0:1], ext[0:64, 1:2], ALU.add))
                dve.tensor_scalar(ext_b, ones[0:64, :], ext[0:64, 0:1], None, ALU.mult).then_inc(drained["dve"], 1)

                def make_g(i, e, s, offset):
                    for t in range(N):
                        ins = dve.tensor_scalar(one_hot[:, s % 2, t, :], slots_iota[:, bass.ds(offset, P)], posm[:, t, bass.ds(e, 1)], None, ALU.is_equal)
                    return ins

                def take_list(s):
                    dve.tensor_copy(row_w[:, s % UNROLL:s % UNROLL + 1], banks[5][:, 2:3])
                    return dve.tensor_scalar(row_idx[:, s % UNROLL, :], banks[5][:, 0:2], float(SKIP), None, ALU.add)

                key = (l, "ENDS")
                wait_filled(dve, *key)
                b = bank_of(*key)
                dve.tensor_scalar(ends[:, 0:64], b[:, 0:64], lane[:, 0:1], None, ALU.is_le)
                linked(dve.tensor_copy(table[:, 0:1], b[:, 63:64]))
                dve.tensor_reduce(table[:, 1:2], ends[:, 0:64], AX.X, ALU.add)
                dve.tensor_tensor(ends[:, 64:128], ends[:, 0:64], b[:, 64:128], ALU.mult).then_inc(drained["dve"], 1)
                wait_drained(dve, *key)
                linked(dve.tensor_reduce(table[:, 2:3], ends[:, 64:128], AX.X, ALU.add))
                linked(dve.tensor_scalar(table[:, 1:2], table[:, 1:2], float(EXPERTS - 1), None, ALU.min))
                linked(dve.tensor_scalar(table[:, 2:3], table[:, 2:3], -1.0, lane[:, 0:1], ALU.mult, ALU.add))
                dve.tensor_scalar(table[:, 2:3], table[:, 2:3], 1.0, 0.0, ALU.add, ALU.max).then_inc(S["table_ready"], 1)
                key = (l, "EXTRA")
                wait_filled(dve, *key)
                dve.tensor_copy(extra_row[:, :], bank_of(*key)[0:1, 0:3 * MAX_EXTRA]).then_inc(drained["dve"], 1)
                wait_drained(dve, *key)
                dve.memset(newton[:, 0:1], 0.0).then_inc(S["extra_ready"], 1)

                dve.wait_ge(drained["dve"], jobs.nth[(l, "POS")])
                for i in range(AHEAD):
                    ge(dve, S["list_filled"], i - 1)
                    make_g(i, i, i, 0).then_inc(S["g_ready"], 1)
                    if i >= 1:
                        dve.wait_ge(S["list_filled"], i)
                        take_list(i - 1).then_inc(S["idx_ready"], 1)
                dve.wait_ge(S["list_filled"], AHEAD)
                take_list(AHEAD - 1).then_inc(S["idx_ready"], 1)

                def x_drain(i, s):
                    dve.wait_ge(S["xt_filled"], i + 1)
                    ge(dve, S["gu_filled"], i - 1)
                    dve.tensor_copy(x_gT[:, s % 2, 4:8, :], split(banks[1][:, :], (4, P))).then_inc(S["xt_dve"], 1)

                def y_drain(i, j, s):
                    dve.wait_ge(S["d_filled"], i + 1)
                    ge(dve, S["scattered"][s % 2], (j * (UNROLL // 2) + s // 2) * 16)
                    c = s % UNROLL
                    dve.tensor_scalar(y_g[:, s % 2, 512:], banks[7][:, :], row_w[:, c:c + 1], None, ALU.mult).then_inc(S["y_dve"], 1)

                x_drain(0, 0)

                def step(j, s):
                    i = j * UNROLL + s
                    x_drain(i + 1, s + 1)
                    dve.wait_ge(S["list_filled"], i + AHEAD - 1)
                    make_g(i, i + AHEAD, s, 0).then_inc(S["g_ready"], 1)
                    dve.wait_ge(S["gu_filled"], i + 1)
                    dve.wait_ge(S["sig_ready"], i + 1)
                    ge(dve, S["ht_filled"], i - 1)
                    b = banks[2 + s % 2]
                    dve.tensor_tensor(hid[:, s % 2, :], sig[:, s % 2, :], b[:, 0:FE], ALU.mult).then_inc(S["hid_part"], 1)
                    dve.wait_ge(S["hid_part"], i + 1)
                    dve.tensor_tensor(hid[:, s % 2, :], hid[:, s % 2, :], b[:, FE:], ALU.mult).then_inc(S["hid_ready"], 1)
                    if not (isinstance(i, int) and i == 0):
                        y_drain(i - 1, j, s - 1)
                    dve.wait_ge(S["list_filled"], i + AHEAD + 1)
                    ge(dve, S["y_act"], i - AHEAD + 1)
                    ge(dve, S["scattered"][s % 2], ((UNROLL // 2) * j + (s - AHEAD) // 2 + 1) * 16)
                    take_list(s + AHEAD).then_inc(S["idx_ready"], 1)
                    dve.wait_ge(S["ht_filled"], i + 1)
                    ge(dve, S["d_filled"], i - 1)
                    dve.tensor_copy(hid_T[:, s % 2], split(banks[4][:, 0:2 * P], (2, P))).then_inc(S["ht_drained"], 1)

                for s in range(UNROLL):
                    step(0, s)
                with dve.Fori(1, EXPERTS // UNROLL) as j:
                    for s in range(UNROLL):
                        step(j, s)
                y_drain(EXPERTS - 1, EXPERTS // UNROLL - 1, UNROLL - 1)

                n_extra = dve.value_load(extra_row[0:1, 0:1], min_val=0, max_val=MAX_EXTRA)
                for s in range(2):
                    dve.wait_ge(S["scattered"][s], 16 * (EXPERTS // 2))
                dve.wait_ge(S["y_act"], EXPERTS)
                with dve.If(n_extra > 0):
                    with dve.Fori(0, n_extra) as o:
                        e = dve.value_load(extra_row[0:1, bass.ds(o + MAX_EXTRA, 1)], min_val=0, max_val=EXPERTS - 1)
                        k = dve.value_load(extra_row[0:1, bass.ds(o + 2 * MAX_EXTRA, 1)], min_val=0, max_val=TILES - 1)
                        make_g(0, e, 0, k * P).then_inc(S["g_ready"], 1)
                        dve.wait_ge(S["list_filled"], o + 1 + LISTED)
                        take_list(0).then_inc(S["idx_ready"], 1)
                        dve.wait_ge(S["xt_filled"], o + 1 + EXPERTS + 1)
                        dve.tensor_copy(x_gT[:, 0, 4:8, :], split(banks[1][:, :], (4, P))).then_inc(S["xt_dve"], 1)
                        dve.wait_ge(S["gu_filled"], o + 1 + EXPERTS)
                        dve.wait_ge(S["sig_ready"], o + 1 + EXPERTS)
                        dve.tensor_tensor(hid[:, 0, :], sig[:, 0, :], banks[2][:, 0:FE], ALU.mult).then_inc(S["hid_part"], 1)
                        dve.wait_ge(S["hid_part"], o + 1 + EXPERTS)
                        dve.tensor_tensor(hid[:, 0, :], hid[:, 0, :], banks[2][:, FE:], ALU.mult).then_inc(S["hid_ready"], 1)
                        dve.wait_ge(S["ht_filled"], o + 1 + EXPERTS)
                        dve.tensor_copy(hid_T[:, 0], split(banks[4][:, 0:2 * P], (2, P))).then_inc(S["ht_drained"], 1)
                        dve.wait_ge(S["d_filled"], o + 1 + EXPERTS)
                        dve.tensor_scalar(y_g[:, 0, 512:], banks[7][:, :], row_w[:, 0:1], None, ALU.mult).then_inc(S["y_dve"], 1)
                        dve.wait_ge(S["e_x"], (o + 1) * 32)

                dve.memset(newton[:, 0:1], 0.0).then_inc(S["rows_back"], 1)

                for t in range(nt):
                    y = y_all[:, t % 3, :]
                    dve.wait_ge(S["y_in"][t % 3], 16 * (t // 3 + 1))
                    for n in (4 * D, 2 * D, D):
                        linked(dve.tensor_tensor(y[:, 0:n], y[:, 0:n], y[:, n:2 * n], ALU.add))
                    linked(dve.tensor_tensor(y[:, 0:D], y[:, 0:D], mods[:, t // 2, 2, :], ALU.mult))
                    dve.tensor_tensor(x_rows[:, t, :], x_rows[:, t, :], y[:, 0:D], ALU.add).then_inc(S["x_done"], 1)

            fin = L[DEPTH - 1]
            n = LATENT_TILES
            dve.wait_ge(fin["norm_sums"], TILES + n)
            dve.tensor_scalar(stats[:, 1, 0:n], stats[:, 0, 0:n], 1.0 / D, EPS, ALU.mult, ALU.add).then_inc(fin["norm_var"], 1)
            rstd(0, n, fin["norm_root"], 2)
            dve.wait_ge(fin["last_gain_in"], 16)
            for t in range(n):
                dve.scalar_tensor_tensor(out=h_rows[:, t, :], in0=x_rows[:, t, :], scalar=stats[:, 3, t:t + 1], in1=mods[:, 1, 0, :],
                                         op0=ALU.mult, op1=ALU.mult).then_inc(fin["x_done"], 1)

        @block.tensor
        def _(pe):
            def claim(*key):
                prev = jobs.before(*key)
                if prev is not None:
                    wait_drained(pe, *prev)
                return bank_of(*key)

            pe.wait_ge(cond_ready, 1)
            for l in range(DEPTH):
                def mod_round(j):
                    for s in range(MOD_SLOTS):
                        c = l * MOD_CHUNKS + j * MOD_SLOTS + s
                        pe.wait_ge(mod_w_in[s], 16 * (j + 1 + l * (MOD_CHUNKS // MOD_SLOTS)))
                        ge(pe, mod_added, c - MOD_SLOTS + 1)
                        for k in range(DK):
                            mm = pe.matmul(banks[s][0:2, :], cond_silu[:, k, :], mod_w[:, s, k, :], start=(k == 0), stop=(k == DK - 1))
                        mm.then_inc(mod_filled, 1)

                mod_round(0)
                with pe.Fori(1, MOD_CHUNKS // MOD_SLOTS) as j:
                    mod_round(j)
            pe.wait_ge(mod_added, DEPTH * MOD_CHUNKS)
            pe.wait_ge(const_in, 8 * 16)
            pe.wait_ge(ones_ready, 1)

            for l in range(DEPTH):
                S = L[l]
                nt = active_tiles(l)

                def chain(key, cols, lhs, rhs, n):
                    b = claim(*key)
                    for k in range(n):
                        mm = pe.matmul(b[:, 0:cols], lhs(k), rhs(k), start=(k == 0), stop=(k == n - 1))
                    mm.then_inc(psum_filled, 1)

                def flips(key, blocks, rows=P):
                    b = claim(*key)
                    for n, x in enumerate(blocks):
                        mm = pe.transpose(b[0:rows, n * P:(n + 1) * P], x, ident[:, :])
                    mm.then_inc(psum_filled, 1)

                for t in range(TILES):
                    pe.wait_ge(S["h_ready"], t + 1)
                    for c in range(2):
                        flips((l, "T1", t, c), [h_rows[:, t, (4 * c + k) * P:(4 * c + k + 1) * P] for k in range(4)])
                pe.wait_ge(S["w_in_in"], 16)
                for t in range(TILES):
                    wait_drained(pe, l, "T1", t, 0)
                    wait_drained(pe, l, "T1", t, 1)
                    for c, (lo, hi) in enumerate(u_chunks(l, t)):
                        chain((l, "U", t, c), hi - lo, lambda k: h_T[:, k, t * P:(t + 1) * P], lambda k: w_in[:, k, lo:hi], DK)
                pe.wait_ge(S["mixer_in"], 14 * 16)
                for t in range(nt):
                    for c in range(len(u_chunks(l, t))):
                        wait_drained(pe, l, "U", t, c)
                for s in range(nt // 2):
                    for c in range(2):
                        b = claim(l, "POOLED", s, c)
                        for g in range(2):
                            for t in range(2):
                                lo = (2 * c + g) * GROUP
                                mm = pe.matmul(b[64 * g:64 * g + 64, 0:SEQ], u_rows[:, 2 * s + t, lo:lo + GROUP], pool_m[:, t, 2 * c + g, :],
                                               start=(t == 0), stop=(t == 1))
                        mm.then_inc(psum_filled, 1)
                    for c in range(2):
                        lo = COL_FNO + c * P
                        chain((l, "DFT_POS", s, c), 2 * SEQ, lambda t: u_rows[:, 2 * s + t, lo:lo + P], lambda t: dft_l[:, t, :], 2)
                    for c in range(2):
                        wait_drained(pe, l, "POOLED", s, c)
                        chain((l, "POOL_OUT", s, c), SEQ, lambda k: w_poolb[:, c, :], lambda k: pooled[:, c, :], 1)
                    for c in range(2):
                        wait_drained(pe, l, "DFT_POS", s, c)
                        chain((l, "DFT_CH", s, c), SEQ, lambda k: dft_c[:, k, :], lambda k: dft_pos[:, c, k * SEQ:(k + 1) * SEQ], 2)
                    for c in range(2):
                        wait_drained(pe, l, "DFT_CH", s, c)
                        chain((l, "FNO_OUT", s, c), SEQ, lambda k: w_fnob[:, c, :], lambda k: dft_ch[:, c, :], 1)
                for t in range(TILES):
                    pe.wait_ge(S["lora_ready"], t + 1)
                    if t < nt:
                        flips((l, "CQ", t), [u_rows[:, t, COL_Q + P * k:COL_Q + P * (k + 1)] for k in range(3)])
                    flips((l, "CKV", t), [u_rows[:, t, COL_KV + P * k:COL_KV + P * (k + 1)] for k in range(2)])
                for t in range(TILES + 1):
                    if t < TILES:
                        if t < nt:
                            wait_drained(pe, l, "CQ", t)
                            for c, (lo, hi) in enumerate(((0, 512), (512, 768))):
                                chain((l, "Q", t, c), hi - lo, lambda k: c_T[:, k, t * P:(t + 1) * P], lambda k: w_uq[:, k, lo:hi], 3)
                        wait_drained(pe, l, "CKV", t)
                        for c in range(2):
                            chain((l, "KV", t, c), 512, lambda k: c_T[:, 3 + k, t * P:(t + 1) * P], lambda k: w_ukv[:, k, 512 * c:512 * c + 512], 2)
                    if t >= 1:
                        u = t - 1
                        if u < nt:
                            wait_drained(pe, l, "Q", u, 0)
                            wait_drained(pe, l, "Q", u, 1)
                            if u < LATENT_TILES:
                                pe.wait_ge(S["q_rotated"], u + 1)
                        pe.wait_ge(S["k_ready"], u + 1)
                        wait_drained(pe, l, "KV", u, 0)
                        for g in range(2):
                            if u < nt:
                                flips((l, "QT", u, g), [q_rows[:, u % 2, h * QK:(h + 1) * QK] for h in range(4 * g, 4 * g + 4)], QK)
                            flips((l, "KT", u, g), [k_rows[:, u % 2, h * QK:(h + 1) * QK] for h in range(4 * g, 4 * g + 4)], QK)
                for g in range(2):
                    wait_drained(pe, l, "QT", nt - 1, g)
                    wait_drained(pe, l, "KT", TILES - 1, g)
                m = len(units(l))
                for i in range(m + 3):
                    if i < m:
                        qt, h = units(l)[i]
                        lo, hi = keys_of(qt)
                        chain((l, "S", i), hi - lo, lambda k: q_T[0:QK, h, qt * P:(qt + 1) * P], lambda k: k_T[0:QK, h, lo:hi], 1)
                    if 2 <= i < m + 2:
                        lo, hi = keys_of(units(l)[i - 2][0])
                        pe.wait_ge(S["p_ready"], i - 1)
                        flips((l, "PT", i - 2), [p_rows[:, i % 2, k * P:(k + 1) * P] for k in range((hi - lo) // P)])
                    if i >= 3:
                        qt, h = units(l)[i - 3]
                        lo, hi = keys_of(qt)
                        wait_drained(pe, l, "PT", i - 3)
                        b = claim(l, "O", i - 3)
                        n = (hi - lo) // P
                        for k in range(n):
                            mm = pe.matmul(b[64 * (h % 2):64 * (h % 2) + 64, 0:P], v_rows[:, lo // P + k, h * V_DIM:(h + 1) * V_DIM],
                                           p_T[:, (i - 3) % 2, k * P:(k + 1) * P], start=(k == 0), stop=(k == n - 1))
                        mm.then_inc(psum_filled, 1)
                pe.wait_ge(S["w_out_in"], 16)
                wait_drained(pe, l, "O", m - 1)
                for t in range(nt):
                    for c in range(2):
                        chain((l, "OUT", t, c), 512, lambda k: mixed[:, k, t * P:(t + 1) * P], lambda k: w_out[:, k, 512 * c:512 * c + 512], DK)
                for t in range(nt):
                    pe.wait_ge(S["h2_ready"], t + 1)
                    for c in range(2):
                        flips((l, "T2", t, c), [h_rows[:, t, 4 * c + k:D:DK] for k in range(4)])
                pe.wait_ge(S["router_in"], 32)
                for t in range(nt):
                    wait_drained(pe, l, "T2", t, 0)
                    wait_drained(pe, l, "T2", t, 1)
                    chain((l, "R", t), EXPERTS, lambda k: h_T[:, k, t * P:(t + 1) * P], lambda k: w_router[:, k, :], DK)
                pe.wait_ge(S["shared_in"], 48)
                gu, dn = slot_gu(SHARED_SLOT), slot_dn(SHARED_SLOT)
                for t in range(nt + 1):
                    if t < nt:
                        b = claim(l, "SG", t)
                        for k in range(DK):
                            mm = pe.matmul(split(b[:, :], (2, FE)), h_T[:, k, t * P:(t + 1) * P], gu[:, :, k, :], start=(k == 0), stop=(k == DK - 1))
                        mm.then_inc(psum_filled, 1)
                    if t >= 1:
                        u = t - 1
                        wait_drained(pe, l, "SG", u)
                        flips((l, "SH", u), [hid[:, u % 2, j:FE:2] for j in range(2)])
                        wait_drained(pe, l, "SH", u)
                        for c in range(2):
                            chain((l, "SD", u, c), 512, lambda k: hid_T[:, u % 2, k, :], lambda k: dn[:, k, 512 * c:512 * c + 512], 2)
                pe.wait_ge(S["chosen_ready"], 1)
                b = claim(l, "MT")
                for t in range(nt):
                    mm = pe.transpose(b[0:64, t * P:(t + 1) * P], chosen[:, t, :], ident[:, :])
                mm.then_inc(psum_filled, 1)
                wait_drained(pe, l, "MT")
                b = claim(l, "RANK")
                for t in range(nt):
                    mm = pe.matmul(b[:, t * EXPERTS:(t + 1) * EXPERTS], ranks_T[0:64, t, :], strict[0:64, 0:64], start=True, stop=True)
                mm.then_inc(psum_filled, 1)
                b = claim(l, "POS")
                for t in range(nt):
                    for q in range(t + 1):
                        pe.matmul(b[:, t * EXPERTS:(t + 1) * EXPERTS], strict[:, :] if q == t else ones[:, :], chosen[:, q, :],
                                  start=(q == 0), stop=(q == t))
                for q in range(nt):
                    mm = pe.matmul(b[0:64, TILES * EXPERTS:TILES * EXPERTS + 1], chosen[:, q, :], ones[:, 0:1], start=(q == 0), stop=(q == nt - 1))
                mm.then_inc(psum_filled, 1)
                wait_drained(pe, l, "POS")
                b = claim(l, "ENDS")
                pe.matmul(b[:, 0:P], ext_b, ends_rhs[:, :], start=True, stop=True).then_inc(psum_filled, 1)

                def make_list(i, e, s):
                    pe.wait_ge(S["g_ready"], i + 1)
                    ge(pe, S["idx_ready"], i)
                    for t in range(nt):
                        mm = pe.matmul(banks[5][:, 0:3], one_hot[:, s % 2, t, :], vals[:, t, bass.ds(e, 1), :].rearrange("p a n -> p (a n)"),
                                       start=(t == 0), stop=(t == nt - 1))
                    mm.then_inc(S["list_filled"], 1)

                pe.wait_ge(S["table_ready"], 1)
                b = claim(l, "EXTRA")
                for c in range(3):
                    mm = pe.matmul(b[0:1, c * MAX_EXTRA:(c + 1) * MAX_EXTRA], table[0:MAX_EXTRA, c:c + 1], ident[0:MAX_EXTRA, 0:MAX_EXTRA], start=True, stop=True)
                mm.then_inc(psum_filled, 1)
                wait_drained(pe, l, "EXTRA")
                for i in range(AHEAD):
                    make_list(i, i, i)

                def flip_rows(i, j, s):
                    pe.wait_ge(S["gathered"][s % 4], ((UNROLL // 4) * j + s // 4 + 1) * 16)
                    ge(pe, S["xt_act"], i)
                    ge(pe, S["xt_dve"], i)
                    for k in range(DK):
                        mm = pe.transpose(banks[k // 4][:, (k % 4) * P:(k % 4 + 1) * P], x_g[:, s % 4, k:D:DK], ident[:, :])
                    mm.then_inc(S["xt_filled"], 1)

                def up(gu, x, bank):
                    for k in range(DK):
                        mm = pe.matmul(split(bank[:, :], (2, FE)), x_gT[:, x, k, :], gu[:, :, k, :], start=(k == 0), stop=(k == DK - 1))
                    return mm

                def down(dn, x):
                    for c in range(2):
                        for k in range(2):
                            mm = pe.matmul(banks[6 + c][:, :], hid_T[:, x, k, :], dn[:, k, 512 * c:512 * c + 512], start=(k == 0), stop=(k == 1))
                    return mm

                def flip_hid(x):
                    for k in range(2):
                        mm = pe.transpose(banks[4][:, k * P:(k + 1) * P], hid[:, x, k:FE:2], ident[:, :])
                    return mm

                def down_step(i, j, s):
                    w = expert_slot(s)
                    pe.wait_ge(S["dn_in"][w], ((UNROLL // 4) * j + s // 4 + 1) * 16)
                    pe.wait_ge(S["ht_drained"], i + 1)
                    ge(pe, S["y_act"], i)
                    ge(pe, S["y_dve"], i)
                    down(slot_dn(w), s % 2).then_inc(S["d_filled"], 1)

                flip_rows(0, 0, 0)

                def step(j, s):
                    i = j * UNROLL + s
                    flip_rows(i + 1, j, s + 1)
                    w = expert_slot(s)
                    pe.wait_ge(S["gu_in"][w], ((UNROLL // 4) * j + s // 4 + 1) * 32)
                    ge(pe, S["hid_ready"], i - 1)
                    up(slot_gu(w), s % 2, banks[2 + s % 2]).then_inc(S["gu_filled"], 1)
                    make_list(i + AHEAD, i + AHEAD, s)
                    if not (isinstance(i, int) and i == 0):
                        down_step(i - 1, j, s - 1)
                    pe.wait_ge(S["hid_ready"], i + 1)
                    ge(pe, S["ht_drained"], i)
                    flip_hid(s % 2).then_inc(S["ht_filled"], 1)

                for s in range(UNROLL):
                    step(0, s)
                with pe.Fori(1, EXPERTS // UNROLL) as j:
                    for s in range(UNROLL):
                        step(j, s)
                down_step(EXPERTS - 1, EXPERTS // UNROLL - 1, UNROLL - 1)

                n_extra = pe.value_load(extra_row[0:1, 0:1], min_val=0, max_val=MAX_EXTRA)
                pe.wait_ge(S["xt_act"], EXPERTS + 1)
                pe.wait_ge(S["xt_dve"], EXPERTS + 1)
                pe.wait_ge(S["y_act"], EXPERTS)
                pe.wait_ge(S["y_dve"], EXPERTS)
                pe.wait_ge(S["idx_ready"], LISTED)
                with pe.If(n_extra > 0):
                    with pe.Fori(0, n_extra) as o:
                        pe.wait_ge(S["g_ready"], o + 1 + LISTED)
                        e = pe.value_load(extra_row[0:1, bass.ds(o + MAX_EXTRA, 1)], min_val=0, max_val=EXPERTS - 1)
                        for t in range(nt):
                            mm = pe.matmul(banks[5][:, 0:3], one_hot[:, 0, t, :], vals[:, t, bass.ds(e, 1), :].rearrange("p a n -> p (a n)"),
                                           start=(t == 0), stop=(t == nt - 1))
                        mm.then_inc(S["list_filled"], 1)
                        pe.wait_ge(S["e_x"], o * 32 + 16)
                        for k in range(DK):
                            mm = pe.transpose(banks[k // 4][:, (k % 4) * P:(k % 4 + 1) * P], x_g[:, 0, k:D:DK], ident[:, :])
                        mm.then_inc(S["xt_filled"], 1)
                        pe.wait_ge(S["e_w"], (o + 1) * 48)
                        pe.wait_ge(S["xt_act"], o + 1 + EXPERTS + 1)
                        pe.wait_ge(S["xt_dve"], o + 1 + EXPERTS + 1)
                        up(slot_gu(0), 0, banks[2]).then_inc(S["gu_filled"], 1)
                        pe.wait_ge(S["hid_ready"], o + 1 + EXPERTS)
                        flip_hid(0).then_inc(S["ht_filled"], 1)
                        pe.wait_ge(S["ht_drained"], o + 1 + EXPERTS)
                        pe.wait_ge(S["y_act"], o + EXPERTS)
                        pe.wait_ge(S["y_dve"], o + EXPERTS)
                        down(slot_dn(0), 0).then_inc(S["d_filled"], 1)
                pe.wait_ge(S["y_act"], n_extra + EXPERTS)
                pe.wait_ge(S["y_dve"], n_extra + EXPERTS)


def shape_constants():
    f = np.float32
    pos = np.arange(SEQ)
    pool = np.zeros((4, SEQ, SEQ), np.float64)
    for g, w in enumerate(POOL_WINDOWS):
        for t in range(SEQ):
            lo, hi = max(t - w // 2, 0), min(t + w // 2, SEQ)
            pool[g, t, lo:hi] = 1.0 / (hi - lo)
            pool[g, t, t] -= 1.0
    ang_l = 2 * np.pi * ((pos[:, None] * pos[None, :]) % SEQ) / SEQ
    ch = np.arange(GROUP)
    ang_c = 2 * np.pi * ((ch[:, None] * ch[None, :]) % GROUP) / GROUP
    norm = 1.0 / np.sqrt(SEQ * GROUP)
    dft_l = np.concatenate([np.cos(ang_l), np.sin(ang_l)], axis=1)
    dft_c = np.zeros((P, 2, P))
    for g in range(2):
        dft_c[g * 64:g * 64 + 64, 0, g * 64:g * 64 + 64] = np.cos(ang_c) * norm
        dft_c[g * 64:g * 64 + 64, 1, g * 64:g * 64 + 64] = -np.sin(ang_c) * norm
    inv = f(ROPE_THETA) ** (-np.arange(ROPE_FREQS, dtype=f) * f(2.0) / f(2 * ROPE_FREQS))
    ang = np.stack([(pos // GRID_W).astype(f)[:, None] * inv, (pos % GRID_W).astype(f)[:, None] * inv], axis=1).reshape(SEQ, 16)
    rope = np.stack([np.cos(ang), np.sin(ang)], axis=1).reshape(2, P, 2, 16).transpose(1, 0, 2, 3)
    strict = np.triu(np.ones((P, P)), 1)
    lane = np.arange(P)
    tok = lane[:, None] + P * np.arange(TILES)[None, :]
    grp = np.arange(8)
    out = {
        "k_ident": np.eye(P),
        "k_strict": strict,
        "k_iota": np.tile(np.arange(TOKENS), (P, 1)),
        "k_ends": np.concatenate([np.triu(np.ones((64, 64))), np.eye(64)], axis=1),
        "k_token": np.concatenate([tok - SKIP, TOP_K * tok - SKIP], axis=1),
        "k_lane": lane[:, None],
        "k_tie": np.tile((grp[None, :] < grp[:, None]).reshape(1, 64), (P, 1)),
        "k_rope": rope,
        "k_pool": pool.transpose(2, 0, 1).reshape(2, P, 4, SEQ).transpose(1, 0, 2, 3),
        "k_dft_l": dft_l.reshape(2, P, 2 * SEQ).transpose(1, 0, 2),
        "k_dft_c": dft_c,
        "k_zero": np.zeros((P, 2, P)),
    }
    return {k: np.ascontiguousarray(v.astype(f)) for k, v in out.items()}


def kernel(**inputs):
    import concourse.bacc as bacc
    from concourse.bass_utils import run_bass_kernel_spmd

    nc = bacc.Bacc("TRN2", target_bir_lowering=False, num_devices=1)
    arrays = {k: np.ascontiguousarray(v) for k, v in inputs.items()}
    arrays.update(shape_constants())
    aps = {k: nc.dram_tensor(f"in_{k}", v.shape, mybir.dt.from_np(v.dtype), kind="ExternalInput").ap() for k, v in arrays.items()}
    out = nc.dram_tensor("out", (1, SEQ, D), F32, kind="ExternalOutput").ap()
    build(nc, aps, out)
    r = run_bass_kernel_spmd(nc, [{f"in_{k}": v for k, v in arrays.items()}], core_ids=[0])
    return r.results[0]["out"]
```

```python
from contextlib import ExitStack

import numpy as np

import concourse.bass as bass
from concourse import mybir

F32 = mybir.dt.float32
F32R = mybir.dt.float32r
I32 = mybir.dt.int32
U32 = mybir.dt.uint32
ALU = mybir.AluOpType
ACT = mybir.ActivationFunctionType
AX = mybir.AxisListType

P = 128
BANKS = 8
BANK = 512

D = 1024
DK = D // P
SEQ = 256
CTX = 256
DEPTH = 2
EPS = 1e-6
TILES = (SEQ + CTX) // P
LATENT_TILES = SEQ // P
STREAM_TILES = 2
TOKENS = TILES * P

GROUP = 64
POOL_WINDOWS = (2, 4, 8, 16)
COL_FNO = 256
COL_Q = 512
Q_LORA = 384
KV_LORA = 256
COL_KV = COL_Q + Q_LORA
COL_KR = COL_KV + KV_LORA
IN_WIDTH = COL_KR + 32
HEADS = 8
NOPE = 64
ROPE = 32
QK = NOPE + ROPE
V_DIM = 64
SCALE = QK ** -0.5
GRID_W = 64
ROPE_FREQS = 8
ROPE_THETA = 10000.0

EXPERTS = 64
TOP_K = 8
EGROUPS = 8
TOP_GROUPS = 4
FE = 256
ROUTED_SCALE = 2.5
AHEAD = 4
LISTED = EXPERTS + AHEAD
UNROLL = 8
SKIP = 65536
MAX_EXTRA = 64

MOD_N = 512
MOD_CHUNKS = 6 * D // MOD_N
MOD_SLOTS = 4
PIECES = 4
PIECE_K = DK // PIECES
W_IN_HEAD = 2 * DK * MOD_N // IN_WIDTH

SLOT = 6144
GU_W = 2 * DK * FE
QTR = D // 4
POOL_QTRS = (3,)


def active_tiles(layer):
    return TILES if layer < DEPTH - 1 else LATENT_TILES


def u_chunks(layer, t):
    if t < active_tiles(layer):
        return [(0, 512), (512, 1024), (1024, IN_WIDTH)]
    return [(COL_KV, IN_WIDTH)]


def units(layer):
    return [(qt, h) for qt in range(active_tiles(layer)) for h in range(HEADS)]


def keys_of(qt):
    return (0, TOKENS) if qt < LATENT_TILES else (SEQ, TOKENS)


def plan_jobs():
    jobs = []

    def add(eng, *key):
        jobs.append((key, eng))

    for l in range(DEPTH):
        nt = active_tiles(l)
        for t in range(TILES):
            add("act", l, "T1", t, 0)
            add("dve", l, "T1", t, 1)
        n = 0
        for t in range(TILES):
            for c in range(len(u_chunks(l, t))):
                add(("act", "dve")[n % 2], l, "U", t, c)
                n += 1
        for s in range(nt // STREAM_TILES):
            for c in range(2):
                add("act", l, "POOLED", s, c)
            for c in range(2):
                add("dve", l, "DFT_POS", s, c)
            for c in range(2):
                add("dve", l, "POOL_OUT", s, c)
            for c in range(2):
                add("act", l, "DFT_CH", s, c)
            for c in range(2):
                add("act", l, "FNO_OUT", s, c)
        for t in range(TILES):
            if t < nt:
                add("act", l, "CQ", t)
            add("dve", l, "CKV", t)
        for t in range(TILES + 1):
            if t < TILES:
                if t < nt:
                    add("act", l, "Q", t, 0)
                    add("dve", l, "Q", t, 1)
                add("act", l, "KV", t, 0)
                add("dve", l, "KV", t, 1)
            if t >= 1:
                for g in range(2):
                    if t - 1 < nt:
                        add("act", l, "QT", t - 1, g)
                    add("dve", l, "KT", t - 1, g)
        m = len(units(l))
        for i in range(m + 3):
            if i < m:
                add("act", l, "S", i)
            if 2 <= i < m + 2:
                add("act", l, "PT", i - 2)
            if 3 <= i:
                add("dve", l, "O", i - 3)
        for t in range(nt):
            for c in range(2):
                add("dve", l, "OUT", t, c)
        for t in range(nt):
            add("act", l, "T2", t, 0)
            add("dve", l, "T2", t, 1)
        for t in range(nt):
            add("act", l, "R", t)
        for t in range(nt + 1):
            if t < nt:
                add("dve", l, "SG", t)
            if t >= 1:
                add("act", l, "SH", t - 1)
                add("dve", l, "SD", t - 1, 0)
                add("dve", l, "SD", t - 1, 1)
        add("dve", l, "MT")
        add("dve", l, "RANK")
        add("dve", l, "POS")
        add("dve", l, "ENDS")
        add("dve", l, "EXTRA")
    return jobs


class Jobs:

    def __init__(self):
        self.number, self.by, self.nth = {}, {}, {}
        count = {"act": 0, "dve": 0}
        self.order = plan_jobs()
        for n, (key, eng) in enumerate(self.order):
            count[eng] += 1
            self.number[key], self.by[key], self.nth[key] = n, eng, count[eng]
        self.total = count

    def bank(self, *key):
        return self.number[key] % BANKS

    def filled(self, *key):
        return self.number[key] + 1

    def before(self, *key):
        n = self.number[key] - BANKS
        return self.order[n][0] if n >= 0 else None


def build(nc, a, out):
    jobs = Jobs()
    with ExitStack() as ctx:
        def sb(name, shape, dt=F32):
            return ctx.enter_context(nc.sbuf_tensor(name, shape, dt))

        def sem(name):
            return ctx.enter_context(nc.semaphore(name))

        banks = [ctx.enter_context(nc.psum_tensor(f"bank{i}", [P, BANK], F32)) for i in range(BANKS)]

        mod_rows_d = nc.dram_tensor("mod_rows_d", [DEPTH, 2, 6 * D], F32, kind="Internal").ap()
        h2_d = [nc.dram_tensor(f"h2_d{l}", [active_tiles(l) * P, D], F32, kind="Internal").ap() for l in range(DEPTH)]
        expert_rows = [nc.dram_tensor(f"expert_rows{l}", [active_tiles(l) * P * TOP_K, D], F32, kind="Internal").ap() for l in range(DEPTH)]

        x_rows = sb("x_rows", [P, TILES, D])
        mods = sb("mods", [P, 2, 3, D])
        ident = sb("ident", [P, P])
        strict = sb("strict", [P, P])
        ones = sb("ones", [P, P])
        slots_iota = sb("slots_iota", [P, TOKENS])
        ends_rhs = sb("ends_rhs", [64, 128])
        token_cols = sb("token_cols", [P, 8])
        lane = sb("lane", [P, 1])
        tie = sb("tie", [P, 64])
        rope_tab = sb("rope_tab", [P, 2, 2, 16])
        g_lora = sb("g_lora", [P, Q_LORA + KV_LORA])
        w_router = sb("w_router", [P, DK, EXPERTS])
        r_bias = sb("r_bias", [P, EXPERTS])
        pool_scale = sb("pool_scale", [P, 2])
        cond = sb("cond", [P, 2, DK])
        cond_silu = sb("cond_silu", [P, DK, 2])
        stats = sb("stats", [P, 4, 8])
        newton = sb("newton", [P, 8])
        soft = sb("soft", [P, 3, 32])
        row_idx = sb("row_idx", [P, UNROLL, 2], U32)
        row_w = sb("row_w", [P, UNROLL])
        extra_row = sb("extra_row", [1, 3 * MAX_EXTRA], I32)

        cond_hi = sb("cond_hi", [P, DK, 2], F32R)
        cond_lo = sb("cond_lo", [P, DK, 2], F32R)

        with ExitStack() as early:
            mod_w = early.enter_context(nc.sbuf_tensor("mod_w", [P, MOD_SLOTS, DK, MOD_N], F32))
            mod_w_hi = early.enter_context(nc.sbuf_tensor("mod_w_hi", [P, PIECES, PIECE_K, MOD_N], F32R))
            mod_w_lo = early.enter_context(nc.sbuf_tensor("mod_w_lo", [P, PIECES, PIECE_K, MOD_N], F32R))
        ring = sb("ring", [P, 4 * SLOT])
        arena = sb("arena", [P, 15488])

        def view(lo, n, *shape):
            v = arena[:, lo:lo + n]
            return split(v, shape)

        def split(v, shape):
            if len(shape) == 1:
                return v
            if len(shape) == 2:
                return v.rearrange("p (a b) -> p a b", b=shape[1])
            return v.rearrange("p (a b c) -> p a b c", b=shape[1], c=shape[2])

        A, B, U, C = 0, 4096, 8192, 12928
        mod_rows = [arena[0:2, U * l:U * l + 6 * D] for l in range(DEPTH)]
        gain_rows = arena[0:2, 6 * D:8 * D]
        first_squares = view(14 * D, D, D)
        h_rows = view(A, 4096, TILES, D)
        mixed = view(A, 4096, DK, TOKENS)
        pooled = view(A + 2048, 512, 2, SEQ)
        dft_pos = view(A + 2560, 1024, 2, 2 * SEQ)
        dft_ch = view(A + 3584, 512, 2, SEQ)
        h_T = view(B, 4096, DK, TOKENS)
        q_rows = view(B, 1536, 2, HEADS * QK)
        k_rows = view(B + 1536, 1536, 2, HEADS * QK)
        square_out = view(B + 3072, 512, 512)
        rope_tmp = view(B + 3584, 512, 4, 128)
        u_rows = view(U, TILES * IN_WIDTH, TILES, IN_WIDTH)
        p_rows = view(U, 1024, 2, 512)
        p_T = view(U + 1024, 1024, 2, 512)
        res_tmp = view(U + 2048, 1024, 2, 512)
        c_T = view(C, 2560, 5, TOKENS)
        x_g = view(A, 4096, 4, D)
        x_gT = view(B, 2048, 2, DK, P)
        y_g = view(B + 2048, 2048, 2, D)
        one_hot = view(U, 1024, 2, TILES, P)
        vals = view(U + 1024, TILES * LISTED * 3, TILES, LISTED, 3)
        posm = view(U + 1840, TILES * LISTED, TILES, LISTED)
        hid = view(U + 2112, 512, 2, FE)
        sig = view(U + 2624, 512, 2, FE)
        hid_T = view(U + 3136, 512, 2, 2, P)
        moe_tmp = view(U + 3648, 1024, 2, 512)
        y_sum = view(U + 2112, QTR, QTR)
        prob = view(C, 256, TILES, EXPERTS)
        sel = view(C + 256, 256, TILES, EXPERTS)
        top2 = view(C + 512, 256, TILES, EGROUPS, 8)
        cmp_a = view(C + 768, 256, TILES, EGROUPS, 8)
        cmp_b = view(C + 1024, 256, TILES, EGROUPS, 8)
        chosen = view(C + 1280, 256, TILES, EXPERTS)
        small = view(C + 1536, 256, 256)
        ranks_T = view(C + 1792, 512, TILES, P)
        gscore = split(small[:, 0:32], (TILES, 8))
        gmask = split(small[:, 32:64], (TILES, 8))
        gneg = split(small[:, 64:96], (TILES, 8))
        top8 = split(small[:, 96:128], (TILES, 8))
        wsum = small[:, 128:132]
        winv = small[:, 132:136]
        ext = small[:, 136:138]
        ext_b = top2.rearrange("p a b c -> p (a b c)")[0:64, 0:128]
        ends = cmp_a.rearrange("p a b c -> p (a b c)")
        table = small[:, 138:141]

        w_in = ring[:, 0:DK * IN_WIDTH].rearrange("p (k n) -> p k n", k=DK)
        w_out = ring[:, 0:8192].rearrange("p (k n) -> p k n", k=DK)
        k_T = ring[:, 8192:12288].rearrange("p (h n) -> p h n", h=HEADS)
        pool_m = ring[:, 9728:11776].rearrange("p (t g n) -> p t g n", t=2, g=4)
        w_uq = ring[:, 12288:12288 + 2304].rearrange("p (k n) -> p k n", k=3)
        w_ukv = ring[:, 14592:14592 + 2048].rearrange("p (k n) -> p k n", k=2)
        dft_l = ring[:, 16640:16640 + 1024].rearrange("p (t n) -> p t n", t=2)
        dft_c = ring[:, 17664:17664 + 256].rearrange("p (t n) -> p t n", t=2)
        w_pool_g = ring[:, 17920:18048].rearrange("p (c n) -> p c n", c=2)
        w_fno_g = ring[:, 18048:18176].rearrange("p (c n) -> p c n", c=2)
        q_T = ring[:, 18432:18432 + 4096].rearrange("p (h n) -> p h n", h=HEADS)
        v_rows = ring[:, 22528:22528 + 2048].rearrange("p (t n) -> p t n", t=TILES)
        y_quarter = [split(v, (TOP_K, QTR)) for v in (
            ring[:, 18432:20480], ring[:, 20480:22528], ring[:, 22528:24576], arena[:, C:C + 2048])]

        def slot_gu(s):
            return ring[:, s * SLOT:s * SLOT + GU_W].rearrange("p (g k f) -> p g k f", g=2, k=DK)

        def slot_dn(s):
            return ring[:, s * SLOT + GU_W:(s + 1) * SLOT].rearrange("p (j n) -> p j n", j=2)

        def expert_slot(i):
            return (i + 3) % 4

        SHARED_SLOT = 2
        EXTRA_SLOT = 3

        psum_filled = sem("psum_filled")
        drained = {"act": sem("drained_by_act"), "dve": sem("drained_by_dve")}
        dve_link = sem("dve_link")
        act_link = sem("act_link")
        pool_link = sem("pool_link")
        const_in = sem("const_in")
        cond_in = sem("cond_in")
        cond_sig = sem("cond_sig")
        cond_ready = sem("cond_ready")
        x_in = sem("x_in")
        ones_ready = sem("ones_ready")
        mod_w_in = [sem(f"mod_w_in{s}") for s in range(MOD_SLOTS)]
        mod_bias_in = sem("mod_bias_in")
        mod_hi = sem("mod_hi")
        mod_lo = sem("mod_lo")
        mod_filled = sem("mod_filled")
        mod_added = sem("mod_added")
        mod_ready = sem("mod_ready")
        mod_stored = sem("mod_stored")
        out_stored = sem("out_stored")
        row_moves = sem("row_moves")

        def layer_sems(l):
            named = {name: sem(f"{name}_{l}") for name in (
                "mods_in", "w_in_in", "w_lora_in", "mixer_in", "w_out_in", "router_in", "norm_sums",
                "norm_var", "norm_root", "h_ready", "lora_ready",
                "q_rotated", "k_ready", "row_max", "p_ready", "x_mixed", 
                "h2_ready", "h2_stored", "shared_in", "shared_sig", "chosen_ready",
                "table_ready", "extra_ready", "g_ready", "list_filled", "idx_ready", "xt_filled", "xt_act",
                "xt_dve", "gu_filled", "sig_ready", "hid_part", "hid_ready", "ht_filled", "ht_drained",
                "d_filled", "y_act", "y_dve", "e_w", "e_x", "rows_back", "last_gain_in", "x_done", "x_done_pool", "gate_in", "out_ready",
            )}
            many = {name: [sem(f"{name}{s}_{l}") for s in range(n)]
                    for name, n in (("gu_in", 4), ("dn_in", 4), ("gathered", 4), ("scattered", 2), ("y_in", 4))}
            return {**named, **many}

        L = [layer_sems(l) for l in range(DEPTH)]

        def ge(eng, s, value):
            if not (isinstance(value, int) and value <= 0):
                eng.wait_ge(s, value)

        def wait_drained(eng, *key):
            eng.wait_ge(drained[jobs.by[key]], jobs.nth[key])

        def wait_filled(eng, *key):
            eng.wait_ge(psum_filled, jobs.filled(*key))

        def bank_of(*key):
            return banks[jobs.bank(*key)]

        def load_w_in(eng, l, lo, hi):
            eng.dma_start(w_in[:, lo:hi], a["w_in"][l].rearrange("(k p) n -> p k n", p=P)[:, lo:hi]).then_inc(L[l]["w_in_in"], 16)

        def load_mixer_weights(eng, l):
            S = L[l]
            eng.dma_start(pool_m, a["k_pool"]).then_inc(S["mixer_in"], 16)
            eng.dma_start(dft_l, a["k_dft_l"]).then_inc(S["mixer_in"], 16)
            eng.dma_start(dft_c, a["k_dft_c"]).then_inc(S["mixer_in"], 16)
            eng.dma_start(pool_scale[:, :], a["pool_scale"][l].rearrange("(c p) -> p c", p=P),
                          allow_slow_non_contiguous=True).then_inc(S["mixer_in"], 16)
            eng.dma_start(w_pool_g, a["w_pool"][l].rearrange("(c b) i o -> (b i) c o", b=2)).then_inc(S["mixer_in"], 16)
            eng.dma_start(w_fno_g, a["w_fno"][l].rearrange("(c b) i o -> (b i) c o", b=2)).then_inc(S["mixer_in"], 16)
            eng.dma_start(w_uq, a["w_uq"][l].rearrange("(k p) n -> p k n", p=P)).then_inc(S["w_lora_in"], 16)
            eng.dma_start(w_ukv, a["w_ukv"][l].rearrange("(k p) n -> p k n", p=P)).then_inc(S["w_lora_in"], 16)
            eng.dma_start(g_lora[:, 0:Q_LORA], a["g_q"][l].partition_broadcast(P)).then_inc(S["w_lora_in"], 16)
            eng.dma_start(g_lora[:, Q_LORA:], a["g_kv"][l].partition_broadcast(P)).then_inc(S["w_lora_in"], 16)
            eng.dma_start(w_router[:, :, :], a["w_router"][l].rearrange("(p k) n -> p k n", k=DK)).then_inc(S["router_in"], 16)
            eng.dma_start(r_bias[:, :], a["router_bias"][l].partition_broadcast(P)).then_inc(S["router_in"], 16)

        block = ctx.enter_context(nc.Block())

        @block.sync
        def _(sp):
            sp.dma_start(cond[:, 0, :], a["c"].rearrange("a (p k) -> (a p) k", k=DK)).then_inc(cond_in, 16)
            sp.dma_start(cond[:, 1, :], a["c_ctx"].rearrange("(p k) -> p k", k=DK)).then_inc(cond_in, 16)
            for l in range(DEPTH):
                wm = a["w_mod"][l].rearrange("(p k) n -> p k n", k=DK)
                if l == 0:
                    for s in range(MOD_SLOTS):
                        sp.dma_start(mod_w[:, s], wm[:, :, s * MOD_N:(s + 1) * MOD_N]).then_inc(mod_w_in[s], 16)
                    first = 1
                else:
                    first = 0
                with sp.Fori(first, MOD_CHUNKS // MOD_SLOTS) as j:
                    for s in range(MOD_SLOTS):
                        sp.wait_ge(mod_lo, PIECES * (l * MOD_CHUNKS + j * MOD_SLOTS + s + 1 - MOD_SLOTS))
                        sp.dma_start(mod_w[:, s], wm[:, :, bass.ds((j * MOD_SLOTS + s) * MOD_N, MOD_N)]).then_inc(mod_w_in[s], 16)
            for dst, name in ((ident, "k_ident"), (strict, "k_strict"), (slots_iota, "k_iota"), (ends_rhs, "k_ends"),
                              (token_cols, "k_token"), (lane, "k_lane"), (tie, "k_tie")):
                sp.dma_start(dst[:, :], a[name]).then_inc(const_in, 16)
            sp.dma_start(rope_tab[:, :, :, :], a["k_rope"]).then_inc(const_in, 16)
            sp.dma_start(x_rows[:, 0:2, :], a["x"].rearrange("a (t p) n -> p (a t) n", p=P)).then_inc(x_in, 16)
            sp.dma_start(x_rows[:, 2:4, :], a["ctx"].rearrange("a (t p) n -> p (a t) n", p=P)).then_inc(x_in, 16)

            for l in range(DEPTH):
                S = L[l]
                nt = active_tiles(l)
                if l == 0:
                    sp.wait_ge(mod_lo, PIECES * (DEPTH * MOD_CHUNKS - 2))
                    load_w_in(sp, l, 0, W_IN_HEAD)
                    sp.wait_ge(mod_lo, PIECES * (DEPTH * MOD_CHUNKS - 1))
                    load_w_in(sp, l, W_IN_HEAD, DK)
                    sp.wait_ge(mod_filled, PIECES * DEPTH * MOD_CHUNKS)
                    sp.wait_ge(mod_stored, 16 * DEPTH)
                    load_mixer_weights(sp, l)
                wait_filled(sp, l, "U", TILES - 1, len(u_chunks(l, TILES - 1)) - 1)
                sp.dma_start(w_out, a["w_out"][l].rearrange("(k p) n -> p k n", p=P)).then_inc(S["w_out_in"], 16)
                wait_filled(sp, l, "KV", TILES - 1, 1)
                gu = slot_gu(SHARED_SLOT)
                sp.dma_start(gu[:, 0], a["w_sh_gate"][l].rearrange("(p k) f -> p k f", k=DK)).then_inc(S["shared_in"], 16)
                sp.dma_start(gu[:, 1], a["w_sh_up"][l].rearrange("(p k) f -> p k f", k=DK)).then_inc(S["shared_in"], 16)
                sp.dma_start(slot_dn(SHARED_SLOT), a["w_sh_down"][l].rearrange("(p j) n -> p j n", j=2)).then_inc(S["shared_in"], 16)

                def load_expert(e, s):
                    gu = slot_gu(s)
                    for g, name in enumerate(("w_gate", "w_up")):
                        w = a[name][l].rearrange("e (p k) f -> e p k f", k=DK)
                        sp.dma_start(gu[:, g], w[bass.ds(e, 1)].rearrange("a p k f -> p (a k) f")).then_inc(S["gu_in"][s], 16)
                    w = a["w_down"][l].rearrange("e (p j) n -> e p j n", j=2)
                    sp.dma_start(slot_dn(s), w[bass.ds(e, 1)].rearrange("a p j n -> p (a j) n")).then_inc(S["dn_in"][s], 16)

                wait_filled(sp, l, "O", len(units(l)) - 1)
                load_expert(0, expert_slot(0))
                wait_filled(sp, l, "OUT", nt - 1, 1)
                load_expert(1, expert_slot(1))
                load_expert(2, expert_slot(2))
                wait_filled(sp, l, "SD", nt - 1, 1)
                load_expert(3, expert_slot(3))
                with sp.Fori(1, EXPERTS // 4) as j:
                    for s in range(4):
                        sp.wait_ge(S["d_filled"], j * 4 + s - 3)
                        load_expert(j * 4 + s, expert_slot(s))

                def load_block(o):
                    e = sp.value_load(extra_row[0:1, bass.ds(o + MAX_EXTRA, 1)], min_val=0, max_val=EXPERTS - 1)
                    gu = slot_gu(EXTRA_SLOT)
                    for g, name in enumerate(("w_gate", "w_up")):
                        w = a[name][l].rearrange("e (p k) f -> e p k f", k=DK)
                        sp.dma_start(gu[:, g], w[bass.ds(e, 1)].rearrange("a p k f -> p (a k) f")).then_inc(S["e_w"], 16)
                    w = a["w_down"][l].rearrange("e (p j) n -> e p j n", j=2)
                    sp.dma_start(slot_dn(EXTRA_SLOT), w[bass.ds(e, 1)].rearrange("a p j n -> p (a j) n")).then_inc(S["e_w"], 16)

                sp.wait_ge(S["extra_ready"], 1)
                n_extra = sp.value_load(extra_row[0:1, 0:1], min_val=0, max_val=MAX_EXTRA)
                sp.wait_ge(S["d_filled"], EXPERTS - 3)
                with sp.If(n_extra > 0):
                    load_block(0)
                with sp.If(n_extra > 1):
                    with sp.Fori(1, n_extra) as o:
                        sp.wait_ge(S["d_filled"], o + EXPERTS)
                        load_block(o)
                sp.wait_ge(S["rows_back"], 1)
                rows = expert_rows[l].rearrange("(t p k) n -> t p k n", p=P, k=TOP_K)
                for t in range(nt):
                    for q in range(4):
                        if t and q in POOL_QTRS:
                            sp.wait_ge(S["x_done_pool"], (t - 1) * len(POOL_QTRS) + POOL_QTRS.index(q) + 1)
                        elif t:
                            sp.wait_ge(S["x_done"], (t - 1) * (4 - len(POOL_QTRS)) + q + 1)
                        sp.dma_start(y_quarter[q], rows[t][:, :, q * QTR:(q + 1) * QTR]).then_inc(S["y_in"][q], 16)
            sp.wait_ge(L[DEPTH - 1]["out_ready"], LATENT_TILES)
            sp.dma_start(out.rearrange("a (t p) n -> p (a t) n", p=P), h_rows[:, 0:2, :]).then_inc(out_stored, 16)
            sp.wait_ge(out_stored, 16)

        @block.gpsimd
        def _(pool):
            link = [0]

            def pool_linked(ins):
                link[0] += 1
                ins.then_inc(pool_link, 1)
                pool.wait_ge(pool_link, link[0])

            def load_mods(l, first, n, at, streams, signal):
                for s in range(streams):
                    pool.dma_start(mods[:, s, at:at + n, :].rearrange("p a n -> p (a n)"),
                                   mod_rows_d[l, s, first * D:(first + n) * D].partition_broadcast(P)).then_inc(signal, 16)

            for l in range(DEPTH):
                pool.dma_start(mod_rows[l], a["b_mod"][l].partition_broadcast(2)).then_inc(mod_bias_in, 16)
            for l in range(DEPTH):
                pool.dma_start(gain_rows[:, 0:D], a["g_mix"][l].partition_broadcast(2)).then_inc(mod_bias_in, 16)
                pool.dma_start(gain_rows[:, D:], a["g_ffn"][l].partition_broadcast(2)).then_inc(mod_bias_in, 16)
                pool.wait_ge(mod_ready, l + 1)
                pool.dma_start(mod_rows_d[l], mod_rows[l]).then_inc(mod_stored, 16)
                pool.wait_ge(mod_stored, 16 * (l + 1))
                if l == 0:
                    load_mods(0, 0, 2, 0, 2, L[0]["mods_in"])
                    load_mods(0, 2, 1, 2, 2, L[0]["gate_in"])

            for l in range(DEPTH):
                S = L[l]
                nt = active_tiles(l)
                streams = nt // STREAM_TILES
                if l:
                    load_mods(l, 2, 1, 2, streams, S["gate_in"])
                pool.wait_ge(S["h_ready"], TILES)
                load_mods(l, 3, 2, 0, streams, S["mods_in"])
                if l == DEPTH - 1:
                    pool.dma_start(mods[:, 1, 0, :], a["g_final"].partition_broadcast(P)).then_inc(S["last_gain_in"], 16)
                pool.wait_ge(S["x_mixed"], nt)
                load_mods(l, 5, 1, 2, streams, S["gate_in"])
                for t in range(nt):
                    pool.wait_ge(S["h2_ready"], t + 1)
                    pool.dma_start(h2_d[l][t * P:(t + 1) * P, :], h_rows[:, t, :]).then_inc(S["h2_stored"], 16)
                if l + 1 < DEPTH:
                    load_mods(l + 1, 0, 2, 0, 2, L[l + 1]["mods_in"])

                last_token = pool.to_reg(nt * P - 1)
                last_row = pool.to_reg(nt * P * TOP_K - 1)

                def gather(slot, idx):
                    pool.sem_inc(row_moves, 1)
                    return pool.indirect_dma_start(
                        out=x_g[:, slot, :], out_offset=None, in_=h2_d[l],
                        in_offset=bass.IndirectOffsetOnAxis(ap=row_idx[:, idx, 0:1], axis=0),
                        bounds_check=last_token, oob_is_err=False)

                def scatter(slot, idx):
                    pool.sem_inc(row_moves, 1)
                    return pool.indirect_dma_start(
                        out=expert_rows[l], out_offset=bass.IndirectOffsetOnAxis(ap=row_idx[:, idx, 1:2], axis=0),
                        in_=y_g[:, slot, :], in_offset=None,
                        bounds_check=last_row, oob_is_err=False)

                pool.wait_ge(S["h2_stored"], 16 * nt)
                wait_filled(pool, l, "T2", nt - 1, 1)
                for i in range(AHEAD):
                    pool.wait_ge(S["idx_ready"], i + 1)
                    gather(i % 4, i).then_inc(S["gathered"][i % 4], 16)

                def step(i, s):
                    pool.wait_ge(S["idx_ready"], i + AHEAD + 1)
                    pool.wait_ge(S["xt_filled"], i + 1)
                    gather(s % 4, (s + AHEAD) % UNROLL).then_inc(S["gathered"][s % 4], 16)
                    if not (isinstance(i, int) and i == 0):
                        pool.wait_ge(S["y_act"], i)
                        pool.wait_ge(S["y_dve"], i)
                        scatter((s - 1) % 2, (s - 1) % UNROLL).then_inc(S["scattered"][(s - 1) % 2], 16)

                for s in range(UNROLL):
                    step(s, s)
                with pool.Fori(1, EXPERTS // UNROLL) as j:
                    for s in range(UNROLL):
                        step(j * UNROLL + s, s)
                pool.wait_ge(S["y_act"], EXPERTS)
                pool.wait_ge(S["y_dve"], EXPERTS)
                scatter(1, UNROLL - 1).then_inc(S["scattered"][1], 16)
                for s in range(4):
                    pool.wait_ge(S["gathered"][s], 16 * (LISTED // 4))
                pool.wait_ge(S["extra_ready"], 1)
                n_extra = pool.value_load(extra_row[0:1, 0:1], min_val=0, max_val=MAX_EXTRA)
                with pool.If(n_extra > 0):
                    with pool.Fori(0, n_extra) as o:
                        pool.wait_ge(S["idx_ready"], o + 1 + LISTED)
                        gather(0, 0).then_inc(S["e_x"], 16)
                        pool.wait_ge(S["y_act"], o + 1 + EXPERTS)
                        pool.wait_ge(S["y_dve"], o + 1 + EXPERTS)
                        scatter(0, 0).then_inc(S["e_x"], 16)
                pool.wait_ge(S["gate_in"], 32 * streams)
                for t in range(nt):
                    for n, q in enumerate(POOL_QTRS):
                        pool.wait_ge(S["y_in"][q], 16 * (t + 1))
                        y = y_quarter[q]
                        for w in (4, 2, 1):
                            pool_linked(pool.tensor_tensor(y[:, 0:w], y[:, 0:w], y[:, w:2 * w], ALU.add))
                        cols = slice(q * QTR, (q + 1) * QTR)
                        pool_linked(pool.tensor_tensor(y[:, 0], y[:, 0], mods[:, t // 2, 2, cols], ALU.mult))
                        pool.tensor_tensor(x_rows[:, t, cols], x_rows[:, t, cols], y[:, 0], ALU.add).then_inc(S["x_done_pool"], 1)
                if l + 1 < DEPTH:
                    pool.wait_ge(S["x_done"], nt * (4 - len(POOL_QTRS)))

        @block.scalar
        def _(act):
            link = [0]

            def linked(ins):
                link[0] += 1
                ins.then_inc(act_link, 1)
                act.wait_ge(act_link, link[0])

            act.wait_ge(cond_in, 32)
            act.activation(cond_silu[:, :, :], cond[:, :, :].rearrange("p s k -> p k s"), ACT.Sigmoid).then_inc(cond_sig, 1)

            act.wait_ge(cond_ready, 1)
            act.activation(cond_hi[:, :, :], cond_silu[:, :, :], ACT.Copy).then_inc(cond_sig, 1)
            for l in range(DEPTH):
                def split_round(j):
                    for s in range(MOD_SLOTS):
                        act.wait_ge(mod_w_in[s], 16 * (j + 1 + l * (MOD_CHUNKS // MOD_SLOTS)))
                        for h in range(PIECES):
                            ge(act, mod_filled, PIECES * (l * MOD_CHUNKS + j * MOD_SLOTS + s - 1) + h + 1)
                            act.activation(mod_w_hi[:, h], mod_w[:, s, h * PIECE_K:(h + 1) * PIECE_K, :], ACT.Copy).then_inc(mod_hi, 1)

                split_round(0)
                with act.Fori(1, MOD_CHUNKS // MOD_SLOTS) as j:
                    split_round(j)

            def drain(key, out, func=ACT.Copy, **kw):
                wait_filled(act, *key)
                act.activation(out, kw.pop("in_"), func, **kw).then_inc(drained["act"], 1)

            def norm_tiles(l, n):
                S = L[min(l, DEPTH - 1)]
                done = TILES + 3 if l == DEPTH else 0
                for t in range(n):
                    if l:
                        act.wait_ge(L[l - 1]["x_done"], (t + 1) * (4 - len(POOL_QTRS)))
                        act.wait_ge(L[l - 1]["x_done_pool"], (t + 1) * len(POOL_QTRS))
                    act.activation(h_rows[:, t, :] if l else first_squares, x_rows[:, t, :], ACT.Square,
                                   accum_out=stats[:, 0, t:t + 1]).then_inc(S["norm_sums"], 1)
                    act.wait_ge(S["norm_var"], done + t + 1)
                    act.activation(stats[:, 2, t:t + 1], stats[:, 1, t:t + 1], ACT.Sqrt).then_inc(S["norm_root"], 1)

            for l in range(DEPTH):
                S = L[l]
                nt = active_tiles(l)
                if l == 0:
                    act.wait_ge(x_in, 32)
                norm_tiles(l, TILES)
                if l:
                    load_mixer_weights(act, l)
                for t in range(TILES):
                    drain((l, "T1", t, 0), h_T[:, 0:4, t * P:(t + 1) * P], in_=split(bank_of(l, "T1", t, 0)[:, :], (4, P)))
                ge(act, mod_stored, 16 * DEPTH * (l == 0))
                for t in range(TILES):
                    for c, (lo, hi) in enumerate(u_chunks(l, t)):
                        key = (l, "U", t, c)
                        if jobs.by[key] == "act":
                            drain(key, u_rows[:, t, lo:hi], in_=bank_of(*key)[:, 0:hi - lo])
                wait_drained(act, l, "U", TILES - 1, 0)
                wait_drained(act, l, "U", TILES - 1, len(u_chunks(l, TILES - 1)) - 1)
                wait_drained(act, l, "U", TILES - 2, len(u_chunks(l, TILES - 2)) - 1)
                wait_filled(act, l, "U", TILES - 1, len(u_chunks(l, TILES - 1)) - 1)
                for t in range(TILES):
                    if t < nt:
                        act.activation(square_out[:, 0:Q_LORA], u_rows[:, t, COL_Q:COL_KV], ACT.Square,
                                       accum_out=stats[:, 0, t:t + 1]).then_inc(act_link, 1)
                        link[0] += 1
                        act.wait_ge(act_link, link[0])
                    act.activation(square_out[:, 0:KV_LORA], u_rows[:, t, COL_KV:COL_KR], ACT.Square,
                                   accum_out=stats[:, 0, 4 + t:5 + t]).then_inc(act_link, 1)
                    link[0] += 1
                    act.wait_ge(act_link, link[0])
                act.activation(square_out[:, 0:1], stats[:, 0, 4:5], ACT.Copy).then_inc(S["norm_sums"], 1)
                act.wait_ge(S["norm_var"], TILES + 2)
                act.activation(stats[:, 2, 4:8], stats[:, 1, 4:8], ACT.Sqrt).then_inc(S["norm_root"], 1)
                act.activation(stats[:, 2, 0:nt], stats[:, 1, 0:nt], ACT.Sqrt).then_inc(S["norm_root"], 1)
                for s in range(nt // 2):
                    for c in range(2):
                        key = (l, "POOLED", s, c)
                        if s:
                            wait_filled(act, l, "POOL_OUT", s - 1, c)
                        drain(key, pooled[:, c, :], in_=bank_of(*key)[:, 0:SEQ])
                    for c in range(2):
                        key = (l, "DFT_CH", s, c)
                        if s:
                            wait_filled(act, l, "FNO_OUT", s - 1, c)
                        drain(key, dft_ch[:, c, :], in_=bank_of(*key)[:, 0:SEQ])
                    for c in range(2):
                        key = (l, "FNO_OUT", s, c)
                        drain(key, mixed[:, 2 + c, s * SEQ:(s + 1) * SEQ], in_=bank_of(*key)[:, 0:SEQ])
                for t in range(nt):
                    drain((l, "CQ", t), c_T[:, 0:3, t * P:(t + 1) * P], in_=split(bank_of(l, "CQ", t)[:, 0:3 * P], (3, P)))
                for t in range(TILES + 1):
                    if t < TILES:
                        if t < nt:
                            drain((l, "Q", t, 0), q_rows[:, t % 2, 0:512], in_=bank_of(l, "Q", t, 0)[:, :], scale=SCALE)
                        key = (l, "KV", t, 0)
                        b = split(bank_of(*key)[:, :], (4, P))
                        wait_filled(act, *key)
                        act.activation(split(k_rows[:, t % 2, 0:4 * QK], (4, QK))[:, :, 0:NOPE], b[:, :, 0:NOPE], ACT.Copy)
                        act.activation(split(v_rows[:, t, 0:256], (4, V_DIM)), b[:, :, NOPE:], ACT.Copy).then_inc(drained["act"], 1)
                    if 1 <= t <= nt:
                        for g in range(2):
                            drain((l, "QT", t - 1, g), q_T[0:QK, 4 * g:4 * g + 4, (t - 1) * P:t * P],
                                  in_=split(bank_of(l, "QT", t - 1, g)[0:QK, :], (4, P)))
                m = len(units(l))
                for i in range(m + 2):
                    if i < m:
                        lo, hi = keys_of(units(l)[i][0])
                        n = hi - lo
                        wait_filled(act, l, "S", i)
                        act.wait_ge(S["row_max"], i + 1)
                        if i >= 2:
                            wait_filled(act, l, "PT", i - 2)
                        act.activation(p_rows[:, i % 2, 0:n], bank_of(l, "S", i)[:, 0:n], ACT.Exp, bias=soft[:, 0, i:i + 1],
                                       accum_out=soft[:, 1, i:i + 1]).then_inc(drained["act"], 1)
                    if i >= 2:
                        lo, hi = keys_of(units(l)[i - 2][0])
                        n = hi - lo
                        if i >= 4:
                            wait_filled(act, l, "O", i - 4)
                        drain((l, "PT", i - 2), p_T[:, i % 2, 0:n], in_=bank_of(l, "PT", i - 2)[:, 0:n])
                act.wait_ge(S["x_mixed"], nt)
                for t in range(nt):
                    act.activation(h_rows[:, t, :], x_rows[:, t, :], ACT.Square, accum_out=stats[:, 0, t:t + 1]).then_inc(S["norm_sums"], 1)
                act.wait_ge(S["norm_var"], TILES + 3)
                act.activation(stats[:, 2, 0:nt], stats[:, 1, 0:nt], ACT.Sqrt).then_inc(S["norm_root"], 1)
                for t in range(nt):
                    drain((l, "T2", t, 0), h_T[:, 0:4, t * P:(t + 1) * P], in_=split(bank_of(l, "T2", t, 0)[:, :], (4, P)))
                for t in range(nt):
                    drain((l, "R", t), prob[:, t, :], ACT.Sigmoid, in_=bank_of(l, "R", t)[:, 0:EXPERTS])
                for t in range(nt + 1):
                    if t < nt:
                        wait_filled(act, l, "SG", t)
                        if t >= 2:
                            wait_drained(act, l, "SG", t - 2)
                        act.activation(sig[:, t % 2, :], bank_of(l, "SG", t)[:, 0:FE], ACT.Sigmoid).then_inc(S["shared_sig"], 1)
                    if t >= 1:
                        if t >= 3:
                            wait_filled(act, l, "SD", t - 3, 1)
                        drain((l, "SH", t - 1), hid_T[:, (t - 1) % 2], in_=split(bank_of(l, "SH", t - 1)[:, 0:2 * P], (2, P)))

                def x_drain(i, s):
                    act.wait_ge(S["xt_filled"], i + 1)
                    ge(act, S["gu_filled"], i - 1)
                    act.activation(x_gT[:, s % 2, 0:4, :], split(banks[0][:, :], (4, P)), ACT.Copy).then_inc(S["xt_act"], 1)

                x_drain(0, 0)

                def step(j, s):
                    i = j * UNROLL + s
                    x_drain(i + 1, s + 1)
                    act.wait_ge(S["gu_filled"], i + 1)
                    ge(act, S["hid_ready"], i - 1)
                    act.activation(sig[:, s % 2, :], banks[2 + s % 2][:, 0:FE], ACT.Sigmoid).then_inc(S["sig_ready"], 1)
                    if not (isinstance(i, int) and i == 0):
                        y_drain(i - 1, j, s - 1)

                def y_drain(i, j, s):
                    act.wait_ge(S["d_filled"], i + 1)
                    act.wait_ge(S["idx_ready"], i + 1)
                    ge(act, S["scattered"][s % 2], (j * (UNROLL // 2) + s // 2) * 16)
                    c = s % UNROLL
                    act.activation(y_g[:, s % 2, 0:512], banks[6][:, :], ACT.Copy, scale=row_w[:, c:c + 1]).then_inc(S["y_act"], 1)

                for s in range(UNROLL):
                    step(0, s)
                with act.Fori(1, EXPERTS // UNROLL) as j:
                    for s in range(UNROLL):
                        step(j, s)
                y_drain(EXPERTS - 1, EXPERTS // UNROLL - 1, UNROLL - 1)
                act.wait_ge(S["extra_ready"], 1)
                n_extra = act.value_load(extra_row[0:1, 0:1], min_val=0, max_val=MAX_EXTRA)

                def block_x(o):
                    act.wait_ge(S["xt_filled"], o + 1 + EXPERTS + 1)
                    act.activation(x_gT[:, 0, 0:4, :], split(banks[0][:, :], (4, P)), ACT.Copy).then_inc(S["xt_act"], 1)

                def block_y(o):
                    act.wait_ge(S["gu_filled"], o + 1 + EXPERTS)
                    act.activation(sig[:, 0, :], banks[2][:, 0:FE], ACT.Sigmoid).then_inc(S["sig_ready"], 1)
                    act.wait_ge(S["d_filled"], o + 1 + EXPERTS)
                    act.activation(y_g[:, 0, 0:512], banks[6][:, :], ACT.Copy, scale=row_w[:, 0:1]).then_inc(S["y_act"], 1)

                with act.If(n_extra > 0):
                    block_x(0)
                if l + 1 < DEPTH:
                    load_w_in(act, l + 1, 0, DK)
                with act.If(n_extra > 0):
                    block_y(0)
                with act.If(n_extra > 1):
                    with act.Fori(1, n_extra) as o:
                        block_x(o)
                        block_y(o)
            norm_tiles(DEPTH, LATENT_TILES)

        @block.vector
        def _(dve):
            link = [0]

            def linked(ins):
                link[0] += 1
                ins.then_inc(dve_link, 1)
                dve.wait_ge(dve_link, link[0])

            dve.memset(ones[:, :], 1.0).then_inc(ones_ready, 1)
            dve.wait_ge(cond_sig, 1)
            dve.tensor_tensor(cond_silu[:, :, :], cond_silu[:, :, :], cond[:, :, :].rearrange("p s k -> p k s"),
                              ALU.mult).then_inc(cond_ready, 1)
            dve.wait_ge(cond_sig, 2)
            dve.tensor_tensor(cond_lo[:, :, :], cond_silu[:, :, :], cond_hi[:, :, :].bitcast(F32), ALU.subtract).then_inc(cond_ready, 1)
            for l in range(DEPTH):
                def add_bias(c, slot):
                    dve.wait_ge(mod_filled, PIECES * (l * MOD_CHUNKS + c + 1))
                    dve.tensor_tensor(mod_rows[l][:, bass.ds(c * MOD_N, MOD_N)], banks[slot][0:2, :], mod_rows[l][:, bass.ds(c * MOD_N, MOD_N)],
                                      ALU.add).then_inc(mod_added, 1)

                def split_round(j, first):
                    for s in range(MOD_SLOTS):
                        for h in range(PIECES):
                            piece = PIECES * (l * MOD_CHUNKS + j * MOD_SLOTS + s) + h
                            dve.wait_ge(mod_hi, piece + 1)
                            ge(dve, mod_filled, piece + 1 - PIECES)
                            dve.tensor_tensor(mod_w_lo[:, h], mod_w[:, s, h * PIECE_K:(h + 1) * PIECE_K, :],
                                              mod_w_hi[:, h].bitcast(F32), ALU.subtract).then_inc(mod_lo, 1)
                        if first and s == 0:
                            if l == 0:
                                dve.wait_ge(mod_bias_in, 64)
                        else:
                            add_bias(j * MOD_SLOTS + s - 1, (s - 1) % MOD_SLOTS)

                split_round(0, True)
                with dve.Fori(1, MOD_CHUNKS // MOD_SLOTS) as j:
                    split_round(j, False)
                add_bias(MOD_CHUNKS - 1, MOD_SLOTS - 1)
                dve.wait_ge(mod_added, (l + 1) * MOD_CHUNKS)
                dve.wait_ge(mod_bias_in, 64 + 32 * l)
                linked(dve.scalar_tensor_tensor(out=mod_rows[l][:, D:2 * D], in0=mod_rows[l][:, D:2 * D], scalar=1.0,
                                                in1=gain_rows[:, 0:D], op0=ALU.add, op1=ALU.mult))
                dve.scalar_tensor_tensor(out=mod_rows[l][:, 4 * D:5 * D], in0=mod_rows[l][:, 4 * D:5 * D], scalar=1.0,
                                         in1=gain_rows[:, D:], op0=ALU.add, op1=ALU.mult).then_inc(mod_ready, 1)

            def rstd(lo, hi, roots, value):
                v, root, r, tmp = stats[:, 1, lo:hi], stats[:, 2, lo:hi], stats[:, 3, lo:hi], newton[:, lo:hi]
                dve.wait_ge(roots, value)
                linked(dve.reciprocal(r, root))
                linked(dve.tensor_tensor(tmp, r, r, ALU.mult))
                linked(dve.tensor_tensor(tmp, tmp, v, ALU.mult))
                linked(dve.tensor_scalar(tmp, tmp, -0.5, 1.5, ALU.mult, ALU.add))
                linked(dve.tensor_tensor(r, r, tmp, ALU.mult))

            def normed(t, ready):
                s = t // STREAM_TILES
                linked(dve.scalar_tensor_tensor(out=h_rows[:, t, :], in0=x_rows[:, t, :], scalar=stats[:, 3, t:t + 1],
                                                in1=mods[:, s, 1, :], op0=ALU.mult, op1=ALU.mult))
                dve.tensor_tensor(h_rows[:, t, :], h_rows[:, t, :], mods[:, s, 0, :], ALU.add).then_inc(ready, 1)

            def drain(key, out, in_):
                wait_filled(dve, *key)
                dve.tensor_copy(out, in_).then_inc(drained["dve"], 1)

            def gated(key, t, c, tmp, last):
                s = t // STREAM_TILES
                wait_filled(dve, *key)
                dve.tensor_tensor(tmp, bank_of(*key)[:, :], mods[:, s, 2, c * 512:(c + 1) * 512], ALU.mult).then_inc(drained["dve"], 1)
                wait_drained(dve, *key)
                ins = dve.tensor_tensor(x_rows[:, t, c * 512:(c + 1) * 512], x_rows[:, t, c * 512:(c + 1) * 512], tmp, ALU.add)
                if last is not None:
                    ins.then_inc(last, 1)
                else:
                    linked(ins)

            def norm_tiles(l, n):
                S = L[min(l, DEPTH - 1)]
                done = TILES + 3 if l == DEPTH else 0
                for t in range(n + 1):
                    if l and t < n:
                        add_expert_rows(l - 1, t)
                    if t >= 1:
                        u = t - 1
                        dve.wait_ge(S["norm_sums"], done + u + 1)
                        dve.tensor_scalar(stats[:, 1, u:t], stats[:, 0, u:t], 1.0 / D, EPS, ALU.mult, ALU.add).then_inc(S["norm_var"], 1)
                        rstd(u, t, S["norm_root"], done + t)
                        if l < DEPTH:
                            if u == 0:
                                dve.wait_ge(S["mods_in"], 32)
                            normed(u, S["h_ready"])
                        else:
                            dve.wait_ge(S["last_gain_in"], 16)
                            dve.scalar_tensor_tensor(out=h_rows[:, u, :], in0=x_rows[:, u, :], scalar=stats[:, 3, u:t], in1=mods[:, 1, 0, :],
                                                     op0=ALU.mult, op1=ALU.mult).then_inc(S["out_ready"], 1)

            def add_expert_rows(l, t):
                S = L[l]
                for q in range(4):
                    if q in POOL_QTRS:
                        continue
                    dve.wait_ge(S["y_in"][q], 16 * (t + 1))
                    y = y_quarter[q]
                    cols = slice(q * QTR, (q + 1) * QTR)
                    linked(dve.tensor_reduce(y_sum[:, :], y.rearrange("p k n -> p n k"), AX.X, ALU.add))
                    linked(dve.tensor_tensor(y_sum[:, :], y_sum[:, :], mods[:, t // 2, 2, cols], ALU.mult))
                    dve.tensor_tensor(x_rows[:, t, cols], x_rows[:, t, cols], y_sum[:, :], ALU.add).then_inc(S["x_done"], 1)
                    dve.wait_ge(S["x_done"], t * (4 - len(POOL_QTRS)) + q + 1)

            dve.wait_ge(const_in, 8 * 16)
            for l in range(DEPTH):
                S = L[l]
                nt = active_tiles(l)
                norm_tiles(l, TILES)
                for t in range(TILES):
                    drain((l, "T1", t, 1), h_T[:, 4:8, t * P:(t + 1) * P], split(bank_of(l, "T1", t, 1)[:, :], (4, P)))
                ge(dve, mod_stored, 16 * DEPTH * (l == 0))
                for t in range(TILES):
                    for c, (lo, hi) in enumerate(u_chunks(l, t)):
                        key = (l, "U", t, c)
                        if jobs.by[key] == "dve":
                            drain(key, u_rows[:, t, lo:hi], bank_of(*key)[:, 0:hi - lo])
                dve.wait_ge(S["norm_sums"], TILES + 1)
                dve.tensor_scalar(stats[:, 1, 0:nt], stats[:, 0, 0:nt], 1.0 / Q_LORA, EPS, ALU.mult, ALU.add).then_inc(S["norm_var"], 1)
                dve.tensor_scalar(stats[:, 1, 4:8], stats[:, 0, 4:8], 1.0 / KV_LORA, EPS, ALU.mult, ALU.add).then_inc(S["norm_var"], 1)
                rstd(0, nt, S["norm_root"], TILES + 2)
                rstd(4, 8, S["norm_root"], TILES + 2)
                dve.wait_ge(S["w_lora_in"], 64)
                for t in range(TILES):
                    if t < nt:
                        dve.scalar_tensor_tensor(out=u_rows[:, t, COL_Q:COL_KV], in0=u_rows[:, t, COL_Q:COL_KV], scalar=stats[:, 3, t:t + 1],
                                                 in1=g_lora[:, 0:Q_LORA], op0=ALU.mult, op1=ALU.mult)
                    dve.scalar_tensor_tensor(out=u_rows[:, t, COL_KV:COL_KR], in0=u_rows[:, t, COL_KV:COL_KR], scalar=stats[:, 3, 4 + t:5 + t],
                                             in1=g_lora[:, Q_LORA:], op0=ALU.mult, op1=ALU.mult).then_inc(S["lora_ready"], 1)
                dve.wait_ge(S["mixer_in"], 6 * 16)
                for s in range(nt // 2):
                    for c in range(2):
                        key = (l, "DFT_POS", s, c)
                        if s:
                            wait_filled(dve, l, "DFT_CH", s - 1, c)
                        drain(key, dft_pos[:, c, :], bank_of(*key)[:, :])
                    for c in range(2):
                        key = (l, "POOL_OUT", s, c)
                        wait_filled(dve, *key)
                        dve.tensor_scalar(mixed[:, c, s * SEQ:(s + 1) * SEQ], bank_of(*key)[:, 0:SEQ], pool_scale[:, c:c + 1], None,
                                          ALU.mult).then_inc(drained["dve"], 1)
                for t in range(TILES):
                    drain((l, "CKV", t), c_T[:, 3:5, t * P:(t + 1) * P], split(bank_of(l, "CKV", t)[:, 0:2 * P], (2, P)))

                def rotate(x1, x2, cos, sin, shape, last):
                    n = shape[0] * shape[1] * shape[2]
                    tmp = [split(rope_tmp[:, i, 0:n], shape) for i in range(4)]
                    for o, x, y in ((tmp[0], x1, cos), (tmp[1], x2, sin), (tmp[2], x2, cos)):
                        dve.tensor_tensor(o, x, y, ALU.mult)
                    linked(dve.tensor_tensor(tmp[3], x1, sin, ALU.mult))
                    dve.tensor_tensor(x1, tmp[0], tmp[1], ALU.subtract)
                    ins = dve.tensor_tensor(x2, tmp[2], tmp[3], ALU.add)
                    if last is None:
                        linked(ins)
                    else:
                        ins.then_inc(last, 1)
                        dve.wait_ge(last, rotations[0])

                rotations = [0]
                for t in range(TILES + 1):
                    if t < TILES:
                        if t < nt:
                            key = (l, "Q", t, 1)
                            wait_filled(dve, *key)
                            dve.tensor_scalar(q_rows[:, t % 2, 512:768], bank_of(*key)[:, 0:256], SCALE, None, ALU.mult).then_inc(drained["dve"], 1)
                            if t < LATENT_TILES:
                                wait_drained(dve, l, "Q", t, 0)
                                wait_drained(dve, l, "Q", t, 1)
                                q4 = q_rows[:, t % 2, :].rearrange("p (h q) -> p h q", h=HEADS)[:, :, NOPE:]
                                q4 = q4.rearrange("p h (x f) -> p h x f", x=4)
                                cos, sin = (split(rope_tab[:, t, i, :], (2, 8)).unsqueeze(1).broadcast_to([P, HEADS, 2, 8]) for i in range(2))
                                rotations[0] += 1
                                rotate(q4[:, :, 0::2, :], q4[:, :, 1::2, :], cos, sin, (HEADS, 2, 8), S["q_rotated"])
                        kr = u_rows[:, t, COL_KR:]
                        if t < LATENT_TILES:
                            k4 = kr.rearrange("p (a x f) -> p a x f", a=1, x=4)
                            cos, sin = (split(rope_tab[:, t, i, :], (1, 2, 8)) for i in range(2))
                            rotate(k4[:, :, 0::2, :], k4[:, :, 1::2, :], cos, sin, (1, 2, 8), None)
                        key = (l, "KV", t, 1)
                        b = split(bank_of(*key)[:, :], (4, P))
                        wait_filled(dve, *key)
                        dve.tensor_copy(split(k_rows[:, t % 2, 4 * QK:], (4, QK))[:, :, 0:NOPE], b[:, :, 0:NOPE])
                        dve.tensor_copy(split(v_rows[:, t, 256:], (4, V_DIM)), b[:, :, NOPE:]).then_inc(drained["dve"], 1)
                        dve.tensor_copy(split(k_rows[:, t % 2, :], (HEADS, QK))[:, :, NOPE:],
                                        kr.unsqueeze(1).broadcast_to([P, HEADS, ROPE])).then_inc(S["k_ready"], 1)
                    if t >= 1:
                        for g in range(2):
                            drain((l, "KT", t - 1, g), k_T[0:QK, 4 * g:4 * g + 4, (t - 1) * P:t * P],
                                  split(bank_of(l, "KT", t - 1, g)[0:QK, :], (4, P)))
                m = len(units(l))
                for i in range(m + 3):
                    if i < m:
                        lo, hi = keys_of(units(l)[i][0])
                        wait_filled(dve, l, "S", i)
                        dve.tensor_reduce(soft[:, 0, i:i + 1], bank_of(l, "S", i)[:, 0:hi - lo], AX.X, ALU.max, negate=True).then_inc(S["row_max"], 1)
                    if 1 <= i < m + 1:
                        lo, hi = keys_of(units(l)[i - 1][0])
                        wait_drained(dve, l, "S", i - 1)
                        linked(dve.reciprocal(soft[:, 2, i - 1:i], soft[:, 1, i - 1:i]))
                        pr = p_rows[:, (i - 1) % 2, 0:hi - lo]
                        dve.tensor_scalar(pr, pr, soft[:, 2, i - 1:i], None, ALU.mult).then_inc(S["p_ready"], 1)
                    if i >= 3:
                        qt, h = units(l)[i - 3]
                        rows = slice(64 * (h % 2), 64 * (h % 2) + 64)
                        drain((l, "O", i - 3), mixed[rows, 4 + h // 2, qt * P:(qt + 1) * P], bank_of(l, "O", i - 3)[rows, 0:P])
                dve.wait_ge(S["gate_in"], 16 * (nt // 2))
                for t in range(nt):
                    for c in range(2):
                        gated((l, "OUT", t, c), t, c, res_tmp[:, c, :], S["x_mixed"] if c else None)
                dve.wait_ge(S["norm_sums"], TILES + 1 + nt)
                dve.tensor_scalar(stats[:, 1, 0:nt], stats[:, 0, 0:nt], 1.0 / D, EPS, ALU.mult, ALU.add).then_inc(S["norm_var"], 1)
                rstd(0, nt, S["norm_root"], TILES + 3)
                dve.wait_ge(S["mods_in"], 32 + 16 * (nt // 2))
                for t in range(nt):
                    normed(t, S["h2_ready"])
                for t in range(nt):
                    drain((l, "T2", t, 1), h_T[:, 4:8, t * P:(t + 1) * P], split(bank_of(l, "T2", t, 1)[:, :], (4, P)))

                N = nt
                dve.wait_ge(S["router_in"], 32)
                for t in range(N):
                    wait_drained(dve, l, "R", t)
                    ins = dve.tensor_tensor(sel[:, t, :], prob[:, t, :], r_bias[:, :], ALU.add)
                linked(ins)
                for t in range(N):
                    for g in range(EGROUPS):
                        ins = dve.max(out=top2[:, t, g, :], in_=sel[:, t, 8 * g:8 * g + 8])
                linked(ins)
                linked(dve.tensor_tensor(gscore[:, 0:N, :], top2[:, 0:N, :, 0], top2[:, 0:N, :, 1], ALU.add))
                other = gscore[:, 0:N, :].unsqueeze(2).broadcast_to([P, N, 8, 8])
                own = gscore[:, 0:N, :].unsqueeze(3).broadcast_to([P, N, 8, 8])
                tie_b = split(tie[:, :], (8, 8)).unsqueeze(1).broadcast_to([P, N, 8, 8])
                dve.tensor_tensor(cmp_a[:, 0:N], other, own, ALU.is_gt)
                linked(dve.tensor_tensor(cmp_b[:, 0:N], other, own, ALU.is_equal))
                linked(dve.tensor_tensor(cmp_b[:, 0:N], cmp_b[:, 0:N], tie_b, ALU.mult))
                linked(dve.tensor_tensor(cmp_a[:, 0:N], cmp_a[:, 0:N], cmp_b[:, 0:N], ALU.add))
                linked(dve.tensor_reduce(gmask[:, 0:N, :], cmp_a[:, 0:N], AX.X, ALU.add))
                linked(dve.tensor_scalar(gmask[:, 0:N, :], gmask[:, 0:N, :], TOP_GROUPS - 0.5, None, ALU.is_lt))
                linked(dve.tensor_scalar(gneg[:, 0:N, :], gmask[:, 0:N, :], 1.0, 1e30, ALU.subtract, ALU.mult))
                sel4 = sel[:, 0:N, :].rearrange("p t (g e) -> p t g e", g=8)
                linked(dve.tensor_tensor(sel4, sel4, gmask[:, 0:N, :].unsqueeze(3).broadcast_to([P, N, 8, 8]), ALU.mult))
                linked(dve.tensor_tensor(sel4, sel4, gneg[:, 0:N, :].unsqueeze(3).broadcast_to([P, N, 8, 8]), ALU.add))
                for t in range(N):
                    ins = dve.max(out=top8[:, t, :], in_=sel[:, t, :])
                linked(ins)
                for t in range(N):
                    ins = dve.match_replace(out=chosen[:, t, :], in_to_replace=top8[:, t, :], in_values=sel[:, t, :], imm_value=-2e30)
                linked(ins)
                dve.tensor_scalar(chosen[:, 0:N, :], chosen[:, 0:N, :], -1.5e30, None, ALU.is_lt).then_inc(S["chosen_ready"], 1)
                dve.wait_ge(S["chosen_ready"], 1)
                linked(dve.tensor_tensor(prob[:, 0:N, :], prob[:, 0:N, :], chosen[:, 0:N, :], ALU.mult))
                linked(dve.tensor_reduce(wsum[:, 0:N], prob[:, 0:N, :], AX.X, ALU.add))
                linked(dve.reciprocal(winv[:, 0:N], wsum[:, 0:N]))
                dve.memset(vals[:, 0:N, :, :], 0.0)
                linked(dve.memset(posm[:, 0:N, :], -1.0))
                for t in range(N):
                    dve.tensor_scalar(vals[:, t, 0:EXPERTS, 2], prob[:, t, :], winv[:, t:t + 1], ROUTED_SCALE, ALU.mult, ALU.mult)
                    dve.tensor_scalar(vals[:, t, 0:EXPERTS, 0], slots_iota[:, 0:EXPERTS], 0.0, token_cols[:, t:t + 1], ALU.mult, ALU.add)

                dve.wait_ge(S["gate_in"], 32 * (nt // 2))
                for t in range(nt + 1):
                    if t < nt:
                        key = (l, "SG", t)
                        b = bank_of(*key)
                        wait_filled(dve, *key)
                        dve.wait_ge(S["shared_sig"], t + 1)
                        if t >= 2:
                            wait_filled(dve, l, "SH", t - 2)
                        linked(dve.tensor_tensor(hid[:, t % 2, :], sig[:, t % 2, :], b[:, 0:FE], ALU.mult))
                        dve.tensor_tensor(hid[:, t % 2, :], hid[:, t % 2, :], b[:, FE:], ALU.mult).then_inc(drained["dve"], 1)
                    if t >= 1:
                        for c in range(2):
                            gated((l, "SD", t - 1, c), t - 1, c, moe_tmp[:, c, :], None)
                drain((l, "MT"), ranks_T[0:64, 0:N, :], split(bank_of(l, "MT")[0:64, 0:N * P], (N, P)))
                key = (l, "RANK")
                wait_filled(dve, *key)
                b = split(bank_of(*key)[:, 0:N * EXPERTS], (N, EXPERTS))
                for t in range(N):
                    ins = dve.tensor_scalar(vals[:, t, 0:EXPERTS, 1], b[:, t, :], token_cols[:, 4 + t:5 + t], None, ALU.add)
                ins.then_inc(drained["dve"], 1)
                key = (l, "POS")
                wait_filled(dve, *key)
                b = split(bank_of(*key)[:, 0:(TILES + 1) * EXPERTS], (TILES + 1, EXPERTS))
                linked(dve.scalar_tensor_tensor(out=posm[:, 0:N, 0:EXPERTS], in0=b[:, 0:N, :], scalar=1.0, in1=chosen[:, 0:N, :],
                                                op0=ALU.add, op1=ALU.mult))
                linked(dve.tensor_scalar(posm[:, 0:N, 0:EXPERTS], posm[:, 0:N, 0:EXPERTS], -1.0, None, ALU.add))
                cnt = bank_of(*key)[0:64, TILES * EXPERTS:TILES * EXPERTS + 1]
                linked(dve.tensor_scalar(ext[0:64, 0:1], cnt, float(P) + 0.5, None, ALU.is_gt))
                for b_ in range(2, N):
                    linked(dve.tensor_scalar(ext[0:64, 1:2], cnt, float(P * b_) + 0.5, None, ALU.is_gt))
                    linked(dve.tensor_tensor(ext[0:64, 0:1], ext[0:64, 0:1], ext[0:64, 1:2], ALU.add))
                dve.tensor_scalar(ext_b, ones[0:64, :], ext[0:64, 0:1], None, ALU.mult).then_inc(drained["dve"], 1)

                def make_g(i, e, s, offset):
                    for t in range(N):
                        ins = dve.tensor_scalar(one_hot[:, s % 2, t, :], slots_iota[:, bass.ds(offset, P)], posm[:, t, bass.ds(e, 1)], None, ALU.is_equal)
                    return ins

                def take_list(s):
                    dve.tensor_copy(row_w[:, s % UNROLL:s % UNROLL + 1], banks[5][:, 2:3])
                    return dve.tensor_scalar(row_idx[:, s % UNROLL, :], banks[5][:, 0:2], float(SKIP), None, ALU.add)

                key = (l, "ENDS")
                wait_filled(dve, *key)
                b = bank_of(*key)
                dve.tensor_scalar(ends[:, 0:64], b[:, 0:64], lane[:, 0:1], None, ALU.is_le)
                linked(dve.tensor_copy(table[:, 0:1], b[:, 63:64]))
                dve.tensor_reduce(table[:, 1:2], ends[:, 0:64], AX.X, ALU.add)
                dve.tensor_tensor(ends[:, 64:128], ends[:, 0:64], b[:, 64:128], ALU.mult).then_inc(drained["dve"], 1)
                wait_drained(dve, *key)
                linked(dve.tensor_reduce(table[:, 2:3], ends[:, 64:128], AX.X, ALU.add))
                linked(dve.tensor_scalar(table[:, 1:2], table[:, 1:2], float(EXPERTS - 1), None, ALU.min))
                linked(dve.tensor_scalar(table[:, 2:3], table[:, 2:3], -1.0, lane[:, 0:1], ALU.mult, ALU.add))
                dve.tensor_scalar(table[:, 2:3], table[:, 2:3], 1.0, 0.0, ALU.add, ALU.max).then_inc(S["table_ready"], 1)
                key = (l, "EXTRA")
                wait_filled(dve, *key)
                dve.tensor_copy(extra_row[:, :], bank_of(*key)[0:1, 0:3 * MAX_EXTRA]).then_inc(drained["dve"], 1)
                wait_drained(dve, *key)
                dve.memset(newton[:, 0:1], 0.0).then_inc(S["extra_ready"], 1)

                dve.wait_ge(drained["dve"], jobs.nth[(l, "POS")])
                for i in range(AHEAD):
                    ge(dve, S["list_filled"], i - 1)
                    make_g(i, i, i, 0).then_inc(S["g_ready"], 1)
                    if i >= 1:
                        dve.wait_ge(S["list_filled"], i)
                        take_list(i - 1).then_inc(S["idx_ready"], 1)
                dve.wait_ge(S["list_filled"], AHEAD)
                take_list(AHEAD - 1).then_inc(S["idx_ready"], 1)

                def x_drain(i, s):
                    dve.wait_ge(S["xt_filled"], i + 1)
                    ge(dve, S["gu_filled"], i - 1)
                    dve.tensor_copy(x_gT[:, s % 2, 4:8, :], split(banks[1][:, :], (4, P))).then_inc(S["xt_dve"], 1)

                def y_drain(i, j, s):
                    dve.wait_ge(S["d_filled"], i + 1)
                    ge(dve, S["scattered"][s % 2], (j * (UNROLL // 2) + s // 2) * 16)
                    c = s % UNROLL
                    dve.tensor_scalar(y_g[:, s % 2, 512:], banks[7][:, :], row_w[:, c:c + 1], None, ALU.mult).then_inc(S["y_dve"], 1)

                x_drain(0, 0)

                def step(j, s):
                    i = j * UNROLL + s
                    x_drain(i + 1, s + 1)
                    dve.wait_ge(S["list_filled"], i + AHEAD - 1)
                    make_g(i, i + AHEAD, s, 0).then_inc(S["g_ready"], 1)
                    dve.wait_ge(S["gu_filled"], i + 1)
                    dve.wait_ge(S["sig_ready"], i + 1)
                    ge(dve, S["ht_filled"], i - 1)
                    b = banks[2 + s % 2]
                    dve.tensor_tensor(hid[:, s % 2, :], sig[:, s % 2, :], b[:, 0:FE], ALU.mult).then_inc(S["hid_part"], 1)
                    dve.wait_ge(S["hid_part"], i + 1)
                    dve.tensor_tensor(hid[:, s % 2, :], hid[:, s % 2, :], b[:, FE:], ALU.mult).then_inc(S["hid_ready"], 1)
                    if not (isinstance(i, int) and i == 0):
                        y_drain(i - 1, j, s - 1)
                    dve.wait_ge(S["list_filled"], i + AHEAD + 1)
                    ge(dve, S["y_act"], i - AHEAD + 1)
                    ge(dve, S["scattered"][s % 2], ((UNROLL // 2) * j + (s - AHEAD) // 2 + 1) * 16)
                    take_list(s + AHEAD).then_inc(S["idx_ready"], 1)
                    dve.wait_ge(S["ht_filled"], i + 1)
                    ge(dve, S["d_filled"], i - 1)
                    dve.tensor_copy(hid_T[:, s % 2], split(banks[4][:, 0:2 * P], (2, P))).then_inc(S["ht_drained"], 1)

                for s in range(UNROLL):
                    step(0, s)
                with dve.Fori(1, EXPERTS // UNROLL) as j:
                    for s in range(UNROLL):
                        step(j, s)
                y_drain(EXPERTS - 1, EXPERTS // UNROLL - 1, UNROLL - 1)

                n_extra = dve.value_load(extra_row[0:1, 0:1], min_val=0, max_val=MAX_EXTRA)
                dve.wait_ge(S["scattered"][0], 16 * (EXPERTS // 2))
                with dve.If(n_extra > 0):
                    with dve.Fori(0, n_extra) as o:
                        e = dve.value_load(extra_row[0:1, bass.ds(o + MAX_EXTRA, 1)], min_val=0, max_val=EXPERTS - 1)
                        k = dve.value_load(extra_row[0:1, bass.ds(o + 2 * MAX_EXTRA, 1)], min_val=0, max_val=TILES - 1)
                        make_g(0, e, 0, k * P).then_inc(S["g_ready"], 1)
                        dve.wait_ge(S["list_filled"], o + 1 + LISTED)
                        take_list(0).then_inc(S["idx_ready"], 1)
                        dve.wait_ge(S["xt_filled"], o + 1 + EXPERTS + 1)
                        dve.tensor_copy(x_gT[:, 0, 4:8, :], split(banks[1][:, :], (4, P))).then_inc(S["xt_dve"], 1)
                        dve.wait_ge(S["gu_filled"], o + 1 + EXPERTS)
                        dve.wait_ge(S["sig_ready"], o + 1 + EXPERTS)
                        dve.tensor_tensor(hid[:, 0, :], sig[:, 0, :], banks[2][:, 0:FE], ALU.mult).then_inc(S["hid_part"], 1)
                        dve.wait_ge(S["hid_part"], o + 1 + EXPERTS)
                        dve.tensor_tensor(hid[:, 0, :], hid[:, 0, :], banks[2][:, FE:], ALU.mult).then_inc(S["hid_ready"], 1)
                        dve.wait_ge(S["ht_filled"], o + 1 + EXPERTS)
                        dve.tensor_copy(hid_T[:, 0], split(banks[4][:, 0:2 * P], (2, P))).then_inc(S["ht_drained"], 1)
                        dve.wait_ge(S["d_filled"], o + 1 + EXPERTS)
                        dve.tensor_scalar(y_g[:, 0, 512:], banks[7][:, :], row_w[:, 0:1], None, ALU.mult).then_inc(S["y_dve"], 1)
                        dve.wait_ge(S["e_x"], (o + 1) * 32)

                dve.wait_ge(S["scattered"][1], 16 * (EXPERTS // 2))
                dve.memset(newton[:, 0:1], 0.0).then_inc(S["rows_back"], 1)

            norm_tiles(DEPTH, LATENT_TILES)

        @block.tensor
        def _(pe):
            def claim(*key):
                prev = jobs.before(*key)
                if prev is not None:
                    wait_drained(pe, *prev)
                return bank_of(*key)

            pe.wait_ge(cond_ready, 2)
            for l in range(DEPTH):
                def mod_round(j):
                    for s in range(MOD_SLOTS):
                        c = l * MOD_CHUNKS + j * MOD_SLOTS + s
                        ge(pe, mod_added, c - MOD_SLOTS + 1)
                        for h in range(PIECES):
                            pe.wait_ge(mod_lo, PIECES * c + h + 1)
                            for k in range(PIECE_K):
                                for n, (x, w) in enumerate(((cond_hi, mod_w_hi), (cond_hi, mod_w_lo), (cond_lo, mod_w_hi))):
                                    mm = pe.matmul(banks[s][0:2, :], x[:, h * PIECE_K + k, :], w[:, h, k, :],
                                                   start=(h == k == n == 0), stop=(h == PIECES - 1 and k == PIECE_K - 1 and n == 2))
                            mm.then_inc(mod_filled, 1)

                mod_round(0)
                with pe.Fori(1, MOD_CHUNKS // MOD_SLOTS) as j:
                    mod_round(j)
            pe.wait_ge(mod_added, DEPTH * MOD_CHUNKS)
            pe.wait_ge(const_in, 8 * 16)
            pe.wait_ge(ones_ready, 1)

            for l in range(DEPTH):
                S = L[l]
                nt = active_tiles(l)

                def chain(key, cols, lhs, rhs, n):
                    b = claim(*key)
                    for k in range(n):
                        mm = pe.matmul(b[:, 0:cols], lhs(k), rhs(k), start=(k == 0), stop=(k == n - 1))
                    mm.then_inc(psum_filled, 1)

                def by_group(key, w, x):
                    b = claim(*key)
                    for g in range(2):
                        half = slice(64 * g, 64 * g + 64)
                        mm = pe.matmul(b[half, 0:SEQ], w[half, :], x[half, :], start=True, stop=True)
                    mm.then_inc(psum_filled, 1)

                def flips(key, blocks, rows=P):
                    b = claim(*key)
                    for n, x in enumerate(blocks):
                        mm = pe.transpose(b[0:rows, n * P:(n + 1) * P], x, ident[:, :])
                    mm.then_inc(psum_filled, 1)

                for t in range(TILES):
                    pe.wait_ge(S["h_ready"], t + 1)
                    for c in range(2):
                        flips((l, "T1", t, c), [h_rows[:, t, (4 * c + k) * P:(4 * c + k + 1) * P] for k in range(4)])
                pe.wait_ge(S["w_in_in"], 16 if l else 2 * 16)
                for t in range(TILES):
                    wait_drained(pe, l, "T1", t, 0)
                    wait_drained(pe, l, "T1", t, 1)
                    for c, (lo, hi) in enumerate(u_chunks(l, t)):
                        chain((l, "U", t, c), hi - lo, lambda k: h_T[:, k, t * P:(t + 1) * P], lambda k: w_in[:, k, lo:hi], DK)
                pe.wait_ge(S["mixer_in"], 6 * 16)
                for t in range(nt):
                    for c in range(len(u_chunks(l, t))):
                        wait_drained(pe, l, "U", t, c)
                for s in range(nt // 2):
                    for c in range(2):
                        b = claim(l, "POOLED", s, c)
                        for g in range(2):
                            for t in range(2):
                                lo = (2 * c + g) * GROUP
                                mm = pe.matmul(b[64 * g:64 * g + 64, 0:SEQ], u_rows[:, 2 * s + t, lo:lo + GROUP], pool_m[:, t, 2 * c + g, :],
                                               start=(t == 0), stop=(t == 1))
                        mm.then_inc(psum_filled, 1)
                    for c in range(2):
                        lo = COL_FNO + c * P
                        chain((l, "DFT_POS", s, c), 2 * SEQ, lambda t: u_rows[:, 2 * s + t, lo:lo + P], lambda t: dft_l[:, t, :], 2)
                    for c in range(2):
                        wait_drained(pe, l, "POOLED", s, c)
                        by_group((l, "POOL_OUT", s, c), w_pool_g[:, c, :], pooled[:, c, :])
                    for c in range(2):
                        wait_drained(pe, l, "DFT_POS", s, c)
                        chain((l, "DFT_CH", s, c), SEQ, lambda k: dft_c[:, k, :], lambda k: dft_pos[:, c, k * SEQ:(k + 1) * SEQ], 2)
                    for c in range(2):
                        wait_drained(pe, l, "DFT_CH", s, c)
                        by_group((l, "FNO_OUT", s, c), w_fno_g[:, c, :], dft_ch[:, c, :])
                for t in range(TILES):
                    pe.wait_ge(S["lora_ready"], t + 1)
                    if t < nt:
                        flips((l, "CQ", t), [u_rows[:, t, COL_Q + P * k:COL_Q + P * (k + 1)] for k in range(3)])
                    flips((l, "CKV", t), [u_rows[:, t, COL_KV + P * k:COL_KV + P * (k + 1)] for k in range(2)])
                for t in range(TILES + 1):
                    if t < TILES:
                        if t < nt:
                            wait_drained(pe, l, "CQ", t)
                            for c, (lo, hi) in enumerate(((0, 512), (512, 768))):
                                chain((l, "Q", t, c), hi - lo, lambda k: c_T[:, k, t * P:(t + 1) * P], lambda k: w_uq[:, k, lo:hi], 3)
                        wait_drained(pe, l, "CKV", t)
                        for c in range(2):
                            chain((l, "KV", t, c), 512, lambda k: c_T[:, 3 + k, t * P:(t + 1) * P], lambda k: w_ukv[:, k, 512 * c:512 * c + 512], 2)
                    if t >= 1:
                        u = t - 1
                        if u < nt:
                            wait_drained(pe, l, "Q", u, 0)
                            wait_drained(pe, l, "Q", u, 1)
                            if u < LATENT_TILES:
                                pe.wait_ge(S["q_rotated"], u + 1)
                        pe.wait_ge(S["k_ready"], u + 1)
                        wait_drained(pe, l, "KV", u, 0)
                        for g in range(2):
                            if u < nt:
                                flips((l, "QT", u, g), [q_rows[:, u % 2, h * QK:(h + 1) * QK] for h in range(4 * g, 4 * g + 4)], QK)
                            flips((l, "KT", u, g), [k_rows[:, u % 2, h * QK:(h + 1) * QK] for h in range(4 * g, 4 * g + 4)], QK)
                for g in range(2):
                    wait_drained(pe, l, "QT", nt - 1, g)
                    wait_drained(pe, l, "KT", TILES - 1, g)
                m = len(units(l))
                for i in range(m + 3):
                    if i < m:
                        qt, h = units(l)[i]
                        lo, hi = keys_of(qt)
                        chain((l, "S", i), hi - lo, lambda k: q_T[0:QK, h, qt * P:(qt + 1) * P], lambda k: k_T[0:QK, h, lo:hi], 1)
                    if 2 <= i < m + 2:
                        lo, hi = keys_of(units(l)[i - 2][0])
                        pe.wait_ge(S["p_ready"], i - 1)
                        flips((l, "PT", i - 2), [p_rows[:, i % 2, k * P:(k + 1) * P] for k in range((hi - lo) // P)])
                    if i >= 3:
                        qt, h = units(l)[i - 3]
                        lo, hi = keys_of(qt)
                        wait_drained(pe, l, "PT", i - 3)
                        b = claim(l, "O", i - 3)
                        n = (hi - lo) // P
                        for k in range(n):
                            mm = pe.matmul(b[64 * (h % 2):64 * (h % 2) + 64, 0:P], v_rows[:, lo // P + k, h * V_DIM:(h + 1) * V_DIM],
                                           p_T[:, (i - 3) % 2, k * P:(k + 1) * P], start=(k == 0), stop=(k == n - 1))
                        mm.then_inc(psum_filled, 1)
                pe.wait_ge(S["w_out_in"], 16)
                wait_drained(pe, l, "O", m - 1)
                for t in range(nt):
                    for c in range(2):
                        chain((l, "OUT", t, c), 512, lambda k: mixed[:, k, t * P:(t + 1) * P], lambda k: w_out[:, k, 512 * c:512 * c + 512], DK)
                for t in range(nt):
                    pe.wait_ge(S["h2_ready"], t + 1)
                    for c in range(2):
                        flips((l, "T2", t, c), [h_rows[:, t, 4 * c + k:D:DK] for k in range(4)])
                pe.wait_ge(S["router_in"], 32)
                for t in range(nt):
                    wait_drained(pe, l, "T2", t, 0)
                    wait_drained(pe, l, "T2", t, 1)
                    chain((l, "R", t), EXPERTS, lambda k: h_T[:, k, t * P:(t + 1) * P], lambda k: w_router[:, k, :], DK)
                pe.wait_ge(S["shared_in"], 48)
                gu, dn = slot_gu(SHARED_SLOT), slot_dn(SHARED_SLOT)
                for t in range(nt + 1):
                    if t < nt:
                        b = claim(l, "SG", t)
                        for k in range(DK):
                            mm = pe.matmul(split(b[:, :], (2, FE)), h_T[:, k, t * P:(t + 1) * P], gu[:, :, k, :], start=(k == 0), stop=(k == DK - 1))
                        mm.then_inc(psum_filled, 1)
                    if t >= 1:
                        u = t - 1
                        wait_drained(pe, l, "SG", u)
                        flips((l, "SH", u), [hid[:, u % 2, j:FE:2] for j in range(2)])
                        wait_drained(pe, l, "SH", u)
                        for c in range(2):
                            chain((l, "SD", u, c), 512, lambda k: hid_T[:, u % 2, k, :], lambda k: dn[:, k, 512 * c:512 * c + 512], 2)
                pe.wait_ge(S["chosen_ready"], 1)
                b = claim(l, "MT")
                for t in range(nt):
                    mm = pe.transpose(b[0:64, t * P:(t + 1) * P], chosen[:, t, :], ident[:, :])
                mm.then_inc(psum_filled, 1)
                wait_drained(pe, l, "MT")
                b = claim(l, "RANK")
                for t in range(nt):
                    mm = pe.matmul(b[:, t * EXPERTS:(t + 1) * EXPERTS], ranks_T[0:64, t, :], strict[0:64, 0:64], start=True, stop=True)
                mm.then_inc(psum_filled, 1)
                b = claim(l, "POS")
                for t in range(nt):
                    for q in range(t + 1):
                        pe.matmul(b[:, t * EXPERTS:(t + 1) * EXPERTS], strict[:, :] if q == t else ones[:, :], chosen[:, q, :],
                                  start=(q == 0), stop=(q == t))
                for q in range(nt):
                    mm = pe.matmul(b[0:64, TILES * EXPERTS:TILES * EXPERTS + 1], chosen[:, q, :], ones[:, 0:1], start=(q == 0), stop=(q == nt - 1))
                mm.then_inc(psum_filled, 1)
                wait_drained(pe, l, "POS")
                b = claim(l, "ENDS")
                pe.matmul(b[:, 0:P], ext_b, ends_rhs[:, :], start=True, stop=True).then_inc(psum_filled, 1)

                def make_list(i, e, s):
                    pe.wait_ge(S["g_ready"], i + 1)
                    ge(pe, S["idx_ready"], i)
                    for t in range(nt):
                        mm = pe.matmul(banks[5][:, 0:3], one_hot[:, s % 2, t, :], vals[:, t, bass.ds(e, 1), :].rearrange("p a n -> p (a n)"),
                                       start=(t == 0), stop=(t == nt - 1))
                    mm.then_inc(S["list_filled"], 1)

                pe.wait_ge(S["table_ready"], 1)
                b = claim(l, "EXTRA")
                for c in range(3):
                    mm = pe.matmul(b[0:1, c * MAX_EXTRA:(c + 1) * MAX_EXTRA], table[0:MAX_EXTRA, c:c + 1], ident[0:MAX_EXTRA, 0:MAX_EXTRA], start=True, stop=True)
                mm.then_inc(psum_filled, 1)
                wait_drained(pe, l, "EXTRA")
                for i in range(AHEAD):
                    make_list(i, i, i)

                def flip_rows(i, j, s):
                    pe.wait_ge(S["gathered"][s % 4], ((UNROLL // 4) * j + s // 4 + 1) * 16)
                    ge(pe, S["xt_act"], i)
                    ge(pe, S["xt_dve"], i)
                    for k in range(DK):
                        mm = pe.transpose(banks[k // 4][:, (k % 4) * P:(k % 4 + 1) * P], x_g[:, s % 4, k:D:DK], ident[:, :])
                    mm.then_inc(S["xt_filled"], 1)

                def up(gu, x, bank):
                    for k in range(DK):
                        mm = pe.matmul(split(bank[:, :], (2, FE)), x_gT[:, x, k, :], gu[:, :, k, :], start=(k == 0), stop=(k == DK - 1))
                    return mm

                def down(dn, x):
                    for c in range(2):
                        for k in range(2):
                            mm = pe.matmul(banks[6 + c][:, :], hid_T[:, x, k, :], dn[:, k, 512 * c:512 * c + 512], start=(k == 0), stop=(k == 1))
                    return mm

                def flip_hid(x):
                    for k in range(2):
                        mm = pe.transpose(banks[4][:, k * P:(k + 1) * P], hid[:, x, k:FE:2], ident[:, :])
                    return mm

                def down_step(i, j, s):
                    w = expert_slot(s)
                    pe.wait_ge(S["dn_in"][w], ((UNROLL // 4) * j + s // 4 + 1) * 16)
                    pe.wait_ge(S["ht_drained"], i + 1)
                    ge(pe, S["y_act"], i)
                    ge(pe, S["y_dve"], i)
                    down(slot_dn(w), s % 2).then_inc(S["d_filled"], 1)

                flip_rows(0, 0, 0)

                def step(j, s):
                    i = j * UNROLL + s
                    flip_rows(i + 1, j, s + 1)
                    w = expert_slot(s)
                    pe.wait_ge(S["gu_in"][w], ((UNROLL // 4) * j + s // 4 + 1) * 32)
                    ge(pe, S["hid_ready"], i - 1)
                    up(slot_gu(w), s % 2, banks[2 + s % 2]).then_inc(S["gu_filled"], 1)
                    make_list(i + AHEAD, i + AHEAD, s)
                    if not (isinstance(i, int) and i == 0):
                        down_step(i - 1, j, s - 1)
                    pe.wait_ge(S["hid_ready"], i + 1)
                    ge(pe, S["ht_drained"], i)
                    flip_hid(s % 2).then_inc(S["ht_filled"], 1)

                for s in range(UNROLL):
                    step(0, s)
                with pe.Fori(1, EXPERTS // UNROLL) as j:
                    for s in range(UNROLL):
                        step(j, s)
                down_step(EXPERTS - 1, EXPERTS // UNROLL - 1, UNROLL - 1)

                n_extra = pe.value_load(extra_row[0:1, 0:1], min_val=0, max_val=MAX_EXTRA)
                pe.wait_ge(S["xt_act"], EXPERTS + 1)
                pe.wait_ge(S["xt_dve"], EXPERTS + 1)
                pe.wait_ge(S["y_act"], EXPERTS)
                pe.wait_ge(S["y_dve"], EXPERTS)
                pe.wait_ge(S["idx_ready"], LISTED)
                with pe.If(n_extra > 0):
                    with pe.Fori(0, n_extra) as o:
                        pe.wait_ge(S["g_ready"], o + 1 + LISTED)
                        e = pe.value_load(extra_row[0:1, bass.ds(o + MAX_EXTRA, 1)], min_val=0, max_val=EXPERTS - 1)
                        for t in range(nt):
                            mm = pe.matmul(banks[5][:, 0:3], one_hot[:, 0, t, :], vals[:, t, bass.ds(e, 1), :].rearrange("p a n -> p (a n)"),
                                           start=(t == 0), stop=(t == nt - 1))
                        mm.then_inc(S["list_filled"], 1)
                        pe.wait_ge(S["e_x"], o * 32 + 16)
                        for k in range(DK):
                            mm = pe.transpose(banks[k // 4][:, (k % 4) * P:(k % 4 + 1) * P], x_g[:, 0, k:D:DK], ident[:, :])
                        mm.then_inc(S["xt_filled"], 1)
                        pe.wait_ge(S["e_w"], (o + 1) * 48)
                        pe.wait_ge(S["xt_act"], o + 1 + EXPERTS + 1)
                        pe.wait_ge(S["xt_dve"], o + 1 + EXPERTS + 1)
                        up(slot_gu(EXTRA_SLOT), 0, banks[2]).then_inc(S["gu_filled"], 1)
                        pe.wait_ge(S["hid_ready"], o + 1 + EXPERTS)
                        flip_hid(0).then_inc(S["ht_filled"], 1)
                        pe.wait_ge(S["ht_drained"], o + 1 + EXPERTS)
                        pe.wait_ge(S["y_act"], o + EXPERTS)
                        pe.wait_ge(S["y_dve"], o + EXPERTS)
                        down(slot_dn(EXTRA_SLOT), 0).then_inc(S["d_filled"], 1)
                pe.wait_ge(S["y_act"], n_extra + EXPERTS)
                pe.wait_ge(S["y_dve"], n_extra + EXPERTS)


def shape_constants():
    f = np.float32
    pos = np.arange(SEQ)
    pool = np.zeros((4, SEQ, SEQ), np.float64)
    for g, w in enumerate(POOL_WINDOWS):
        for t in range(SEQ):
            lo, hi = max(t - w // 2, 0), min(t + w // 2, SEQ)
            pool[g, t, lo:hi] = 1.0 / (hi - lo)
            pool[g, t, t] -= 1.0
    ang_l = 2 * np.pi * ((pos[:, None] * pos[None, :]) % SEQ) / SEQ
    ch = np.arange(GROUP)
    ang_c = 2 * np.pi * ((ch[:, None] * ch[None, :]) % GROUP) / GROUP
    norm = 1.0 / np.sqrt(SEQ * GROUP)
    dft_l = np.concatenate([np.cos(ang_l), np.sin(ang_l)], axis=1)
    dft_c = np.zeros((P, 2, P))
    for g in range(2):
        dft_c[g * 64:g * 64 + 64, 0, g * 64:g * 64 + 64] = np.cos(ang_c) * norm
        dft_c[g * 64:g * 64 + 64, 1, g * 64:g * 64 + 64] = -np.sin(ang_c) * norm
    inv = f(ROPE_THETA) ** (-np.arange(ROPE_FREQS, dtype=f) * f(2.0) / f(2 * ROPE_FREQS))
    ang = np.stack([(pos // GRID_W).astype(f)[:, None] * inv, (pos % GRID_W).astype(f)[:, None] * inv], axis=1).reshape(SEQ, 16)
    rope = np.stack([np.cos(ang), np.sin(ang)], axis=1).reshape(2, P, 2, 16).transpose(1, 0, 2, 3)
    strict = np.triu(np.ones((P, P)), 1)
    lane = np.arange(P)
    tok = lane[:, None] + P * np.arange(TILES)[None, :]
    grp = np.arange(8)
    out = {
        "k_ident": np.eye(P),
        "k_strict": strict,
        "k_iota": np.tile(np.arange(TOKENS), (P, 1)),
        "k_ends": np.concatenate([np.triu(np.ones((64, 64))), np.eye(64)], axis=1),
        "k_token": np.concatenate([tok - SKIP, TOP_K * tok - SKIP], axis=1),
        "k_lane": lane[:, None],
        "k_tie": np.tile((grp[None, :] < grp[:, None]).reshape(1, 64), (P, 1)),
        "k_rope": rope,
        "k_pool": pool.transpose(2, 0, 1).reshape(2, P, 4, SEQ).transpose(1, 0, 2, 3),
        "k_dft_l": dft_l.reshape(2, P, 2 * SEQ).transpose(1, 0, 2),
        "k_dft_c": dft_c,
    }
    return {k: np.ascontiguousarray(v.astype(f)) for k, v in out.items()}


def kernel(**inputs):
    import concourse.bacc as bacc
    from concourse.bass_utils import run_bass_kernel_spmd

    nc = bacc.Bacc("TRN2", target_bir_lowering=False, num_devices=1)
    arrays = {k: np.ascontiguousarray(v) for k, v in inputs.items()}
    arrays.update(shape_constants())
    aps = {k: nc.dram_tensor(f"in_{k}", v.shape, mybir.dt.from_np(v.dtype), kind="ExternalInput").ap() for k, v in arrays.items()}
    out = nc.dram_tensor("out", (1, SEQ, D), F32, kind="ExternalOutput").ap()
    build(nc, aps, out)
    r = run_bass_kernel_spmd(nc, [{f"in_{k}": v for k, v in arrays.items()}], core_ids=[0])
    return r.results[0]["out"]
```

```python
from contextlib import ExitStack

import numpy as np

import concourse.bass as bass
from concourse import mybir

F32 = mybir.dt.float32
F32R = mybir.dt.float32r
I32 = mybir.dt.int32
U32 = mybir.dt.uint32
ALU = mybir.AluOpType
ACT = mybir.ActivationFunctionType
AX = mybir.AxisListType

P = 128
BANKS = 8
BANK = 512
LIST_BANK = 5

D = 1024
DK = D // P
SEQ = 256
CTX = 256
DEPTH = 2
EPS = 1e-6
TILES = (SEQ + CTX) // P
LATENT_TILES = SEQ // P
STREAM_TILES = 2
TOKENS = TILES * P

GROUP = 64
POOL_WINDOWS = (2, 4, 8, 16)
COL_FNO = 256
COL_Q = 512
Q_LORA = 384
KV_LORA = 256
COL_KV = COL_Q + Q_LORA
COL_KR = COL_KV + KV_LORA
IN_WIDTH = COL_KR + 32
HEADS = 8
NOPE = 64
ROPE = 32
QK = NOPE + ROPE
V_DIM = 64
SCALE = QK ** -0.5
GRID_W = 64
ROPE_FREQS = 8
ROPE_THETA = 10000.0

EXPERTS = 64
TOP_K = 8
EGROUPS = 8
TOP_GROUPS = 4
FE = 256
ROUTED_SCALE = 2.5
AHEAD = 4
LISTED = EXPERTS + AHEAD
UNROLL = 8
SKIP = 65536
MAX_EXTRA = 64

MOD_N = 512
MOD_CHUNKS = 6 * D // MOD_N
MOD_SLOTS = 4
PIECES = 4
PIECE_K = DK // PIECES
W_IN_HEAD = 2 * DK * MOD_N // IN_WIDTH

SLOT = 6144
GU_W = 2 * DK * FE
QTR = D // 4
ARENA = 15488
PARTS_AT = 10816
POOL_QTRS = (3,)


def active_tiles(layer):
    return TILES if layer < DEPTH - 1 else LATENT_TILES


def u_chunks(layer, t):
    if t < active_tiles(layer):
        return [(0, 512), (512, 1024), (1024, IN_WIDTH)]
    return [(COL_KV, IN_WIDTH)]


def list_rows(layer):
    return P if active_tiles(layer) == TILES else 96


def units(layer):
    return [(qt, h) for qt in range(active_tiles(layer)) for h in range(HEADS)]


def keys_of(qt):
    return (0, TOKENS) if qt < LATENT_TILES else (SEQ, TOKENS)


def in_steps(layer):
    steps = [("NORM", 0), ("T1", 0)]
    for t in range(TILES):
        chunks = [("U", t, c) for c in range(len(u_chunks(layer, t)))]
        if t + 1 < TILES:
            chunks.insert(1, ("NORM", t + 1))
            chunks.insert(len(chunks) if len(chunks) < 4 else len(chunks) - 1, ("T1", t + 1))
        steps += chunks
    return steps


def head_steps(layer):
    nt = active_tiles(layer)
    steps = [("OUT", 0)]
    for t in range(1, nt):
        steps += [("OUT", t), ("T2", t - 1)]
    return steps + [("R", t) for t in range(nt - 1)] + [("T2", nt - 1), ("R", nt - 1)]


def tail_steps(layer):
    if active_tiles(layer) == 4:
        return [("SG", 0), ("SG", 1), ("MT",), ("SD", 0), ("PLACES",), ("SG", 2), ("ENDS",), ("SD", 1), ("EXTRA",),
                ("SG", 3), ("LIST", 0), ("SD", 2), ("LIST", 1), ("SD", 3), ("LIST", 2), ("LIST", 3)]
    return [("SG", 0), ("SG", 1), ("MT",), ("SD", 0), ("PLACES",), ("ENDS",), ("EXTRA",), ("LIST", 0), ("LIST", 1),
            ("SD", 1), ("LIST", 2), ("LIST", 3)]


def plan_jobs():
    jobs = []

    def add(eng, *key):
        jobs.append((key, eng))

    for l in range(DEPTH):
        nt = active_tiles(l)
        for step in in_steps(l):
            if step[0] == "T1":
                add("act", l, *step, 0)
                add("act", l, *step, 1)
            elif step[0] == "U":
                add("act", l, *step)
        for s in range(nt // STREAM_TILES):
            for c in range(2):
                add("act", l, "POOLED", s, c)
            for c in range(2):
                add("dve", l, "DFT_POS", s, c)
            for c in range(2):
                add("dve", l, "POOL_OUT", s, c)
            for c in range(2):
                add("act", l, "DFT_CH", s, c)
            for c in range(2):
                add("act", l, "FNO_OUT", s, c)
        for t in range(TILES):
            if t < nt:
                add("act", l, "CQ", t)
            add("dve", l, "CKV", t)
        for t in range(TILES + 1):
            if t < TILES:
                if t < nt:
                    add("act", l, "Q", t, 0)
                    add("dve", l, "Q", t, 1)
                add("act", l, "KV", t, 0)
                add("dve", l, "KV", t, 1)
            if t >= 1:
                for g in range(2):
                    if t - 1 < nt:
                        add("act", l, "QT", t - 1, g)
                    add("dve", l, "KT", t - 1, g)
        m = len(units(l))
        for i in range(m + 3):
            if i < m:
                add("act", l, "S", i)
            if 2 <= i < m + 2:
                add("act", l, "PT", i - 2)
            if 3 <= i:
                add("dve", l, "O", i - 3)
        for name, t in head_steps(l):
            if name == "OUT":
                add("dve", l, "OUT", t, 0)
                add("dve", l, "OUT", t, 1)
            elif name == "T2":
                add("act", l, "T2", t, 0)
                add("dve", l, "T2", t, 1)
            else:
                add("act", l, "R", t)
        for step in tail_steps(l):
            if step[0] == "SD":
                add("act", l, "SH", step[1])
                add("dve", l, "SD", step[1], 0)
                add("dve", l, "SD", step[1], 1)
            elif step[0] == "PLACES":
                add("dve", l, "RANK")
                add("dve", l, "POS")
            elif step[0] != "LIST":
                add("dve", l, *step)
    return jobs


class Jobs:

    def __init__(self):
        self.number, self.by, self.nth, self.banks, self.last = {}, {}, {}, {}, {}
        count = {"act": 0, "dve": 0}
        in_bank = [None] * BANKS
        bank = 0
        for n, (key, eng) in enumerate(plan_jobs()):
            count[eng] += 1
            self.number[key], self.by[key], self.nth[key] = n, eng, count[eng]
            if (key[0], "EXTRA") in self.number and bank == LIST_BANK:
                bank += 1
            self.banks[key], self.last[key] = bank, in_bank[bank]
            in_bank[bank] = key
            bank = (bank + 1) % BANKS

    def bank(self, *key):
        return self.banks[key]

    def filled(self, *key):
        return self.number[key] + 1

    def before(self, *key):
        return self.last[key]


def build(nc, a, out):
    jobs = Jobs()
    with ExitStack() as ctx:
        def sb(name, shape, dt=F32):
            return ctx.enter_context(nc.sbuf_tensor(name, shape, dt))

        def sem(name):
            return ctx.enter_context(nc.semaphore(name))

        banks = [ctx.enter_context(nc.psum_tensor(f"bank{i}", [P, BANK], F32)) for i in range(BANKS)]

        mod_rows_d = nc.dram_tensor("mod_rows_d", [DEPTH, 2, 6 * D], F32, kind="Internal").ap()
        h2_d = [nc.dram_tensor(f"h2_d{l}", [active_tiles(l) * P, D], F32, kind="Internal").ap() for l in range(DEPTH)]
        expert_rows = [nc.dram_tensor(f"expert_rows{l}", [active_tiles(l) * P * TOP_K, D], F32, kind="Internal").ap() for l in range(DEPTH)]

        x_rows = sb("x_rows", [P, TILES, D])
        mods = sb("mods", [P, 2, 3, D])
        ident = sb("ident", [P, P])
        strict = sb("strict", [P, P])
        ones = sb("ones", [P, P])
        slots_iota = sb("slots_iota", [P, TOKENS])
        ends_rhs = sb("ends_rhs", [64, 128])
        token_cols = sb("token_cols", [P, 8])
        lane = sb("lane", [P, 1])
        tie = sb("tie", [P, 64])
        rope_tab = sb("rope_tab", [P, 2, 2, 16])
        g_lora = sb("g_lora", [P, Q_LORA + KV_LORA])
        w_router = sb("w_router", [P, DK, EXPERTS])
        r_bias = sb("r_bias", [P, EXPERTS])
        pool_scale = sb("pool_scale", [P, 2])
        cond = sb("cond", [P, 2, DK])
        cond_silu = sb("cond_silu", [P, DK, 2])
        stats = sb("stats", [P, 4, 8])
        newton = sb("newton", [P, 8])
        soft = sb("soft", [P, 3, 32])
        row_idx = sb("row_idx", [P, UNROLL, 2], U32)
        row_w = sb("row_w", [P, UNROLL])
        extra_row = sb("extra_row", [1, 3 * MAX_EXTRA], I32)

        cond_hi = sb("cond_hi", [P, DK, 2], F32R)
        cond_lo = sb("cond_lo", [P, DK, 2], F32R)

        with ExitStack() as early:
            mod_w = early.enter_context(nc.sbuf_tensor("mod_w", [P, MOD_SLOTS, DK, MOD_N], F32))
            mod_w_hi = early.enter_context(nc.sbuf_tensor("mod_w_hi", [P, PIECES, PIECE_K, MOD_N], F32R))
            mod_w_lo = early.enter_context(nc.sbuf_tensor("mod_w_lo", [P, PIECES, PIECE_K, MOD_N], F32R))
        ring = sb("ring", [P, 4 * SLOT])
        with ExitStack() as early:
            early.enter_context(nc.sbuf_tensor("before_parts", [P, PARTS_AT], F32))
            dn_hi = early.enter_context(nc.sbuf_tensor("dn_hi", [P, 2, D], F32R))
            dn_lo = early.enter_context(nc.sbuf_tensor("dn_lo", [P, 2, D], F32R))
            hid_hi = early.enter_context(nc.sbuf_tensor("hid_hi", [P, 2, P], F32R))
            hid_lo = early.enter_context(nc.sbuf_tensor("hid_lo", [P, 2, P], F32R))
        arena = sb("arena", [P, ARENA])

        def view(lo, n, *shape):
            v = arena[:, lo:lo + n]
            return split(v, shape)

        def split(v, shape):
            if len(shape) == 1:
                return v
            if len(shape) == 2:
                return v.rearrange("p (a b) -> p a b", b=shape[1])
            return v.rearrange("p (a b c) -> p a b c", b=shape[1], c=shape[2])

        A, B, U, C = 0, 4096, 8192, 12928
        mod_rows = [arena[0:2, U * l:U * l + 6 * D] for l in range(DEPTH)]
        gain_rows = arena[0:2, 6 * D:8 * D]
        first_squares = view(14 * D, D, D)
        h_rows = view(A, 4096, TILES, D)
        mixed = view(A, 4096, DK, TOKENS)
        pooled = view(A + 2048, 512, 2, SEQ)
        dft_pos = view(A + 2560, 1024, 2, 2 * SEQ)
        dft_ch = view(A + 3584, 512, 2, SEQ)
        h_T = view(B, 4096, DK, TOKENS)
        q_rows = view(B, 1536, 2, HEADS * QK)
        k_rows = view(B + 1536, 1536, 2, HEADS * QK)
        lora_squares = h_rows
        rope_tmp = view(B + 3584, 512, 4, 128)
        u_rows = view(U, TILES * IN_WIDTH, TILES, IN_WIDTH)
        p_rows = view(U, 1024, 2, 512)
        p_T = view(U + 1024, 1024, 2, 512)
        res_tmp = view(U + 2048, 1024, 2, 512)
        res_squares = view(U, D, D)
        c_T = view(C, 2560, 5, TOKENS)
        x_g = view(A, 4096, 4, D)
        x_gT = view(B, 2048, 2, DK, P)
        y_g = view(B + 2048, 2048, 2, D)
        one_hot = view(U, 1024, 2, TILES, P)
        vals = view(U + 1024, TILES * LISTED * 3, TILES, LISTED, 3)
        posm = view(U + 1840, TILES * LISTED, TILES, LISTED)
        hid = view(U + 2112, 512, 2, FE)
        sig = view(U + 2624, 512, 2, FE)
        hid_T = view(U + 3136, 512, 2, 2, P)
        hid_x = view(U + 2112, FE, FE)
        sig_x = view(U + 2368, FE, FE)
        hid_T_x = view(U + 2624, 2 * P, 2, P)
        moe_tmp = view(U + 3648, 1024, 2, 512)
        y_sum = view(C + 2048, QTR, QTR)
        prob = view(C, 256, TILES, EXPERTS)
        sel = view(C + 256, 256, TILES, EXPERTS)
        top2 = view(C + 512, 256, TILES, EGROUPS, 8)
        cmp_a = view(C + 768, 256, TILES, EGROUPS, 8)
        cmp_b = view(C + 1024, 256, TILES, EGROUPS, 8)
        chosen = view(C + 1280, 256, TILES, EXPERTS)
        small = view(C + 1536, 256, 256)
        ranks_T = view(C + 1792, 512, TILES, P)
        gscore = split(small[:, 0:32], (TILES, 8))
        gmask = split(small[:, 32:64], (TILES, 8))
        gneg = split(small[:, 64:96], (TILES, 8))
        top8 = split(small[:, 96:128], (TILES, 8))
        wsum = small[:, 128:132]
        winv = small[:, 132:136]
        ext = small[:, 136:138]
        ext_b = top2.rearrange("p a b c -> p (a b c)")[0:64, 0:128]
        ends = cmp_a.rearrange("p a b c -> p (a b c)")
        table = small[:, 138:141]

        w_in = ring[:, 0:DK * IN_WIDTH].rearrange("p (k n) -> p k n", k=DK)
        w_out = ring[:, 0:8192].rearrange("p (k n) -> p k n", k=DK)
        k_T = ring[:, 8192:12288].rearrange("p (h n) -> p h n", h=HEADS)
        pool_m = ring[:, 9728:11776].rearrange("p (t g n) -> p t g n", t=2, g=4)
        w_uq = ring[:, 12288:12288 + 2304].rearrange("p (k n) -> p k n", k=3)
        w_ukv = ring[:, 14592:14592 + 2048].rearrange("p (k n) -> p k n", k=2)
        dft_l = ring[:, 16640:16640 + 1024].rearrange("p (t n) -> p t n", t=2)
        dft_c = ring[:, 17664:17664 + 256].rearrange("p (t n) -> p t n", t=2)
        w_pool_g = ring[:, 17920:18048].rearrange("p (c n) -> p c n", c=2)
        w_fno_g = ring[:, 18048:18176].rearrange("p (c n) -> p c n", c=2)
        h2_rows = ring[:, 8192:12288].rearrange("p (t n) -> p t n", t=TILES)
        q_T = ring[:, 18432:18432 + 4096].rearrange("p (h n) -> p h n", h=HEADS)
        v_rows = ring[:, 22528:22528 + 2048].rearrange("p (t n) -> p t n", t=TILES)
        y_quarter = [split(v, (TOP_K, QTR)) for v in (
            ring[:, 18432:20480], ring[:, 20480:22528], ring[:, 22528:24576], arena[:, C:C + 2048])]

        def slot_gu(s):
            return ring[:, s * SLOT:s * SLOT + GU_W].rearrange("p (g k f) -> p g k f", g=2, k=DK)

        def slot_dn(s):
            return ring[:, s * SLOT + GU_W:(s + 1) * SLOT].rearrange("p (j n) -> p j n", j=2)

        def expert_slot(i):
            return (i + 3) % 4

        SHARED_SLOT = 2
        EXTRA_SLOT = 3

        psum_filled = sem("psum_filled")
        drained = {"act": sem("drained_by_act"), "dve": sem("drained_by_dve")}
        dve_link = sem("dve_link")
        act_link = sem("act_link")
        pool_link = sem("pool_link")
        const_in = sem("const_in")
        cond_in = sem("cond_in")
        cond_sig = sem("cond_sig")
        cond_ready = sem("cond_ready")
        x_in = sem("x_in")
        ones_ready = sem("ones_ready")
        mod_w_in = [sem(f"mod_w_in{s}") for s in range(MOD_SLOTS)]
        mod_bias_in = sem("mod_bias_in")
        mod_hi = sem("mod_hi")
        mod_lo = sem("mod_lo")
        mod_filled = sem("mod_filled")
        mod_added = sem("mod_added")
        mod_ready = sem("mod_ready")
        mod_stored = sem("mod_stored")
        out_stored = sem("out_stored")
        row_moves = sem("row_moves")

        def layer_sems(l):
            named = {name: sem(f"{name}_{l}") for name in (
                "mods_in", "w_in_in", "w_lora_in", "mixer_in", "w_out_in", "router_in", "norm_sums",
                "norm_var", "norm_root", "h_ready", "lora_ready",
                "q_rotated", "k_ready", "row_max", "p_ready", "x_mixed", 
                "h2_ready", "h2_stored", "shared_in", "shared_sig", "chosen_ready",
                "table_ready", "extra_ready", "g_ready", "list_filled", "idx_ready", "xt_filled", "xt_drained",
                "gu_filled", "sig_ready", "hid_ready", "dn_hi", "dn_lo", "hid_hi", "ht_filled", "ht_drained",
                "d_filled", "y_ready", "e_w", "e_x", "rows_back", "last_gain_in", "x_done", "x_done_pool", "gate_in", "out_ready",
            )}
            many = {name: [sem(f"{name}{s}_{l}") for s in range(n)]
                    for name, n in (("gu_in", 4), ("dn_in", 4), ("gathered", 4), ("scattered", 2), ("y_in", 4))}
            return {**named, **many}

        L = [layer_sems(l) for l in range(DEPTH)]

        def ge(eng, s, value):
            if not (isinstance(value, int) and value <= 0):
                eng.wait_ge(s, value)

        def wait_drained(eng, *key):
            eng.wait_ge(drained[jobs.by[key]], jobs.nth[key])

        def wait_filled(eng, *key):
            eng.wait_ge(psum_filled, jobs.filled(*key))

        def bank_of(*key):
            return banks[jobs.bank(*key)]

        def load_w_in(eng, l, lo, hi):
            eng.dma_start(w_in[:, lo:hi], a["w_in"][l].rearrange("(k p) n -> p k n", p=P)[:, lo:hi]).then_inc(L[l]["w_in_in"], 16)

        def load_mixer_weights(eng, l):
            S = L[l]
            eng.dma_start(pool_m, a["k_pool"]).then_inc(S["mixer_in"], 16)
            eng.dma_start(dft_l, a["k_dft_l"]).then_inc(S["mixer_in"], 16)
            eng.dma_start(dft_c, a["k_dft_c"]).then_inc(S["mixer_in"], 16)
            eng.dma_start(pool_scale[:, :], a["pool_scale"][l].rearrange("(c p) -> p c", p=P),
                          allow_slow_non_contiguous=True).then_inc(S["mixer_in"], 16)
            eng.dma_start(w_pool_g, a["w_pool"][l].rearrange("(c b) i o -> (b i) c o", b=2)).then_inc(S["mixer_in"], 16)
            eng.dma_start(w_fno_g, a["w_fno"][l].rearrange("(c b) i o -> (b i) c o", b=2)).then_inc(S["mixer_in"], 16)
            eng.dma_start(w_uq, a["w_uq"][l].rearrange("(k p) n -> p k n", p=P)).then_inc(S["w_lora_in"], 16)
            eng.dma_start(w_ukv, a["w_ukv"][l].rearrange("(k p) n -> p k n", p=P)).then_inc(S["w_lora_in"], 16)
            eng.dma_start(g_lora[:, 0:Q_LORA], a["g_q"][l].partition_broadcast(P)).then_inc(S["w_lora_in"], 16)
            eng.dma_start(g_lora[:, Q_LORA:], a["g_kv"][l].partition_broadcast(P)).then_inc(S["w_lora_in"], 16)
            eng.dma_start(w_router[:, :, :], a["w_router"][l].rearrange("(p k) n -> p k n", k=DK)).then_inc(S["router_in"], 16)
            eng.dma_start(r_bias[:, :], a["router_bias"][l].partition_broadcast(P)).then_inc(S["router_in"], 16)

        block = ctx.enter_context(nc.Block())

        @block.sync
        def _(sp):
            sp.dma_start(cond[:, 0, :], a["c"].rearrange("a (p k) -> (a p) k", k=DK)).then_inc(cond_in, 16)
            sp.dma_start(cond[:, 1, :], a["c_ctx"].rearrange("(p k) -> p k", k=DK)).then_inc(cond_in, 16)
            for l in range(DEPTH):
                wm = a["w_mod"][l].rearrange("(p k) n -> p k n", k=DK)
                if l == 0:
                    for s in range(MOD_SLOTS):
                        sp.dma_start(mod_w[:, s], wm[:, :, s * MOD_N:(s + 1) * MOD_N]).then_inc(mod_w_in[s], 16)
                    first = 1
                else:
                    first = 0
                with sp.Fori(first, MOD_CHUNKS // MOD_SLOTS) as j:
                    for s in range(MOD_SLOTS):
                        sp.wait_ge(mod_lo, PIECES * (l * MOD_CHUNKS + j * MOD_SLOTS + s + 1 - MOD_SLOTS))
                        sp.dma_start(mod_w[:, s], wm[:, :, bass.ds((j * MOD_SLOTS + s) * MOD_N, MOD_N)]).then_inc(mod_w_in[s], 16)
            for dst, name in ((ident, "k_ident"), (strict, "k_strict"), (slots_iota, "k_iota"), (ends_rhs, "k_ends"),
                              (token_cols, "k_token"), (lane, "k_lane"), (tie, "k_tie")):
                sp.dma_start(dst[:, :], a[name]).then_inc(const_in, 16)
            sp.dma_start(rope_tab[:, :, :, :], a["k_rope"]).then_inc(const_in, 16)
            sp.dma_start(x_rows[:, 0:2, :], a["x"].rearrange("a (t p) n -> p (a t) n", p=P)).then_inc(x_in, 16)
            sp.dma_start(x_rows[:, 2:4, :], a["ctx"].rearrange("a (t p) n -> p (a t) n", p=P)).then_inc(x_in, 16)

            for l in range(DEPTH):
                S = L[l]
                nt = active_tiles(l)
                if l == 0:
                    sp.wait_ge(mod_lo, PIECES * (DEPTH * MOD_CHUNKS - 2))
                    load_w_in(sp, l, 0, W_IN_HEAD)
                    sp.wait_ge(mod_lo, PIECES * (DEPTH * MOD_CHUNKS - 1))
                    load_w_in(sp, l, W_IN_HEAD, DK)
                    sp.wait_ge(mod_filled, PIECES * DEPTH * MOD_CHUNKS)
                    sp.wait_ge(mod_stored, 16 * DEPTH)
                    load_mixer_weights(sp, l)
                wait_filled(sp, l, "U", TILES - 1, len(u_chunks(l, TILES - 1)) - 1)
                sp.dma_start(w_out, a["w_out"][l].rearrange("(k p) n -> p k n", p=P)).then_inc(S["w_out_in"], 16)
                wait_filled(sp, l, "KV", TILES - 1, 1)
                gu = slot_gu(SHARED_SLOT)
                sp.dma_start(gu[:, 0], a["w_sh_gate"][l].rearrange("(p k) f -> p k f", k=DK)).then_inc(S["shared_in"], 16)
                sp.dma_start(gu[:, 1], a["w_sh_up"][l].rearrange("(p k) f -> p k f", k=DK)).then_inc(S["shared_in"], 16)
                sp.dma_start(slot_dn(SHARED_SLOT), a["w_sh_down"][l].rearrange("(p j) n -> p j n", j=2)).then_inc(S["shared_in"], 16)

                def load_expert(e, s):
                    gu = slot_gu(s)
                    for g, name in enumerate(("w_gate", "w_up")):
                        w = a[name][l].rearrange("e (p k) f -> e p k f", k=DK)
                        sp.dma_start(gu[:, g], w[bass.ds(e, 1)].rearrange("a p k f -> p (a k) f")).then_inc(S["gu_in"][s], 16)
                    w = a["w_down"][l].rearrange("e (p j) n -> e p j n", j=2)
                    sp.dma_start(slot_dn(s), w[bass.ds(e, 1)].rearrange("a p j n -> p (a j) n")).then_inc(S["dn_in"][s], 16)

                wait_filled(sp, l, "O", len(units(l)) - 1)
                load_expert(0, expert_slot(0))
                wait_filled(sp, l, "OUT", nt - 1, 1)
                load_expert(1, expert_slot(1))
                wait_filled(sp, l, "T2", nt - 1, 1)
                sp.wait_ge(S["h2_stored"], 16 * nt)
                load_expert(2, expert_slot(2))
                wait_filled(sp, l, "SD", nt - 1, 1)
                load_expert(3, expert_slot(3))
                with sp.Fori(1, EXPERTS // 4) as j:
                    for s in range(4):
                        sp.wait_ge(S["d_filled"], j * 4 + s - 3)
                        load_expert(j * 4 + s, expert_slot(s))

                def load_block(o):
                    e = sp.value_load(extra_row[0:1, bass.ds(o + MAX_EXTRA, 1)], min_val=0, max_val=EXPERTS - 1)
                    gu = slot_gu(EXTRA_SLOT)
                    for g, name in enumerate(("w_gate", "w_up")):
                        w = a[name][l].rearrange("e (p k) f -> e p k f", k=DK)
                        sp.dma_start(gu[:, g], w[bass.ds(e, 1)].rearrange("a p k f -> p (a k) f")).then_inc(S["e_w"], 16)
                    w = a["w_down"][l].rearrange("e (p j) n -> e p j n", j=2)
                    sp.dma_start(slot_dn(EXTRA_SLOT), w[bass.ds(e, 1)].rearrange("a p j n -> p (a j) n")).then_inc(S["e_w"], 16)

                sp.wait_ge(S["extra_ready"], 1)
                n_extra = sp.value_load(extra_row[0:1, 0:1], min_val=0, max_val=MAX_EXTRA)
                sp.wait_ge(S["d_filled"], EXPERTS - 3)
                with sp.If(n_extra > 0):
                    load_block(0)
                with sp.If(n_extra > 1):
                    with sp.Fori(1, n_extra) as o:
                        sp.wait_ge(S["d_filled"], o + EXPERTS)
                        load_block(o)
                sp.wait_ge(S["rows_back"], 1)
                rows = expert_rows[l].rearrange("(t p k) n -> t p k n", p=P, k=TOP_K)
                for t in range(nt):
                    for q in POOL_QTRS + tuple(q for q in range(4) if q not in POOL_QTRS):
                        if t and q in POOL_QTRS:
                            sp.wait_ge(S["x_done_pool"], (t - 1) * len(POOL_QTRS) + POOL_QTRS.index(q) + 1)
                        elif t:
                            sp.wait_ge(S["x_done"], (t - 1) * (4 - len(POOL_QTRS)) + q + 1)
                        sp.dma_start(y_quarter[q], rows[t][:, :, q * QTR:(q + 1) * QTR]).then_inc(S["y_in"][q], 16)
            for t in range(LATENT_TILES):
                sp.wait_ge(L[DEPTH - 1]["out_ready"], t + 1)
                sp.dma_start(out.rearrange("a (t p) n -> p (a t) n", p=P)[:, t:t + 1], h_rows[:, t:t + 1, :]).then_inc(out_stored, 16)
            sp.wait_ge(out_stored, 16 * LATENT_TILES)

        @block.gpsimd
        def _(pool):
            link = [0]

            def pool_linked(ins):
                link[0] += 1
                ins.then_inc(pool_link, 1)
                pool.wait_ge(pool_link, link[0])

            def load_mods(l, first, n, at, streams, signal):
                for s in range(streams):
                    pool.dma_start(mods[:, s, at:at + n, :].rearrange("p a n -> p (a n)"),
                                   mod_rows_d[l, s, first * D:(first + n) * D].partition_broadcast(P)).then_inc(signal, 16)

            for l in range(DEPTH):
                pool.dma_start(mod_rows[l], a["b_mod"][l].partition_broadcast(2)).then_inc(mod_bias_in, 16)
            for l in range(DEPTH):
                pool.dma_start(gain_rows[:, 0:D], a["g_mix"][l].partition_broadcast(2)).then_inc(mod_bias_in, 16)
                pool.dma_start(gain_rows[:, D:], a["g_ffn"][l].partition_broadcast(2)).then_inc(mod_bias_in, 16)
                pool.wait_ge(mod_ready, l + 1)
                pool.dma_start(mod_rows_d[l], mod_rows[l]).then_inc(mod_stored, 16)
                pool.wait_ge(mod_stored, 16 * (l + 1))
                if l == 0:
                    load_mods(0, 0, 2, 0, 2, L[0]["mods_in"])
                    load_mods(0, 2, 1, 2, 2, L[0]["gate_in"])

            for l in range(DEPTH):
                S = L[l]
                nt = active_tiles(l)
                streams = nt // STREAM_TILES
                if l:
                    load_mods(l, 2, 1, 2, streams, S["gate_in"])
                pool.wait_ge(S["h_ready"], TILES)
                load_mods(l, 3, 2, 0, streams, S["mods_in"])
                if l == DEPTH - 1:
                    pool.dma_start(mods[:, 1, 0, :], a["g_final"].partition_broadcast(P)).then_inc(S["last_gain_in"], 16)
                for t in range(nt):
                    if t == nt - 1:
                        pool.wait_ge(S["x_mixed"], nt)
                        load_mods(l, 5, 1, 2, streams, S["gate_in"])
                    pool.wait_ge(S["h2_ready"], t + 1)
                    pool.dma_start(h2_d[l][t * P:(t + 1) * P, :], h2_rows[:, t, :]).then_inc(S["h2_stored"], 16)
                if l + 1 < DEPTH:
                    load_mods(l + 1, 0, 2, 0, 2, L[l + 1]["mods_in"])

                rows = list_rows(l)
                last_token = pool.to_reg(nt * P - 1)
                last_row = pool.to_reg(nt * P * TOP_K - 1)

                def gather(slot, idx):
                    pool.sem_inc(row_moves, 1)
                    return pool.indirect_dma_start(
                        out=x_g[0:rows, slot, :], out_offset=None, in_=h2_d[l],
                        in_offset=bass.IndirectOffsetOnAxis(ap=row_idx[0:rows, idx, 0:1], axis=0),
                        bounds_check=last_token, oob_is_err=False)

                def scatter(slot, idx):
                    pool.sem_inc(row_moves, 1)
                    return pool.indirect_dma_start(
                        out=expert_rows[l], out_offset=bass.IndirectOffsetOnAxis(ap=row_idx[0:rows, idx, 1:2], axis=0),
                        in_=y_g[0:rows, slot, :], in_offset=None,
                        bounds_check=last_row, oob_is_err=False)

                pool.wait_ge(S["h2_stored"], 16 * nt)
                wait_filled(pool, l, "T2", nt - 1, 1)
                for i in range(AHEAD):
                    pool.wait_ge(S["idx_ready"], i + 1)
                    gather(i % 4, i).then_inc(S["gathered"][i % 4], 16)

                def step(i, s):
                    pool.wait_ge(S["idx_ready"], i + AHEAD + 1)
                    pool.wait_ge(S["xt_filled"], i + 1)
                    gather(s % 4, (s + AHEAD) % UNROLL).then_inc(S["gathered"][s % 4], 16)
                    if not (isinstance(i, int) and i == 0):
                        pool.wait_ge(S["y_ready"], 2 * i)
                        scatter((s - 1) % 2, (s - 1) % UNROLL).then_inc(S["scattered"][(s - 1) % 2], 16)

                for s in range(UNROLL):
                    step(s, s)
                with pool.Fori(1, EXPERTS // UNROLL) as j:
                    for s in range(UNROLL):
                        step(j * UNROLL + s, s)
                def block_gather(o):
                    pool.wait_ge(S["idx_ready"], o + 1 + LISTED)
                    gather(0, 0).then_inc(S["e_x"], 16)

                def block_scatter(o):
                    pool.wait_ge(S["y_ready"], 2 * (o + 1 + EXPERTS))
                    scatter(0, 0).then_inc(S["e_x"], 16)

                pool.wait_ge(S["extra_ready"], 1)
                n_extra = pool.value_load(extra_row[0:1, 0:1], min_val=0, max_val=MAX_EXTRA)
                with pool.If(n_extra > 0):
                    block_gather(0)
                pool.wait_ge(S["y_ready"], 2 * EXPERTS)
                scatter(1, UNROLL - 1).then_inc(S["scattered"][1], 16)
                for s in range(4):
                    pool.wait_ge(S["gathered"][s], 16 * (LISTED // 4))
                with pool.If(n_extra > 0):
                    block_scatter(0)
                with pool.If(n_extra > 1):
                    with pool.Fori(1, n_extra) as o:
                        block_gather(o)
                        block_scatter(o)
                pool.wait_ge(S["gate_in"], 32 * streams)
                for t in range(nt):
                    for n, q in enumerate(POOL_QTRS):
                        pool.wait_ge(S["y_in"][q], 16 * (t + 1))
                        y = y_quarter[q]
                        for w in (4, 2, 1):
                            pool_linked(pool.tensor_tensor(y[:, 0:w], y[:, 0:w], y[:, w:2 * w], ALU.add))
                        cols = slice(q * QTR, (q + 1) * QTR)
                        pool_linked(pool.tensor_tensor(y[:, 0], y[:, 0], mods[:, t // 2, 2, cols], ALU.mult))
                        pool.tensor_tensor(x_rows[:, t, cols], x_rows[:, t, cols], y[:, 0], ALU.add).then_inc(S["x_done_pool"], 1)
                if l + 1 < DEPTH:
                    pool.wait_ge(S["x_done"], nt * (4 - len(POOL_QTRS)))

        @block.scalar
        def _(act):
            link = [0]

            def linked(ins):
                link[0] += 1
                ins.then_inc(act_link, 1)
                act.wait_ge(act_link, link[0])

            act.wait_ge(cond_in, 32)
            act.activation(cond_silu[:, :, :], cond[:, :, :].rearrange("p s k -> p k s"), ACT.Sigmoid).then_inc(cond_sig, 1)

            act.wait_ge(cond_ready, 1)
            act.activation(cond_hi[:, :, :], cond_silu[:, :, :], ACT.Copy).then_inc(cond_sig, 1)
            for l in range(DEPTH):
                def split_round(j):
                    for s in range(MOD_SLOTS):
                        act.wait_ge(mod_w_in[s], 16 * (j + 1 + l * (MOD_CHUNKS // MOD_SLOTS)))
                        for h in range(PIECES):
                            ge(act, mod_filled, PIECES * (l * MOD_CHUNKS + j * MOD_SLOTS + s - 1) + h + 1)
                            act.activation(mod_w_hi[:, h], mod_w[:, s, h * PIECE_K:(h + 1) * PIECE_K, :], ACT.Copy).then_inc(mod_hi, 1)

                split_round(0)
                with act.Fori(1, MOD_CHUNKS // MOD_SLOTS) as j:
                    split_round(j)

            def drain(key, out, func=ACT.Copy, **kw):
                wait_filled(act, *key)
                act.activation(out, kw.pop("in_"), func, **kw).then_inc(drained["act"], 1)

            def norm_tile(l, t):
                S = L[min(l, DEPTH - 1)]
                done = TILES + 2 + LATENT_TILES if l == DEPTH else 0
                if l:
                    act.wait_ge(L[l - 1]["x_done"], (t + 1) * (4 - len(POOL_QTRS)))
                    act.wait_ge(L[l - 1]["x_done_pool"], (t + 1) * len(POOL_QTRS))
                act.activation(h_rows[:, t, :] if l else first_squares, x_rows[:, t, :], ACT.Square,
                               accum_out=stats[:, 0, t:t + 1]).then_inc(S["norm_sums"], 1)
                act.wait_ge(S["norm_var"], done + t + 1)
                act.activation(stats[:, 2, t:t + 1], stats[:, 1, t:t + 1], ACT.Sqrt).then_inc(S["norm_root"], 1)

            for l in range(DEPTH):
                S = L[l]
                nt = active_tiles(l)
                rows = list_rows(l)

                def h2_squares(t):
                    act.wait_ge(S["x_mixed"], t + 1)
                    act.activation(res_squares, x_rows[:, t, :], ACT.Square, accum_out=stats[:, 0, t:t + 1]).then_inc(S["norm_sums"], 1)

                def h2_root(t):
                    act.wait_ge(S["norm_var"], TILES + 3 + t)
                    act.activation(stats[:, 2, t:t + 1], stats[:, 1, t:t + 1], ACT.Sqrt).then_inc(S["norm_root"], 1)

                if l == 0:
                    act.wait_ge(x_in, 32)
                for step in in_steps(l):
                    if step[0] == "NORM":
                        norm_tile(l, step[1])
                        if l and step[1] == TILES - 1:
                            load_mixer_weights(act, l)
                    elif step[0] == "T1":
                        t = step[1]
                        for c in range(2):
                            drain((l, "T1", t, c), h_T[:, 4 * c:4 * c + 4, t * P:(t + 1) * P], in_=split(bank_of(l, "T1", t, c)[:, :], (4, P)))
                    else:
                        _, t, c = step
                        if l == t == c == 0:
                            act.wait_ge(mod_stored, 16 * DEPTH)
                        lo, hi = u_chunks(l, t)[c]
                        drain((l, "U", t, c), u_rows[:, t, lo:hi], in_=bank_of(l, "U", t, c)[:, 0:hi - lo])
                        if hi == IN_WIDTH:
                            wait_drained(act, l, "U", t, c)
                            if t < nt:
                                linked(act.activation(lora_squares[:, t, 0:Q_LORA], u_rows[:, t, COL_Q:COL_KV], ACT.Square,
                                                      accum_out=stats[:, 0, t:t + 1]))
                            linked(act.activation(lora_squares[:, t, 0:KV_LORA], u_rows[:, t, COL_KV:COL_KR], ACT.Square,
                                                  accum_out=stats[:, 0, 4 + t:5 + t]))
                act.activation(lora_squares[:, TILES - 1, 0:1], stats[:, 0, 4:5], ACT.Copy).then_inc(S["norm_sums"], 1)
                act.wait_ge(S["norm_var"], TILES + 2)
                act.activation(stats[:, 2, 4:8], stats[:, 1, 4:8], ACT.Sqrt).then_inc(S["norm_root"], 1)
                act.activation(stats[:, 2, 0:nt], stats[:, 1, 0:nt], ACT.Sqrt).then_inc(S["norm_root"], 1)
                for s in range(nt // 2):
                    for c in range(2):
                        key = (l, "POOLED", s, c)
                        if s:
                            wait_filled(act, l, "POOL_OUT", s - 1, c)
                        drain(key, pooled[:, c, :], in_=bank_of(*key)[:, 0:SEQ])
                    for c in range(2):
                        key = (l, "DFT_CH", s, c)
                        if s:
                            wait_filled(act, l, "FNO_OUT", s - 1, c)
                        drain(key, dft_ch[:, c, :], in_=bank_of(*key)[:, 0:SEQ])
                    for c in range(2):
                        key = (l, "FNO_OUT", s, c)
                        drain(key, mixed[:, 2 + c, s * SEQ:(s + 1) * SEQ], in_=bank_of(*key)[:, 0:SEQ])
                for t in range(nt):
                    drain((l, "CQ", t), c_T[:, 0:3, t * P:(t + 1) * P], in_=split(bank_of(l, "CQ", t)[:, 0:3 * P], (3, P)))
                for t in range(TILES + 1):
                    if t < TILES:
                        if t < nt:
                            drain((l, "Q", t, 0), q_rows[:, t % 2, 0:512], in_=bank_of(l, "Q", t, 0)[:, :], scale=SCALE)
                        key = (l, "KV", t, 0)
                        b = split(bank_of(*key)[:, :], (4, P))
                        wait_filled(act, *key)
                        act.activation(split(k_rows[:, t % 2, 0:4 * QK], (4, QK))[:, :, 0:NOPE], b[:, :, 0:NOPE], ACT.Copy)
                        act.activation(split(v_rows[:, t, 0:256], (4, V_DIM)), b[:, :, NOPE:], ACT.Copy).then_inc(drained["act"], 1)
                    if 1 <= t <= nt:
                        for g in range(2):
                            drain((l, "QT", t - 1, g), q_T[0:QK, 4 * g:4 * g + 4, (t - 1) * P:t * P],
                                  in_=split(bank_of(l, "QT", t - 1, g)[0:QK, :], (4, P)))
                m = len(units(l))
                for i in range(m + 2):
                    if i < m:
                        lo, hi = keys_of(units(l)[i][0])
                        n = hi - lo
                        wait_filled(act, l, "S", i)
                        act.wait_ge(S["row_max"], i + 1)
                        if i >= 2:
                            wait_filled(act, l, "PT", i - 2)
                        act.activation(p_rows[:, i % 2, 0:n], bank_of(l, "S", i)[:, 0:n], ACT.Exp, bias=soft[:, 0, i:i + 1],
                                       accum_out=soft[:, 1, i:i + 1]).then_inc(drained["act"], 1)
                    if i >= 2:
                        lo, hi = keys_of(units(l)[i - 2][0])
                        n = hi - lo
                        if i >= 4:
                            wait_filled(act, l, "O", i - 4)
                        drain((l, "PT", i - 2), p_T[:, i % 2, 0:n], in_=bank_of(l, "PT", i - 2)[:, 0:n])
                for name, t in head_steps(l):
                    if name == "T2":
                        if t + 1 < nt:
                            h2_squares(t + 1)
                        drain((l, "T2", t, 0), h_T[:, 0:4, t * P:(t + 1) * P], in_=split(bank_of(l, "T2", t, 0)[:, :], (4, P)))
                        if t + 1 < nt:
                            h2_root(t + 1)
                    elif name == "R":
                        drain((l, "R", t), prob[:, t, :], ACT.Sigmoid, in_=bank_of(l, "R", t)[:, 0:EXPERTS])
                    elif t == 0:
                        h2_squares(0)
                        h2_root(0)
                for t in range(nt + 1):
                    if t < nt:
                        wait_filled(act, l, "SG", t)
                        if t >= 2:
                            wait_drained(act, l, "SG", t - 2)
                        act.activation(sig[:, t % 2, :], bank_of(l, "SG", t)[:, 0:FE], ACT.Sigmoid).then_inc(S["shared_sig"], 1)
                    if t >= 1:
                        if t >= 3:
                            wait_filled(act, l, "SD", t - 3, 1)
                        drain((l, "SH", t - 1), hid_T[:, (t - 1) % 2], in_=split(bank_of(l, "SH", t - 1)[:, 0:2 * P], (2, P)))

                def x_drain(i, s):
                    act.wait_ge(S["xt_filled"], i + 1)
                    ge(act, S["gu_filled"], i - 1)
                    act.activation(x_gT[:, s % 2, 0:4, 0:rows], split(banks[0][:, :], (4, P))[:, :, 0:rows], ACT.Copy).then_inc(S["xt_drained"], 1)

                wait_drained(act, l, "SD", nt - 1, 1)
                x_drain(0, 0)

                def split_down(i, w, n):
                    act.wait_ge(S["dn_in"][w], n)
                    ge(act, S["d_filled"], i)
                    for k in range(2):
                        act.activation(dn_hi[:, k, :], slot_dn(w)[:, k, :], ACT.Copy).then_inc(S["dn_hi"], 1)

                def step(j, s):
                    i = j * UNROLL + s
                    x_drain(i + 1, s + 1)
                    if not (isinstance(i, int) and i == 0):
                        split_down(i - 1, expert_slot(s - 1), ((UNROLL // 4) * j + (s - 1) // 4 + 1) * 16)
                    act.wait_ge(S["gu_filled"], i + 1)
                    ge(act, S["hid_ready"], 2 * i)
                    act.activation(sig_x, banks[2 + s % 2][:, 0:FE], ACT.Sigmoid).then_inc(S["sig_ready"], 1)
                    if not (isinstance(i, int) and i == 0):
                        y_drain(i - 1, j, s - 1)
                    act.wait_ge(S["ht_filled"], i + 1)
                    ge(act, S["d_filled"], i)
                    act.activation(hid_hi[:, :, :], split(banks[4][:, 0:2 * P], (2, P)), ACT.Copy).then_inc(S["hid_hi"], 1)

                def y_drain(i, j, s):
                    act.wait_ge(S["d_filled"], i + 1)
                    act.wait_ge(S["idx_ready"], i + 1)
                    ge(act, S["scattered"][s % 2], (j * (UNROLL // 2) + s // 2) * 16)
                    c = s % UNROLL
                    act.activation(y_g[0:rows, s % 2, 0:512], banks[6][0:rows, :], ACT.Copy, scale=row_w[0:rows, c:c + 1]).then_inc(S["y_ready"], 1)

                for s in range(UNROLL):
                    step(0, s)
                with act.Fori(1, EXPERTS // UNROLL) as j:
                    for s in range(UNROLL):
                        step(j, s)
                split_down(EXPERTS - 1, expert_slot(UNROLL - 1), (EXPERTS // 4) * 16)
                y_drain(EXPERTS - 1, EXPERTS // UNROLL - 1, UNROLL - 1)
                act.wait_ge(S["extra_ready"], 1)
                n_extra = act.value_load(extra_row[0:1, 0:1], min_val=0, max_val=MAX_EXTRA)

                def block_x(o):
                    act.wait_ge(S["xt_filled"], o + 1 + EXPERTS + 1)
                    act.activation(x_gT[:, 0, 0:4, 0:rows], split(banks[0][:, :], (4, P))[:, :, 0:rows], ACT.Copy).then_inc(S["xt_drained"], 1)

                def block_y(o):
                    act.wait_ge(S["gu_filled"], o + 1 + EXPERTS)
                    act.activation(sig_x, banks[2][:, 0:FE], ACT.Sigmoid).then_inc(S["sig_ready"], 1)
                    act.wait_ge(S["d_filled"], o + 1 + EXPERTS)
                    act.activation(y_g[0:rows, 0, 0:512], banks[6][0:rows, :], ACT.Copy, scale=row_w[0:rows, 0:1]).then_inc(S["y_ready"], 1)

                with act.If(n_extra > 0):
                    block_x(0)
                if l + 1 < DEPTH:
                    load_w_in(act, l + 1, 0, DK)
                with act.If(n_extra > 0):
                    act.wait_ge(S["scattered"][0], 16 * (EXPERTS // 2))
                    block_y(0)
                with act.If(n_extra > 1):
                    with act.Fori(1, n_extra) as o:
                        block_x(o)
                        block_y(o)
            for t in range(LATENT_TILES):
                norm_tile(DEPTH, t)

        @block.vector
        def _(dve):
            link = [0]

            def linked(ins):
                link[0] += 1
                ins.then_inc(dve_link, 1)
                dve.wait_ge(dve_link, link[0])

            dve.memset(ones[:, :], 1.0).then_inc(ones_ready, 1)
            dve.wait_ge(cond_sig, 1)
            dve.tensor_tensor(cond_silu[:, :, :], cond_silu[:, :, :], cond[:, :, :].rearrange("p s k -> p k s"),
                              ALU.mult).then_inc(cond_ready, 1)
            dve.wait_ge(cond_sig, 2)
            dve.tensor_tensor(cond_lo[:, :, :], cond_silu[:, :, :], cond_hi[:, :, :].bitcast(F32), ALU.subtract).then_inc(cond_ready, 1)
            for l in range(DEPTH):
                def add_bias(c, slot):
                    dve.wait_ge(mod_filled, PIECES * (l * MOD_CHUNKS + c + 1))
                    dve.tensor_tensor(mod_rows[l][:, bass.ds(c * MOD_N, MOD_N)], banks[slot][0:2, :], mod_rows[l][:, bass.ds(c * MOD_N, MOD_N)],
                                      ALU.add).then_inc(mod_added, 1)

                def split_round(j, first):
                    for s in range(MOD_SLOTS):
                        for h in range(PIECES):
                            piece = PIECES * (l * MOD_CHUNKS + j * MOD_SLOTS + s) + h
                            dve.wait_ge(mod_hi, piece + 1)
                            ge(dve, mod_filled, piece + 1 - PIECES)
                            dve.tensor_tensor(mod_w_lo[:, h], mod_w[:, s, h * PIECE_K:(h + 1) * PIECE_K, :],
                                              mod_w_hi[:, h].bitcast(F32), ALU.subtract).then_inc(mod_lo, 1)
                        if first and s == 0:
                            if l == 0:
                                dve.wait_ge(mod_bias_in, 64)
                        else:
                            add_bias(j * MOD_SLOTS + s - 1, (s - 1) % MOD_SLOTS)

                split_round(0, True)
                with dve.Fori(1, MOD_CHUNKS // MOD_SLOTS) as j:
                    split_round(j, False)
                add_bias(MOD_CHUNKS - 1, MOD_SLOTS - 1)
                dve.wait_ge(mod_added, (l + 1) * MOD_CHUNKS)
                dve.wait_ge(mod_bias_in, 64 + 32 * l)
                linked(dve.scalar_tensor_tensor(out=mod_rows[l][:, D:2 * D], in0=mod_rows[l][:, D:2 * D], scalar=1.0,
                                                in1=gain_rows[:, 0:D], op0=ALU.add, op1=ALU.mult))
                dve.scalar_tensor_tensor(out=mod_rows[l][:, 4 * D:5 * D], in0=mod_rows[l][:, 4 * D:5 * D], scalar=1.0,
                                         in1=gain_rows[:, D:], op0=ALU.add, op1=ALU.mult).then_inc(mod_ready, 1)

            def rstd(lo, hi, roots, value):
                v, root, r, tmp = stats[:, 1, lo:hi], stats[:, 2, lo:hi], stats[:, 3, lo:hi], newton[:, lo:hi]
                dve.wait_ge(roots, value)
                linked(dve.reciprocal(r, root))
                linked(dve.tensor_tensor(tmp, r, r, ALU.mult))
                linked(dve.tensor_tensor(tmp, tmp, v, ALU.mult))
                linked(dve.tensor_scalar(tmp, tmp, -0.5, 1.5, ALU.mult, ALU.add))
                linked(dve.tensor_tensor(r, r, tmp, ALU.mult))

            def normed(t, ready, to):
                s = t // STREAM_TILES
                linked(dve.scalar_tensor_tensor(out=to[:, t, :], in0=x_rows[:, t, :], scalar=stats[:, 3, t:t + 1],
                                                in1=mods[:, s, 1, :], op0=ALU.mult, op1=ALU.mult))
                dve.tensor_tensor(to[:, t, :], to[:, t, :], mods[:, s, 0, :], ALU.add).then_inc(ready, 1)

            def drain(key, out, in_):
                wait_filled(dve, *key)
                dve.tensor_copy(out, in_).then_inc(drained["dve"], 1)

            def gated(key, t, c, tmp, last):
                s = t // STREAM_TILES
                wait_filled(dve, *key)
                dve.tensor_tensor(tmp, bank_of(*key)[:, :], mods[:, s, 2, c * 512:(c + 1) * 512], ALU.mult).then_inc(drained["dve"], 1)
                wait_drained(dve, *key)
                ins = dve.tensor_tensor(x_rows[:, t, c * 512:(c + 1) * 512], x_rows[:, t, c * 512:(c + 1) * 512], tmp, ALU.add)
                if last is not None:
                    ins.then_inc(last, 1)
                else:
                    linked(ins)

            def norm_tiles(l, n):
                S = L[min(l, DEPTH - 1)]
                done = TILES + 1 + LATENT_TILES if l == DEPTH else 0
                for t in range(n):
                    if l == DEPTH and t == 0:
                        for u in range(n):
                            add_expert_rows(l - 1, u)
                    elif 0 < l < DEPTH:
                        add_expert_rows(l - 1, t)
                    dve.wait_ge(S["norm_sums"], done + t + 1)
                    dve.tensor_scalar(stats[:, 1, t:t + 1], stats[:, 0, t:t + 1], 1.0 / D, EPS, ALU.mult, ALU.add).then_inc(S["norm_var"], 1)
                    rstd(t, t + 1, S["norm_root"], done + (l == DEPTH) + t + 1)
                    if l < DEPTH:
                        if t == 0:
                            dve.wait_ge(S["mods_in"], 32)
                        normed(t, S["h_ready"], h_rows)
                    else:
                        dve.wait_ge(S["last_gain_in"], 16)
                        dve.scalar_tensor_tensor(out=h_rows[:, t, :], in0=x_rows[:, t, :], scalar=stats[:, 3, t:t + 1], in1=mods[:, 1, 0, :],
                                                 op0=ALU.mult, op1=ALU.mult).then_inc(S["out_ready"], 1)

            def add_expert_rows(l, t):
                S = L[l]
                for q in range(4):
                    if q in POOL_QTRS:
                        continue
                    dve.wait_ge(S["y_in"][q], 16 * (t + 1))
                    y = y_quarter[q]
                    cols = slice(q * QTR, (q + 1) * QTR)
                    linked(dve.tensor_reduce(y_sum[:, :], y.rearrange("p k n -> p n k"), AX.X, ALU.add))
                    linked(dve.tensor_tensor(y_sum[:, :], y_sum[:, :], mods[:, t // 2, 2, cols], ALU.mult))
                    dve.tensor_tensor(x_rows[:, t, cols], x_rows[:, t, cols], y_sum[:, :], ALU.add).then_inc(S["x_done"], 1)
                    dve.wait_ge(S["x_done"], t * (4 - len(POOL_QTRS)) + q + 1)

            dve.wait_ge(const_in, 8 * 16)
            for l in range(DEPTH):
                S = L[l]
                nt = active_tiles(l)
                norm_tiles(l, TILES)
                dve.wait_ge(S["norm_sums"], TILES + 1)
                dve.tensor_scalar(stats[:, 1, 0:nt], stats[:, 0, 0:nt], 1.0 / Q_LORA, EPS, ALU.mult, ALU.add).then_inc(S["norm_var"], 1)
                dve.tensor_scalar(stats[:, 1, 4:8], stats[:, 0, 4:8], 1.0 / KV_LORA, EPS, ALU.mult, ALU.add).then_inc(S["norm_var"], 1)
                rstd(0, nt, S["norm_root"], TILES + 2)
                rstd(4, 8, S["norm_root"], TILES + 2)
                dve.wait_ge(S["w_lora_in"], 64)
                for t in range(TILES):
                    if t < nt:
                        dve.scalar_tensor_tensor(out=u_rows[:, t, COL_Q:COL_KV], in0=u_rows[:, t, COL_Q:COL_KV], scalar=stats[:, 3, t:t + 1],
                                                 in1=g_lora[:, 0:Q_LORA], op0=ALU.mult, op1=ALU.mult)
                    dve.scalar_tensor_tensor(out=u_rows[:, t, COL_KV:COL_KR], in0=u_rows[:, t, COL_KV:COL_KR], scalar=stats[:, 3, 4 + t:5 + t],
                                             in1=g_lora[:, Q_LORA:], op0=ALU.mult, op1=ALU.mult).then_inc(S["lora_ready"], 1)
                dve.wait_ge(S["mixer_in"], 6 * 16)
                for s in range(nt // 2):
                    for c in range(2):
                        key = (l, "DFT_POS", s, c)
                        if s:
                            wait_filled(dve, l, "DFT_CH", s - 1, c)
                        drain(key, dft_pos[:, c, :], bank_of(*key)[:, :])
                    for c in range(2):
                        key = (l, "POOL_OUT", s, c)
                        wait_filled(dve, *key)
                        dve.tensor_scalar(mixed[:, c, s * SEQ:(s + 1) * SEQ], bank_of(*key)[:, 0:SEQ], pool_scale[:, c:c + 1], None,
                                          ALU.mult).then_inc(drained["dve"], 1)
                for t in range(TILES):
                    drain((l, "CKV", t), c_T[:, 3:5, t * P:(t + 1) * P], split(bank_of(l, "CKV", t)[:, 0:2 * P], (2, P)))

                def rotate(x1, x2, cos, sin, shape, last):
                    n = shape[0] * shape[1] * shape[2]
                    tmp = [split(rope_tmp[:, i, 0:n], shape) for i in range(4)]
                    for o, x, y in ((tmp[0], x1, cos), (tmp[1], x2, sin), (tmp[2], x2, cos)):
                        dve.tensor_tensor(o, x, y, ALU.mult)
                    linked(dve.tensor_tensor(tmp[3], x1, sin, ALU.mult))
                    dve.tensor_tensor(x1, tmp[0], tmp[1], ALU.subtract)
                    ins = dve.tensor_tensor(x2, tmp[2], tmp[3], ALU.add)
                    if last is None:
                        linked(ins)
                    else:
                        ins.then_inc(last, 1)
                        dve.wait_ge(last, rotations[0])

                rotations = [0]
                for t in range(TILES + 1):
                    if t < TILES:
                        if t < nt:
                            key = (l, "Q", t, 1)
                            wait_filled(dve, *key)
                            dve.tensor_scalar(q_rows[:, t % 2, 512:768], bank_of(*key)[:, 0:256], SCALE, None, ALU.mult).then_inc(drained["dve"], 1)
                            if t < LATENT_TILES:
                                wait_drained(dve, l, "Q", t, 0)
                                wait_drained(dve, l, "Q", t, 1)
                                q4 = q_rows[:, t % 2, :].rearrange("p (h q) -> p h q", h=HEADS)[:, :, NOPE:]
                                q4 = q4.rearrange("p h (x f) -> p h x f", x=4)
                                cos, sin = (split(rope_tab[:, t, i, :], (2, 8)).unsqueeze(1).broadcast_to([P, HEADS, 2, 8]) for i in range(2))
                                rotations[0] += 1
                                rotate(q4[:, :, 0::2, :], q4[:, :, 1::2, :], cos, sin, (HEADS, 2, 8), S["q_rotated"])
                        kr = u_rows[:, t, COL_KR:]
                        if t < LATENT_TILES:
                            k4 = kr.rearrange("p (a x f) -> p a x f", a=1, x=4)
                            cos, sin = (split(rope_tab[:, t, i, :], (1, 2, 8)) for i in range(2))
                            rotate(k4[:, :, 0::2, :], k4[:, :, 1::2, :], cos, sin, (1, 2, 8), None)
                        key = (l, "KV", t, 1)
                        b = split(bank_of(*key)[:, :], (4, P))
                        wait_filled(dve, *key)
                        dve.tensor_copy(split(k_rows[:, t % 2, 4 * QK:], (4, QK))[:, :, 0:NOPE], b[:, :, 0:NOPE])
                        dve.tensor_copy(split(v_rows[:, t, 256:], (4, V_DIM)), b[:, :, NOPE:]).then_inc(drained["dve"], 1)
                        dve.tensor_copy(split(k_rows[:, t % 2, :], (HEADS, QK))[:, :, NOPE:],
                                        kr.unsqueeze(1).broadcast_to([P, HEADS, ROPE])).then_inc(S["k_ready"], 1)
                    if t >= 1:
                        for g in range(2):
                            drain((l, "KT", t - 1, g), k_T[0:QK, 4 * g:4 * g + 4, (t - 1) * P:t * P],
                                  split(bank_of(l, "KT", t - 1, g)[0:QK, :], (4, P)))
                m = len(units(l))
                for i in range(m + 3):
                    if i < m:
                        lo, hi = keys_of(units(l)[i][0])
                        wait_filled(dve, l, "S", i)
                        dve.tensor_reduce(soft[:, 0, i:i + 1], bank_of(l, "S", i)[:, 0:hi - lo], AX.X, ALU.max, negate=True).then_inc(S["row_max"], 1)
                    if 1 <= i < m + 1:
                        lo, hi = keys_of(units(l)[i - 1][0])
                        wait_drained(dve, l, "S", i - 1)
                        linked(dve.reciprocal(soft[:, 2, i - 1:i], soft[:, 1, i - 1:i]))
                        pr = p_rows[:, (i - 1) % 2, 0:hi - lo]
                        dve.tensor_scalar(pr, pr, soft[:, 2, i - 1:i], None, ALU.mult).then_inc(S["p_ready"], 1)
                    if i >= 3:
                        qt, h = units(l)[i - 3]
                        rows = slice(64 * (h % 2), 64 * (h % 2) + 64)
                        drain((l, "O", i - 3), mixed[rows, 4 + h // 2, qt * P:(qt + 1) * P], bank_of(l, "O", i - 3)[rows, 0:P])
                dve.wait_ge(S["gate_in"], 16 * (nt // 2))
                for name, t in head_steps(l):
                    if name == "OUT":
                        for c in range(2):
                            gated((l, "OUT", t, c), t, c, res_tmp[:, c, :], S["x_mixed"] if c else None)
                        if t:
                            drain((l, "T2", t - 1, 1), h_T[:, 4:8, (t - 1) * P:t * P], split(bank_of(l, "T2", t - 1, 1)[:, :], (4, P)))
                        dve.wait_ge(S["norm_sums"], TILES + 2 + t)
                        dve.tensor_scalar(stats[:, 1, t:t + 1], stats[:, 0, t:t + 1], 1.0 / D, EPS, ALU.mult, ALU.add).then_inc(S["norm_var"], 1)
                        rstd(t, t + 1, S["norm_root"], TILES + 3 + t)
                        if t == 0:
                            dve.wait_ge(S["mods_in"], 32 + 16 * (nt // 2))
                        normed(t, S["h2_ready"], h2_rows)
                drain((l, "T2", nt - 1, 1), h_T[:, 4:8, (nt - 1) * P:nt * P], split(bank_of(l, "T2", nt - 1, 1)[:, :], (4, P)))

                N = nt
                rows = list_rows(l)
                dve.wait_ge(S["router_in"], 32)
                for t in range(N):
                    wait_drained(dve, l, "R", t)
                    ins = dve.tensor_tensor(sel[:, t, :], prob[:, t, :], r_bias[:, :], ALU.add)
                linked(ins)
                for t in range(N):
                    for g in range(EGROUPS):
                        ins = dve.max(out=top2[:, t, g, :], in_=sel[:, t, 8 * g:8 * g + 8])
                linked(ins)
                linked(dve.tensor_tensor(gscore[:, 0:N, :], top2[:, 0:N, :, 0], top2[:, 0:N, :, 1], ALU.add))
                other = gscore[:, 0:N, :].unsqueeze(2).broadcast_to([P, N, 8, 8])
                own = gscore[:, 0:N, :].unsqueeze(3).broadcast_to([P, N, 8, 8])
                tie_b = split(tie[:, :], (8, 8)).unsqueeze(1).broadcast_to([P, N, 8, 8])
                dve.tensor_tensor(cmp_a[:, 0:N], other, own, ALU.is_gt)
                linked(dve.tensor_tensor(cmp_b[:, 0:N], other, own, ALU.is_equal))
                linked(dve.tensor_tensor(cmp_b[:, 0:N], cmp_b[:, 0:N], tie_b, ALU.mult))
                linked(dve.tensor_tensor(cmp_a[:, 0:N], cmp_a[:, 0:N], cmp_b[:, 0:N], ALU.add))
                linked(dve.tensor_reduce(gmask[:, 0:N, :], cmp_a[:, 0:N], AX.X, ALU.add))
                linked(dve.tensor_scalar(gmask[:, 0:N, :], gmask[:, 0:N, :], TOP_GROUPS - 0.5, None, ALU.is_lt))
                linked(dve.tensor_scalar(gneg[:, 0:N, :], gmask[:, 0:N, :], 1.0, 1e30, ALU.subtract, ALU.mult))
                sel4 = sel[:, 0:N, :].rearrange("p t (g e) -> p t g e", g=8)
                linked(dve.tensor_tensor(sel4, sel4, gmask[:, 0:N, :].unsqueeze(3).broadcast_to([P, N, 8, 8]), ALU.mult))
                linked(dve.tensor_tensor(sel4, sel4, gneg[:, 0:N, :].unsqueeze(3).broadcast_to([P, N, 8, 8]), ALU.add))
                for t in range(N):
                    ins = dve.max(out=top8[:, t, :], in_=sel[:, t, :])
                linked(ins)
                for t in range(N):
                    ins = dve.match_replace(out=chosen[:, t, :], in_to_replace=top8[:, t, :], in_values=sel[:, t, :], imm_value=-2e30)
                linked(ins)
                dve.tensor_scalar(chosen[:, 0:N, :], chosen[:, 0:N, :], -1.5e30, None, ALU.is_lt).then_inc(S["chosen_ready"], 1)
                dve.wait_ge(S["chosen_ready"], 1)
                linked(dve.tensor_tensor(prob[:, 0:N, :], prob[:, 0:N, :], chosen[:, 0:N, :], ALU.mult))
                linked(dve.tensor_reduce(wsum[:, 0:N], prob[:, 0:N, :], AX.X, ALU.add))
                linked(dve.reciprocal(winv[:, 0:N], wsum[:, 0:N]))
                dve.memset(vals[:, 0:N, :, :], 0.0)
                linked(dve.memset(posm[:, 0:N, :], -1.0))
                for t in range(N):
                    dve.tensor_scalar(vals[:, t, 0:EXPERTS, 2], prob[:, t, :], winv[:, t:t + 1], ROUTED_SCALE, ALU.mult, ALU.mult)
                    dve.tensor_scalar(vals[:, t, 0:EXPERTS, 0], slots_iota[:, 0:EXPERTS], 0.0, token_cols[:, t:t + 1], ALU.mult, ALU.add)

                def make_g(i, e, s, offset):
                    for t in range(N):
                        ins = dve.tensor_scalar(one_hot[:, s % 2, t, 0:rows], slots_iota[:, bass.ds(offset, rows)], posm[:, t, bass.ds(e, 1)], None, ALU.is_equal)
                    return ins

                def take_list(s):
                    dve.tensor_copy(row_w[0:rows, s % UNROLL:s % UNROLL + 1], banks[LIST_BANK][0:rows, 2:3])
                    return dve.tensor_scalar(row_idx[0:rows, s % UNROLL, :], banks[LIST_BANK][0:rows, 0:2], float(SKIP), None, ALU.add)

                dve.wait_ge(S["gate_in"], 32 * (nt // 2))
                for step in tail_steps(l):
                    t = step[1] if len(step) > 1 else None
                    if step[0] == "SG":
                        key = (l, "SG", t)
                        b = bank_of(*key)
                        wait_filled(dve, *key)
                        dve.wait_ge(S["shared_sig"], t + 1)
                        if t >= 2:
                            wait_filled(dve, l, "SH", t - 2)
                        linked(dve.tensor_tensor(hid[:, t % 2, :], sig[:, t % 2, :], b[:, 0:FE], ALU.mult))
                        dve.tensor_tensor(hid[:, t % 2, :], hid[:, t % 2, :], b[:, FE:], ALU.mult).then_inc(drained["dve"], 1)
                    elif step[0] == "SD":
                        for c in range(2):
                            gated((l, "SD", t, c), t, c, moe_tmp[:, c, :], None)
                    elif step[0] == "MT":
                        drain((l, "MT"), ranks_T[0:64, 0:N, :], split(bank_of(l, "MT")[0:64, 0:N * P], (N, P)))
                    elif step[0] == "PLACES":
                        key = (l, "RANK")
                        wait_filled(dve, *key)
                        b = split(bank_of(*key)[:, 0:N * EXPERTS], (N, EXPERTS))
                        for t in range(N):
                            ins = dve.tensor_scalar(vals[:, t, 0:EXPERTS, 1], b[:, t, :], token_cols[:, 4 + t:5 + t], None, ALU.add)
                        ins.then_inc(drained["dve"], 1)
                        key = (l, "POS")
                        wait_filled(dve, *key)
                        b = split(bank_of(*key)[:, 0:(TILES + 1) * EXPERTS], (TILES + 1, EXPERTS))
                        linked(dve.scalar_tensor_tensor(out=posm[:, 0:N, 0:EXPERTS], in0=b[:, 0:N, :], scalar=1.0, in1=chosen[:, 0:N, :],
                                                        op0=ALU.add, op1=ALU.mult))
                        linked(dve.tensor_scalar(posm[:, 0:N, 0:EXPERTS], posm[:, 0:N, 0:EXPERTS], -1.0, None, ALU.add))
                        cnt = bank_of(*key)[0:64, TILES * EXPERTS:TILES * EXPERTS + 1]
                        linked(dve.tensor_scalar(ext[0:64, 0:1], cnt, float(rows) + 0.5, None, ALU.is_gt))
                        for b_ in range(2, -(-N * P // rows)):
                            linked(dve.tensor_scalar(ext[0:64, 1:2], cnt, float(rows * b_) + 0.5, None, ALU.is_gt))
                            linked(dve.tensor_tensor(ext[0:64, 0:1], ext[0:64, 0:1], ext[0:64, 1:2], ALU.add))
                        dve.tensor_scalar(ext_b, ones[0:64, :], ext[0:64, 0:1], None, ALU.mult).then_inc(drained["dve"], 1)
                    elif step[0] == "ENDS":
                        key = (l, "ENDS")
                        wait_filled(dve, *key)
                        b = bank_of(*key)
                        dve.tensor_scalar(ends[:, 0:64], b[:, 0:64], lane[:, 0:1], None, ALU.is_le)
                        linked(dve.tensor_copy(table[:, 0:1], b[:, 63:64]))
                        dve.tensor_reduce(table[:, 1:2], ends[:, 0:64], AX.X, ALU.add)
                        dve.tensor_tensor(ends[:, 64:128], ends[:, 0:64], b[:, 64:128], ALU.mult).then_inc(drained["dve"], 1)
                        wait_drained(dve, *key)
                        linked(dve.tensor_reduce(table[:, 2:3], ends[:, 64:128], AX.X, ALU.add))
                        linked(dve.tensor_scalar(table[:, 1:2], table[:, 1:2], float(EXPERTS - 1), None, ALU.min))
                        linked(dve.tensor_scalar(table[:, 2:3], table[:, 2:3], -1.0, lane[:, 0:1], ALU.mult, ALU.add))
                        dve.tensor_scalar(table[:, 2:3], table[:, 2:3], 1.0, 0.0, ALU.add, ALU.max).then_inc(S["table_ready"], 1)
                    elif step[0] == "EXTRA":
                        key = (l, "EXTRA")
                        wait_filled(dve, *key)
                        dve.tensor_copy(extra_row[:, :], bank_of(*key)[0:1, 0:3 * MAX_EXTRA]).then_inc(drained["dve"], 1)
                        wait_drained(dve, *key)
                        dve.memset(newton[:, 0:1], 0.0).then_inc(S["extra_ready"], 1)
                        for i in range(2):
                            make_g(i, i, i, 0).then_inc(S["g_ready"], 1)
                    else:
                        dve.wait_ge(S["list_filled"], t + 1)
                        take_list(t).then_inc(S["idx_ready"], 1)
                        if t + 2 < AHEAD:
                            make_g(t + 2, t + 2, t, 0).then_inc(S["g_ready"], 1)

                def x_drain(i, s):
                    dve.wait_ge(S["xt_filled"], i + 1)
                    ge(dve, S["gu_filled"], i - 1)
                    dve.tensor_copy(x_gT[:, s % 2, 4:8, 0:rows], split(banks[1][:, :], (4, P))[:, :, 0:rows]).then_inc(S["xt_drained"], 1)

                def y_drain(i, j, s):
                    dve.wait_ge(S["d_filled"], i + 1)
                    ge(dve, S["scattered"][s % 2], (j * (UNROLL // 2) + s // 2) * 16)
                    c = s % UNROLL
                    dve.tensor_scalar(y_g[0:rows, s % 2, 512:], banks[7][0:rows, :], row_w[0:rows, c:c + 1], None, ALU.mult).then_inc(S["y_ready"], 1)

                x_drain(0, 0)

                def split_down(i, w):
                    for k in range(2):
                        dve.wait_ge(S["dn_hi"], 2 * i + k + 1)
                        ge(dve, S["d_filled"], i)
                        dve.tensor_tensor(dn_lo[:, k, :], slot_dn(w)[:, k, :], dn_hi[:, k, :].bitcast(F32), ALU.subtract).then_inc(S["dn_lo"], 1)

                def step(j, s):
                    i = j * UNROLL + s
                    x_drain(i + 1, s + 1)
                    dve.wait_ge(S["list_filled"], i + AHEAD - 1)
                    make_g(i, i + AHEAD, s, 0).then_inc(S["g_ready"], 1)
                    if not (isinstance(i, int) and i == 0):
                        split_down(i - 1, expert_slot(s - 1))
                    dve.wait_ge(S["gu_filled"], i + 1)
                    dve.wait_ge(S["sig_ready"], i + 1)
                    ge(dve, S["ht_filled"], i)
                    b = banks[2 + s % 2]
                    dve.tensor_tensor(hid_x, sig_x, b[:, 0:FE], ALU.mult).then_inc(S["hid_ready"], 1)
                    dve.wait_ge(S["hid_ready"], 2 * i + 1)
                    dve.tensor_tensor(hid_x, hid_x, b[:, FE:], ALU.mult).then_inc(S["hid_ready"], 1)
                    if not (isinstance(i, int) and i == 0):
                        y_drain(i - 1, j, s - 1)
                    dve.wait_ge(S["list_filled"], i + AHEAD + 1)
                    ge(dve, S["y_ready"], 2 * (i - AHEAD + 1))
                    ge(dve, S["scattered"][s % 2], ((UNROLL // 2) * j + (s - AHEAD) // 2 + 1) * 16)
                    take_list(s + AHEAD).then_inc(S["idx_ready"], 1)
                    dve.wait_ge(S["hid_hi"], i + 1)
                    ge(dve, S["d_filled"], i)
                    dve.tensor_tensor(hid_lo[:, :, :], split(banks[4][:, 0:2 * P], (2, P)), hid_hi[:, :, :].bitcast(F32),
                                      ALU.subtract).then_inc(S["ht_drained"], 1)

                for s in range(UNROLL):
                    step(0, s)
                def block_of(o):
                    return (dve.value_load(extra_row[0:1, bass.ds(o + MAX_EXTRA, 1)], min_val=0, max_val=EXPERTS - 1),
                            dve.value_load(extra_row[0:1, bass.ds(o + 2 * MAX_EXTRA, 1)], min_val=0, max_val=TILES - 1))

                dve.wait_ge(S["extra_ready"], 1)
                n_extra = dve.value_load(extra_row[0:1, 0:1], min_val=0, max_val=MAX_EXTRA)
                e_first, k_first = block_of(0)
                with dve.Fori(1, EXPERTS // UNROLL) as j:
                    for s in range(UNROLL):
                        step(j, s)
                def block_list(o, e, k):
                    make_g(0, e, 0, k * rows).then_inc(S["g_ready"], 1)
                    dve.wait_ge(S["list_filled"], o + 1 + LISTED)
                    take_list(0).then_inc(S["idx_ready"], 1)

                def block_run(o):
                    dve.wait_ge(S["xt_filled"], o + 1 + EXPERTS + 1)
                    dve.tensor_copy(x_gT[:, 0, 4:8, 0:rows], split(banks[1][:, :], (4, P))[:, :, 0:rows]).then_inc(S["xt_drained"], 1)
                    dve.wait_ge(S["gu_filled"], o + 1 + EXPERTS)
                    dve.wait_ge(S["sig_ready"], o + 1 + EXPERTS)
                    dve.tensor_tensor(hid_x, sig_x, banks[2][:, 0:FE], ALU.mult).then_inc(S["hid_ready"], 1)
                    dve.wait_ge(S["hid_ready"], 2 * (o + EXPERTS) + 1)
                    dve.tensor_tensor(hid_x, hid_x, banks[2][:, FE:], ALU.mult).then_inc(S["hid_ready"], 1)
                    dve.wait_ge(S["ht_filled"], o + 1 + EXPERTS)
                    dve.tensor_copy(hid_T_x, split(banks[4][:, 0:2 * P], (2, P))).then_inc(S["ht_drained"], 1)
                    dve.wait_ge(S["d_filled"], o + 1 + EXPERTS)
                    dve.tensor_scalar(y_g[0:rows, 0, 512:], banks[7][0:rows, :], row_w[0:rows, 0:1], None, ALU.mult).then_inc(S["y_ready"], 1)
                    dve.wait_ge(S["e_x"], (o + 1) * 32)

                with dve.If(n_extra > 0):
                    block_list(0, e_first, k_first)
                split_down(EXPERTS - 1, expert_slot(UNROLL - 1))
                y_drain(EXPERTS - 1, EXPERTS // UNROLL - 1, UNROLL - 1)
                dve.wait_ge(S["scattered"][0], 16 * (EXPERTS // 2))
                with dve.If(n_extra > 0):
                    block_run(0)
                with dve.If(n_extra > 1):
                    with dve.Fori(1, n_extra) as o:
                        block_list(o, *block_of(o))
                        block_run(o)

                dve.wait_ge(S["scattered"][1], 16 * (EXPERTS // 2))
                dve.memset(newton[:, 0:1], 0.0).then_inc(S["rows_back"], 1)

            norm_tiles(DEPTH, LATENT_TILES)

        @block.tensor
        def _(pe):
            def claim(*key):
                prev = jobs.before(*key)
                if prev is not None:
                    wait_drained(pe, *prev)
                return bank_of(*key)

            pe.wait_ge(cond_ready, 2)
            for l in range(DEPTH):
                def mod_round(j):
                    for s in range(MOD_SLOTS):
                        c = l * MOD_CHUNKS + j * MOD_SLOTS + s
                        ge(pe, mod_added, c - MOD_SLOTS + 1)
                        for h in range(PIECES):
                            pe.wait_ge(mod_lo, PIECES * c + h + 1)
                            for k in range(PIECE_K):
                                for n, (x, w) in enumerate(((cond_hi, mod_w_hi), (cond_hi, mod_w_lo), (cond_lo, mod_w_hi))):
                                    mm = pe.matmul(banks[s][0:2, :], x[:, h * PIECE_K + k, :], w[:, h, k, :],
                                                   start=(h == k == n == 0), stop=(h == PIECES - 1 and k == PIECE_K - 1 and n == 2))
                            mm.then_inc(mod_filled, 1)

                mod_round(0)
                with pe.Fori(1, MOD_CHUNKS // MOD_SLOTS) as j:
                    mod_round(j)
            pe.wait_ge(mod_added, DEPTH * MOD_CHUNKS)
            pe.wait_ge(const_in, 8 * 16)
            pe.wait_ge(ones_ready, 1)

            for l in range(DEPTH):
                S = L[l]
                nt = active_tiles(l)
                rows = list_rows(l)

                def chain(key, cols, lhs, rhs, n):
                    b = claim(*key)
                    for k in range(n):
                        mm = pe.matmul(b[:, 0:cols], lhs(k), rhs(k), start=(k == 0), stop=(k == n - 1))
                    mm.then_inc(psum_filled, 1)

                def by_group(key, w, x):
                    b = claim(*key)
                    for g in range(2):
                        half = slice(64 * g, 64 * g + 64)
                        mm = pe.matmul(b[half, 0:SEQ], w[half, :], x[half, :], start=True, stop=True)
                    mm.then_inc(psum_filled, 1)

                def flips(key, blocks, rows=P):
                    b = claim(*key)
                    for n, x in enumerate(blocks):
                        mm = pe.transpose(b[0:rows, n * P:(n + 1) * P], x, ident[:, :])
                    mm.then_inc(psum_filled, 1)

                for step in in_steps(l):
                    if step[0] == "T1":
                        t = step[1]
                        pe.wait_ge(S["h_ready"], t + 1)
                        for c in range(2):
                            flips((l, "T1", t, c), [h_rows[:, t, (4 * c + k) * P:(4 * c + k + 1) * P] for k in range(4)])
                    elif step[0] == "U":
                        _, t, c = step
                        if t == c == 0:
                            pe.wait_ge(S["w_in_in"], 16 if l else 2 * 16)
                        if c == 0:
                            wait_drained(pe, l, "T1", t, 0)
                            wait_drained(pe, l, "T1", t, 1)
                        lo, hi = u_chunks(l, t)[c]
                        chain((l, "U", t, c), hi - lo, lambda k: h_T[:, k, t * P:(t + 1) * P], lambda k: w_in[:, k, lo:hi], DK)
                pe.wait_ge(S["mixer_in"], 6 * 16)
                for t in range(nt):
                    for c in range(len(u_chunks(l, t))):
                        wait_drained(pe, l, "U", t, c)
                for s in range(nt // 2):
                    for c in range(2):
                        b = claim(l, "POOLED", s, c)
                        for g in range(2):
                            for t in range(2):
                                lo = (2 * c + g) * GROUP
                                mm = pe.matmul(b[64 * g:64 * g + 64, 0:SEQ], u_rows[:, 2 * s + t, lo:lo + GROUP], pool_m[:, t, 2 * c + g, :],
                                               start=(t == 0), stop=(t == 1))
                        mm.then_inc(psum_filled, 1)
                    for c in range(2):
                        lo = COL_FNO + c * P
                        chain((l, "DFT_POS", s, c), 2 * SEQ, lambda t: u_rows[:, 2 * s + t, lo:lo + P], lambda t: dft_l[:, t, :], 2)
                    for c in range(2):
                        wait_drained(pe, l, "POOLED", s, c)
                        by_group((l, "POOL_OUT", s, c), w_pool_g[:, c, :], pooled[:, c, :])
                    for c in range(2):
                        wait_drained(pe, l, "DFT_POS", s, c)
                        chain((l, "DFT_CH", s, c), SEQ, lambda k: dft_c[:, k, :], lambda k: dft_pos[:, c, k * SEQ:(k + 1) * SEQ], 2)
                    for c in range(2):
                        wait_drained(pe, l, "DFT_CH", s, c)
                        by_group((l, "FNO_OUT", s, c), w_fno_g[:, c, :], dft_ch[:, c, :])
                for t in range(TILES):
                    pe.wait_ge(S["lora_ready"], t + 1)
                    if t < nt:
                        flips((l, "CQ", t), [u_rows[:, t, COL_Q + P * k:COL_Q + P * (k + 1)] for k in range(3)])
                    flips((l, "CKV", t), [u_rows[:, t, COL_KV + P * k:COL_KV + P * (k + 1)] for k in range(2)])
                for t in range(TILES + 1):
                    if t < TILES:
                        if t < nt:
                            wait_drained(pe, l, "CQ", t)
                            for c, (lo, hi) in enumerate(((0, 512), (512, 768))):
                                chain((l, "Q", t, c), hi - lo, lambda k: c_T[:, k, t * P:(t + 1) * P], lambda k: w_uq[:, k, lo:hi], 3)
                        wait_drained(pe, l, "CKV", t)
                        for c in range(2):
                            chain((l, "KV", t, c), 512, lambda k: c_T[:, 3 + k, t * P:(t + 1) * P], lambda k: w_ukv[:, k, 512 * c:512 * c + 512], 2)
                    if t >= 1:
                        u = t - 1
                        if u < nt:
                            wait_drained(pe, l, "Q", u, 0)
                            wait_drained(pe, l, "Q", u, 1)
                            if u < LATENT_TILES:
                                pe.wait_ge(S["q_rotated"], u + 1)
                        pe.wait_ge(S["k_ready"], u + 1)
                        wait_drained(pe, l, "KV", u, 0)
                        for g in range(2):
                            if u < nt:
                                flips((l, "QT", u, g), [q_rows[:, u % 2, h * QK:(h + 1) * QK] for h in range(4 * g, 4 * g + 4)], QK)
                            flips((l, "KT", u, g), [k_rows[:, u % 2, h * QK:(h + 1) * QK] for h in range(4 * g, 4 * g + 4)], QK)
                for g in range(2):
                    wait_drained(pe, l, "QT", nt - 1, g)
                    wait_drained(pe, l, "KT", TILES - 1, g)
                m = len(units(l))
                for i in range(m + 3):
                    if i < m:
                        qt, h = units(l)[i]
                        lo, hi = keys_of(qt)
                        chain((l, "S", i), hi - lo, lambda k: q_T[0:QK, h, qt * P:(qt + 1) * P], lambda k: k_T[0:QK, h, lo:hi], 1)
                    if 2 <= i < m + 2:
                        lo, hi = keys_of(units(l)[i - 2][0])
                        pe.wait_ge(S["p_ready"], i - 1)
                        flips((l, "PT", i - 2), [p_rows[:, i % 2, k * P:(k + 1) * P] for k in range((hi - lo) // P)])
                    if i >= 3:
                        qt, h = units(l)[i - 3]
                        lo, hi = keys_of(qt)
                        wait_drained(pe, l, "PT", i - 3)
                        b = claim(l, "O", i - 3)
                        n = (hi - lo) // P
                        for k in range(n):
                            mm = pe.matmul(b[64 * (h % 2):64 * (h % 2) + 64, 0:P], v_rows[:, lo // P + k, h * V_DIM:(h + 1) * V_DIM],
                                           p_T[:, (i - 3) % 2, k * P:(k + 1) * P], start=(k == 0), stop=(k == n - 1))
                        mm.then_inc(psum_filled, 1)
                pe.wait_ge(S["w_out_in"], 16)
                wait_drained(pe, l, "O", m - 1)
                for name, t in head_steps(l):
                    if name == "OUT":
                        for c in range(2):
                            chain((l, "OUT", t, c), 512, lambda k: mixed[:, k, t * P:(t + 1) * P], lambda k: w_out[:, k, 512 * c:512 * c + 512], DK)
                    elif name == "T2":
                        pe.wait_ge(S["h2_ready"], t + 1)
                        for c in range(2):
                            flips((l, "T2", t, c), [h2_rows[:, t, 4 * c + k:D:DK] for k in range(4)])
                    else:
                        if t == 0:
                            pe.wait_ge(S["router_in"], 32)
                        wait_drained(pe, l, "T2", t, 0)
                        wait_drained(pe, l, "T2", t, 1)
                        chain((l, "R", t), EXPERTS, lambda k: h_T[:, k, t * P:(t + 1) * P], lambda k: w_router[:, k, :], DK)
                pe.wait_ge(S["shared_in"], 48)
                def make_list(i, e, s):
                    pe.wait_ge(S["g_ready"], i + 1)
                    ge(pe, S["idx_ready"], i)
                    for t in range(nt):
                        mm = pe.matmul(banks[LIST_BANK][0:rows, 0:3], one_hot[:, s % 2, t, 0:rows], vals[:, t, bass.ds(e, 1), :].rearrange("p a n -> p (a n)"),
                                       start=(t == 0), stop=(t == nt - 1))
                    mm.then_inc(S["list_filled"], 1)

                gu, dn = slot_gu(SHARED_SLOT), slot_dn(SHARED_SLOT)
                for step in tail_steps(l):
                    u = step[1] if len(step) > 1 else None
                    if step[0] == "SG":
                        b = claim(l, "SG", u)
                        for k in range(DK):
                            mm = pe.matmul(split(b[:, :], (2, FE)), h_T[:, k, u * P:(u + 1) * P], gu[:, :, k, :], start=(k == 0), stop=(k == DK - 1))
                        mm.then_inc(psum_filled, 1)
                    elif step[0] == "SD":
                        wait_drained(pe, l, "SG", u)
                        flips((l, "SH", u), [hid[:, u % 2, j:FE:2] for j in range(2)])
                        wait_drained(pe, l, "SH", u)
                        for c in range(2):
                            chain((l, "SD", u, c), 512, lambda k: hid_T[:, u % 2, k, :], lambda k: dn[:, k, 512 * c:512 * c + 512], 2)
                    elif step[0] == "MT":
                        pe.wait_ge(S["chosen_ready"], 1)
                        b = claim(l, "MT")
                        for t in range(nt):
                            mm = pe.transpose(b[0:64, t * P:(t + 1) * P], chosen[:, t, :], ident[:, :])
                        mm.then_inc(psum_filled, 1)
                    elif step[0] == "PLACES":
                        wait_drained(pe, l, "MT")
                        b = claim(l, "RANK")
                        for t in range(nt):
                            mm = pe.matmul(b[:, t * EXPERTS:(t + 1) * EXPERTS], ranks_T[0:64, t, :], strict[0:64, 0:64], start=True, stop=True)
                        mm.then_inc(psum_filled, 1)
                        b = claim(l, "POS")
                        for t in range(nt):
                            for q in range(t + 1):
                                pe.matmul(b[:, t * EXPERTS:(t + 1) * EXPERTS], strict[:, :] if q == t else ones[:, :], chosen[:, q, :],
                                          start=(q == 0), stop=(q == t))
                        for q in range(nt):
                            mm = pe.matmul(b[0:64, TILES * EXPERTS:TILES * EXPERTS + 1], chosen[:, q, :], ones[:, 0:1], start=(q == 0), stop=(q == nt - 1))
                        mm.then_inc(psum_filled, 1)
                    elif step[0] == "ENDS":
                        wait_drained(pe, l, "POS")
                        b = claim(l, "ENDS")
                        pe.matmul(b[:, 0:P], ext_b, ends_rhs[:, :], start=True, stop=True).then_inc(psum_filled, 1)
                    elif step[0] == "EXTRA":
                        pe.wait_ge(S["table_ready"], 1)
                        b = claim(l, "EXTRA")
                        for c in range(3):
                            mm = pe.matmul(b[0:1, c * MAX_EXTRA:(c + 1) * MAX_EXTRA], table[0:MAX_EXTRA, c:c + 1], ident[0:MAX_EXTRA, 0:MAX_EXTRA], start=True, stop=True)
                        mm.then_inc(psum_filled, 1)
                        wait_drained(pe, l, "EXTRA")
                    else:
                        make_list(u, u, u)
                wait_drained(pe, l, "SD", nt - 1, 1)

                def flip_rows(i, j, s):
                    pe.wait_ge(S["gathered"][s % 4], ((UNROLL // 4) * j + s // 4 + 1) * 16)
                    ge(pe, S["xt_drained"], 2 * i)
                    for k in range(DK):
                        mm = pe.transpose(banks[k // 4][:, (k % 4) * P:(k % 4) * P + rows], x_g[0:rows, s % 4, k:D:DK], ident[0:rows, 0:rows])
                    mm.then_inc(S["xt_filled"], 1)

                def up(gu, x, bank):
                    for k in range(DK):
                        mm = pe.matmul(split(bank[:, :], (2, FE)), x_gT[:, x, k, :], gu[:, :, k, :], start=(k == 0), stop=(k == DK - 1))
                    return mm

                def down(dn):
                    for c in range(2):
                        for k in range(2):
                            mm = pe.matmul(banks[6 + c][:, :], hid_T_x[:, k, :], dn[:, k, 512 * c:512 * c + 512], start=(k == 0), stop=(k == 1))
                    return mm

                def flip_hid():
                    for k in range(2):
                        mm = pe.transpose(banks[4][:, k * P:(k + 1) * P], hid_x[:, k:FE:2], ident[:, :])
                    return mm

                def down_step(i):
                    pe.wait_ge(S["ht_drained"], i + 1)
                    ge(pe, S["y_ready"], 2 * i)
                    for k in range(2):
                        pe.wait_ge(S["dn_lo"], 2 * i + k + 1)
                        for c in range(2):
                            for n, (x, w) in enumerate(((hid_hi, dn_hi), (hid_hi, dn_lo), (hid_lo, dn_hi))):
                                mm = pe.matmul(banks[6 + c][:, :], x[:, k, :], w[:, k, 512 * c:512 * c + 512],
                                               start=(k == n == 0), stop=(k == 1 and n == 2))
                    mm.then_inc(S["d_filled"], 1)

                flip_rows(0, 0, 0)

                def step(j, s):
                    i = j * UNROLL + s
                    flip_rows(i + 1, j, s + 1)
                    w = expert_slot(s)
                    pe.wait_ge(S["gu_in"][w], ((UNROLL // 4) * j + s // 4 + 1) * 32)
                    ge(pe, S["hid_ready"], 2 * (i - 1))
                    up(slot_gu(w), s % 2, banks[2 + s % 2]).then_inc(S["gu_filled"], 1)
                    make_list(i + AHEAD, i + AHEAD, s)
                    if not (isinstance(i, int) and i == 0):
                        down_step(i - 1)
                    pe.wait_ge(S["hid_ready"], 2 * (i + 1))
                    ge(pe, S["ht_drained"], i)
                    flip_hid().then_inc(S["ht_filled"], 1)

                for s in range(UNROLL):
                    step(0, s)
                def expert_of(o):
                    return pe.value_load(extra_row[0:1, bass.ds(o + MAX_EXTRA, 1)], min_val=0, max_val=EXPERTS - 1)

                n_extra = pe.value_load(extra_row[0:1, 0:1], min_val=0, max_val=MAX_EXTRA)
                e_first = expert_of(0)
                with pe.Fori(1, EXPERTS // UNROLL) as j:
                    for s in range(UNROLL):
                        step(j, s)
                def block_list(o, e):
                    pe.wait_ge(S["g_ready"], o + 1 + LISTED)
                    for t in range(nt):
                        mm = pe.matmul(banks[LIST_BANK][0:rows, 0:3], one_hot[:, 0, t, 0:rows], vals[:, t, bass.ds(e, 1), :].rearrange("p a n -> p (a n)"),
                                       start=(t == 0), stop=(t == nt - 1))
                    mm.then_inc(S["list_filled"], 1)

                def block_run(o):
                    pe.wait_ge(S["e_x"], o * 32 + 16)
                    for k in range(DK):
                        mm = pe.transpose(banks[k // 4][:, (k % 4) * P:(k % 4) * P + rows], x_g[0:rows, 0, k:D:DK], ident[0:rows, 0:rows])
                    mm.then_inc(S["xt_filled"], 1)
                    pe.wait_ge(S["e_w"], (o + 1) * 48)
                    pe.wait_ge(S["xt_drained"], 2 * (o + 1 + EXPERTS + 1))
                    up(slot_gu(EXTRA_SLOT), 0, banks[2]).then_inc(S["gu_filled"], 1)
                    pe.wait_ge(S["hid_ready"], 2 * (o + 1 + EXPERTS))
                    flip_hid().then_inc(S["ht_filled"], 1)
                    pe.wait_ge(S["ht_drained"], o + 1 + EXPERTS)
                    pe.wait_ge(S["y_ready"], 2 * (o + EXPERTS))
                    down(slot_dn(EXTRA_SLOT)).then_inc(S["d_filled"], 1)

                pe.wait_ge(S["idx_ready"], LISTED)
                with pe.If(n_extra > 0):
                    block_list(0, e_first)
                down_step(EXPERTS - 1)
                pe.wait_ge(S["xt_drained"], 2 * (EXPERTS + 1))
                with pe.If(n_extra > 0):
                    block_run(0)
                with pe.If(n_extra > 1):
                    with pe.Fori(1, n_extra) as o:
                        block_list(o, expert_of(o))
                        block_run(o)
                pe.wait_ge(S["y_ready"], 2 * (n_extra + EXPERTS))


def shape_constants():
    f = np.float32
    pos = np.arange(SEQ)
    pool = np.zeros((4, SEQ, SEQ), np.float64)
    for g, w in enumerate(POOL_WINDOWS):
        for t in range(SEQ):
            lo, hi = max(t - w // 2, 0), min(t + w // 2, SEQ)
            pool[g, t, lo:hi] = 1.0 / (hi - lo)
            pool[g, t, t] -= 1.0
    ang_l = 2 * np.pi * ((pos[:, None] * pos[None, :]) % SEQ) / SEQ
    ch = np.arange(GROUP)
    ang_c = 2 * np.pi * ((ch[:, None] * ch[None, :]) % GROUP) / GROUP
    norm = 1.0 / np.sqrt(SEQ * GROUP)
    dft_l = np.concatenate([np.cos(ang_l), np.sin(ang_l)], axis=1)
    dft_c = np.zeros((P, 2, P))
    for g in range(2):
        dft_c[g * 64:g * 64 + 64, 0, g * 64:g * 64 + 64] = np.cos(ang_c) * norm
        dft_c[g * 64:g * 64 + 64, 1, g * 64:g * 64 + 64] = -np.sin(ang_c) * norm
    inv = f(ROPE_THETA) ** (-np.arange(ROPE_FREQS, dtype=f) * f(2.0) / f(2 * ROPE_FREQS))
    ang = np.stack([(pos // GRID_W).astype(f)[:, None] * inv, (pos % GRID_W).astype(f)[:, None] * inv], axis=1).reshape(SEQ, 16)
    rope = np.stack([np.cos(ang), np.sin(ang)], axis=1).reshape(2, P, 2, 16).transpose(1, 0, 2, 3)
    strict = np.triu(np.ones((P, P)), 1)
    lane = np.arange(P)
    tok = lane[:, None] + P * np.arange(TILES)[None, :]
    grp = np.arange(8)
    out = {
        "k_ident": np.eye(P),
        "k_strict": strict,
        "k_iota": np.tile(np.arange(TOKENS), (P, 1)),
        "k_ends": np.concatenate([np.triu(np.ones((64, 64))), np.eye(64)], axis=1),
        "k_token": np.concatenate([tok - SKIP, TOP_K * tok - SKIP], axis=1),
        "k_lane": lane[:, None],
        "k_tie": np.tile((grp[None, :] < grp[:, None]).reshape(1, 64), (P, 1)),
        "k_rope": rope,
        "k_pool": pool.transpose(2, 0, 1).reshape(2, P, 4, SEQ).transpose(1, 0, 2, 3),
        "k_dft_l": dft_l.reshape(2, P, 2 * SEQ).transpose(1, 0, 2),
        "k_dft_c": dft_c,
    }
    return {k: np.ascontiguousarray(v.astype(f)) for k, v in out.items()}


def kernel(**inputs):
    import concourse.bacc as bacc
    from concourse.bass_utils import run_bass_kernel_spmd

    nc = bacc.Bacc("TRN2", target_bir_lowering=False, num_devices=1)
    arrays = {k: np.ascontiguousarray(v) for k, v in inputs.items()}
    arrays.update(shape_constants())
    aps = {k: nc.dram_tensor(f"in_{k}", v.shape, mybir.dt.from_np(v.dtype), kind="ExternalInput").ap() for k, v in arrays.items()}
    out = nc.dram_tensor("out", (1, SEQ, D), F32, kind="ExternalOutput").ap()
    build(nc, aps, out)
    r = run_bass_kernel_spmd(nc, [{f"in_{k}": v for k, v in arrays.items()}], core_ids=[0])
    return r.results[0]["out"]
```
